# Optimizing a Trainium2 kernel written in Bass

```python
import jax, jax.numpy as jnp
from jax import lax
import numpy as np
import math
import jax
import jax.numpy as jnp

D_MODEL = 1024
BATCH = 1
SEQ = 1024
DEPTH = 1

PLE_DIM = 256
MIX_WIDTH = D_MODEL
HG_WIDTH = D_MODEL // 2
HG_HEADS = 4
HG_DK = HG_WIDTH // HG_HEADS
HG_DV = HG_WIDTH // HG_HEADS
HG_CHUNK = 64
SB_WIDTH = MIX_WIDTH - HG_WIDTH
SB_HEADS = 8
SB_DH = SB_WIDTH // SB_HEADS
SB_BLOCK = 128
D_FF = -(-8 * D_MODEL // (3 * 256)) * 256
IN_COLS = 4 * HG_WIDTH + 3 * SB_WIDTH
EPS = 1e-6


def rmsnorm(x, w):
    xf = x.astype(jnp.float32)
    xf = xf * lax.rsqrt(jnp.mean(xf * xf, axis=-1, keepdims=True) + EPS)
    return xf.astype(x.dtype) * w

def _to_chunks(a, heads, d):
    B, T, _ = a.shape
    return a.reshape(B, T // HG_CHUNK, HG_CHUNK, heads, d).transpose(1, 0, 3, 2, 4)

def hgrn2_mix(q, f_logit, i_in, lb):
    B, T, _ = q.shape
    q = jax.nn.silu(q.astype(jnp.float32))
    z = f_logit.astype(jnp.float32)
    log_f = jnp.logaddexp(jnp.log(lb), jnp.log1p(-lb) + jax.nn.log_sigmoid(z))
    k = -jnp.expm1(log_f)
    v = i_in.astype(jnp.float32)
    qc = _to_chunks(q, HG_HEADS, HG_DK)
    kc = _to_chunks(k, HG_HEADS, HG_DK)
    gc = _to_chunks(log_f, HG_HEADS, HG_DK)
    vc = _to_chunks(v, HG_HEADS, HG_DV)
    incl = jnp.tril(jnp.ones((HG_CHUNK, HG_CHUNK), dtype=bool))

    def step(S, inp):
        qb, kb, gb, vb = inp
        b = jnp.cumsum(gb, axis=2)
        o_inter = jnp.einsum('bhtk,bhkv->bhtv', qb * jnp.exp(b), S)
        diff = b[:, :, :, None, :] - b[:, :, None, :, :]
        decay = jnp.where(incl[:, :, None], jnp.exp(jnp.minimum(diff, 0.0)), 0.0)
        scores = jnp.einsum('bhtsk,bhsk->bhts', qb[:, :, :, None, :] * decay, kb)
        o_intra = jnp.einsum('bhts,bhsv->bhtv', scores, vb)
        b_last = b[:, :, -1:, :]
        S_new = jnp.exp(b_last[:, :, 0, :])[..., None] * S + jnp.einsum(
            'bhsk,bhsv->bhkv', kb * jnp.exp(b_last - b), vb)
        return S_new, o_inter + o_intra

    S0 = jnp.zeros((B, HG_HEADS, HG_DK, HG_DV), jnp.float32)
    _, oc = lax.scan(step, S0, (qc, kc, gc, vc))
    return oc.transpose(1, 0, 3, 2, 4).reshape(B, T, HG_HEADS * HG_DV)

def stick_breaking_mix(q, k, v):
    B, T, H, d = q.shape
    scale = d ** -0.5
    outs = []
    for blk in range(T // SB_BLOCK):
        t0 = blk * SB_BLOCK
        t1 = t0 + SB_BLOCK
        qb = q[:, t0:t1]
        kp = k[:, :t1]
        vp = v[:, :t1]
        z = jnp.einsum('bthd,bshd->bhts', qb, kp).astype(jnp.float32) * scale
        causal = jnp.arange(t1)[None, :] < jnp.arange(t0, t1)[:, None]
        log_1mb = jnp.where(causal, -jax.nn.softplus(z), 0.0)
        rem = lax.cumsum(log_1mb, axis=3, reverse=True) - log_1mb
        a = jnp.where(causal, jnp.exp(jax.nn.log_sigmoid(z) + rem), 0.0)
        outs.append(jnp.einsum('bhts,bshd->bthd', a.astype(v.dtype), vp))
    return jnp.concatenate(outs, axis=1)

def first_inputs(seed: int = 0) -> dict:
    key = jax.random.key(seed)
    ks = jax.random.split(key, 16)
    f32 = jnp.float32
    nrm = lambda k, shape, s: jax.random.normal(k, shape, f32) * s
    gain = lambda k, shape: 1.0 + 0.05 * jax.random.normal(k, shape, f32)
    return {
        "x": jax.random.normal(ks[0], (BATCH, SEQ, D_MODEL), f32),
        "p": jax.random.normal(ks[1], (DEPTH, BATCH, SEQ, PLE_DIM), f32),
        "attn_pre_norm": gain(ks[2], (DEPTH, D_MODEL)),
        "w_in": nrm(ks[3], (DEPTH, D_MODEL, IN_COLS), D_MODEL ** -0.5),
        "hg_lower_gamma": nrm(ks[4], (DEPTH + 1, HG_WIDTH), 0.5),
        "hg_out_norm": gain(ks[5], (DEPTH, HG_WIDTH)),
        "sb_out_norm": gain(ks[6], (DEPTH, SB_WIDTH)),
        "w_out": nrm(ks[7], (DEPTH, MIX_WIDTH, D_MODEL), MIX_WIDTH ** -0.5),
        "attn_post_norm": gain(ks[8], (DEPTH, D_MODEL)),
        "ffn_pre_norm": gain(ks[9], (DEPTH, D_MODEL)),
        "w_gate_up": nrm(ks[10], (DEPTH, D_MODEL, 2 * D_FF), D_MODEL ** -0.5),
        "w_down": nrm(ks[11], (DEPTH, D_FF, D_MODEL), D_FF ** -0.5),
        "ffn_post_norm": gain(ks[12], (DEPTH, D_MODEL)),
        "ple_proj": nrm(ks[13], (DEPTH, PLE_DIM, D_MODEL), PLE_DIM ** -0.5),
        "ple_gate": nrm(ks[14], (DEPTH, D_MODEL, D_MODEL), D_MODEL ** -0.5),
    }

def first_block(x, p, attn_pre_norm, w_in, hg_lower_gamma, hg_out_norm, sb_out_norm, w_out,
              attn_post_norm, ffn_pre_norm, w_gate_up, w_down, ffn_post_norm, ple_proj, ple_gate):
    B, T, _ = x.shape
    lb_all = jnp.cumsum(jax.nn.softmax(hg_lower_gamma.astype(jnp.float32), axis=0), axis=0)
    splits = [HG_WIDTH, 2 * HG_WIDTH, 3 * HG_WIDTH, 4 * HG_WIDTH,
              4 * HG_WIDTH + SB_WIDTH, 4 * HG_WIDTH + 2 * SB_WIDTH]
    h = x
    for i in range(DEPTH):
        u = rmsnorm(h, attn_pre_norm[i])
        proj = u @ w_in[i]
        hq, hf, hi, hg, sq, sk, sv = jnp.split(proj, splits, axis=-1)
        o_hg = hgrn2_mix(hq, hf, hi, lb_all[i])
        o_hg = rmsnorm(o_hg.astype(x.dtype), hg_out_norm[i]) * jax.nn.silu(hg)
        o_sb = stick_breaking_mix(sq.reshape(B, T, SB_HEADS, SB_DH),
                                  sk.reshape(B, T, SB_HEADS, SB_DH),
                                  sv.reshape(B, T, SB_HEADS, SB_DH)).reshape(B, T, SB_WIDTH)
        o_sb = rmsnorm(o_sb, sb_out_norm[i])
        mix = jnp.concatenate([o_hg, o_sb], axis=-1) @ w_out[i]
        h = h + rmsnorm(mix, attn_post_norm[i])
        u = rmsnorm(h, ffn_pre_norm[i])
        gate, up = jnp.split(u @ w_gate_up[i], [D_FF], axis=-1)
        y = (jax.nn.silu(gate) * up) @ w_down[i]
        h = h + rmsnorm(y, ffn_post_norm[i])
        h = h + (p[i] @ ple_proj[i]) * jax.nn.sigmoid(h @ ple_gate[i])
    return h


CHUNK = 64
Q_BLOCK = 128
NEG_INF = -1e30

MLA_HEADS = 8
MLA_Q_RANK = 256
MLA_KV_RANK = 128
MLA_NOPE = 64
MLA_ROPE = 32
MLA_QK = MLA_NOPE + MLA_ROPE
MLA_V = 64
ROPE_THETA = 10000.0

DIFF_HEADS = 4
DIFF_QK = 64
DIFF_V = 2 * DIFF_QK

MIX_WIDTH_2 = MLA_HEADS * MLA_V + DIFF_HEADS * DIFF_V

NUM_BUCKETS = 32
MAX_DISTANCE = 1024

D_FF_2 = 2816
CONV_WIDTH = 3

OFF_Q_LAT = 0
OFF_KV_LAT = OFF_Q_LAT + MLA_Q_RANK
OFF_K_ROPE = OFF_KV_LAT + MLA_KV_RANK
OFF_DIFF_Q = OFF_K_ROPE + MLA_ROPE
OFF_DIFF_K = OFF_DIFF_Q + DIFF_HEADS * 2 * DIFF_QK
OFF_DIFF_V = OFF_DIFF_K + DIFF_HEADS * 2 * DIFF_QK
IN_COLS_2 = OFF_DIFF_V + DIFF_HEADS * DIFF_V


def lambda_init(layer):
    return 0.8 - 0.6 * math.exp(-0.3 * layer)

def rms_norm(x, g):
    xf = x.astype(jnp.float32)
    y = xf * lax.rsqrt(jnp.mean(xf * xf, axis=-1, keepdims=True) + EPS)
    return (y * g.astype(jnp.float32)).astype(x.dtype)

def apply_rope(t, pos):
    half = t.shape[-1] // 2
    inv_freq = ROPE_THETA ** (-jnp.arange(half, dtype=jnp.float32) / half)
    ang = pos.astype(jnp.float32)[:, None] * inv_freq[None, :]
    cos = jnp.cos(ang)[None, :, None, :].astype(t.dtype)
    sin = jnp.sin(ang)[None, :, None, :].astype(t.dtype)
    t1, t2 = t[..., :half], t[..., half:]
    return jnp.concatenate([t1 * cos - t2 * sin, t2 * cos + t1 * sin], axis=-1)

def t5_bucket(rel):
    nb = NUM_BUCKETS // 2
    max_exact = nb // 2
    sign_off = (rel > 0).astype(jnp.int32) * nb
    n = jnp.abs(rel)
    nf = jnp.maximum(n, 1).astype(jnp.float32)
    large = max_exact + (jnp.log(nf / max_exact) / math.log(MAX_DISTANCE / max_exact)
                         * (nb - max_exact)).astype(jnp.int32)
    large = jnp.minimum(large, nb - 1)
    return sign_off + jnp.where(n < max_exact, n, large)

def block_indices(blk, seq):
    q_idx = blk * Q_BLOCK + jnp.arange(Q_BLOCK, dtype=jnp.int32)
    k_idx = jnp.arange(seq, dtype=jnp.int32)
    return q_idx, k_idx

def chunk_allowed(q_idx, k_idx):
    return (k_idx[None, :] // CHUNK) <= (q_idx[:, None] // CHUNK)

def to_blocks(t):
    b, s, h, d = t.shape
    return t.reshape(b, s // Q_BLOCK, Q_BLOCK, h, d).transpose(1, 0, 3, 2, 4)

def from_blocks(t):
    n, b, h, qb, d = t.shape
    return t.transpose(1, 0, 3, 2, 4).reshape(b, n * qb, h, d)

def mla_group(q_lat, kv_lat, k_rope, pos, q_lat_g, w_uq, kv_lat_g, w_ukv, q_g, k_g):
    b, s, _ = q_lat.shape
    q = (rms_norm(q_lat, q_lat_g) @ w_uq).reshape(b, s, MLA_HEADS, MLA_QK)
    kv = (rms_norm(kv_lat, kv_lat_g) @ w_ukv).reshape(b, s, MLA_HEADS, MLA_NOPE + MLA_V)
    k_nope, v = kv[..., :MLA_NOPE], kv[..., MLA_NOPE:]
    k_r = jnp.broadcast_to(k_rope[:, :, None, :], (b, s, MLA_HEADS, MLA_ROPE))
    k = jnp.concatenate([k_nope, k_r], axis=-1)
    q = rms_norm(q, q_g)
    k = rms_norm(k, k_g)
    q = jnp.concatenate([q[..., :MLA_NOPE], apply_rope(q[..., MLA_NOPE:], pos)], axis=-1)
    k = jnp.concatenate([k[..., :MLA_NOPE], apply_rope(k[..., MLA_NOPE:], pos)], axis=-1)
    k_t = k.transpose(0, 2, 1, 3)
    v_t = v.transpose(0, 2, 1, 3)
    scale = MLA_QK ** -0.5

    def one_block(args):
        qb, blk = args
        q_idx, k_idx = block_indices(blk, s)
        allowed = chunk_allowed(q_idx, k_idx)
        logits = jnp.einsum('bhqd,bhkd->bhqk', qb, k_t).astype(jnp.float32) * scale
        logits = jnp.where(allowed[None, None], logits, NEG_INF)
        probs = jax.nn.softmax(logits, axis=-1).astype(v_t.dtype)
        return jnp.einsum('bhqk,bhkd->bhqd', probs, v_t)

    o = lax.map(one_block, (to_blocks(q), jnp.arange(s // Q_BLOCK, dtype=jnp.int32)))
    return from_blocks(o).reshape(b, s, MLA_HEADS * MLA_V)

def diff_group(dq, dk, dv, q_g, k_g, lq1, lk1, lq2, lk2, out_g, rel_bias, lam_init):
    b, s, _ = dq.shape
    q = rms_norm(dq.reshape(b, s, DIFF_HEADS, 2, DIFF_QK), q_g)
    k = rms_norm(dk.reshape(b, s, DIFF_HEADS, 2, DIFF_QK), k_g)
    k_t = k.transpose(0, 2, 3, 1, 4)
    v_t = dv.reshape(b, s, DIFF_HEADS, DIFF_V).transpose(0, 2, 1, 3)
    f32 = jnp.float32
    lam = (jnp.exp(jnp.sum(lq1.astype(f32) * lk1.astype(f32)))
           - jnp.exp(jnp.sum(lq2.astype(f32) * lk2.astype(f32))) + lam_init)
    scale = DIFF_QK ** -0.5
    table = rel_bias.astype(f32)

    def one_block(args):
        qb, blk = args
        qb = qb.reshape(b, DIFF_HEADS, Q_BLOCK, 2, DIFF_QK)
        q_idx, k_idx = block_indices(blk, s)
        allowed = chunk_allowed(q_idx, k_idx)
        bias = table[t5_bucket(k_idx[None, :] - q_idx[:, None])].transpose(2, 0, 1)
        logits = jnp.einsum('bhqmd,bhmkd->bhmqk', qb, k_t).astype(f32) * scale
        logits = logits + bias[None, :, None]
        logits = jnp.where(allowed[None, None, None], logits, NEG_INF)
        probs = jax.nn.softmax(logits, axis=-1)
        attn = (probs[:, :, 0] - lam * probs[:, :, 1]).astype(v_t.dtype)
        return jnp.einsum('bhqk,bhkd->bhqd', attn, v_t)

    qf = q.reshape(b, s, DIFF_HEADS, 2 * DIFF_QK)
    o = lax.map(one_block, (to_blocks(qf), jnp.arange(s // Q_BLOCK, dtype=jnp.int32)))
    o = rms_norm(from_blocks(o), out_g) * (1.0 - lam_init)
    return o.reshape(b, s, DIFF_HEADS * DIFF_V)

def conv_ffn(h, w_gate, w_up, conv_w, conv_b, w_down):
    s = h.shape[1]
    g = h @ w_gate
    gp = jnp.pad(g, ((0, 0), (CONV_WIDTH - 1, 0), (0, 0)))
    conv = conv_b
    for j in range(CONV_WIDTH):
        conv = conv + gp[:, j:j + s, :] * conv_w[j]
    return (jax.nn.silu(conv) * (h @ w_up)) @ w_down

def second_inputs(seed: int = 0) -> dict:
    key = jax.random.key(seed)
    ks = jax.random.split(key, 28)
    f32 = jnp.float32

    def nrm(k, shape, scale):
        return jax.random.normal(k, shape, dtype=f32) * scale

    def gain(k, shape):
        return 1.0 + 0.1 * jax.random.normal(k, shape, dtype=f32)

    return {
        'x': nrm(ks[0], (BATCH, SEQ, D_MODEL), 1.0),
        'p': nrm(ks[1], (DEPTH, BATCH, SEQ, PLE_DIM), 1.0),
        'attn_norm_g': gain(ks[2], (DEPTH, D_MODEL)),
        'w_in': nrm(ks[3], (DEPTH, D_MODEL, IN_COLS_2), D_MODEL ** -0.5),
        'q_lat_norm_g': gain(ks[4], (DEPTH, MLA_Q_RANK)),
        'w_uq': nrm(ks[5], (DEPTH, MLA_Q_RANK, MLA_HEADS * MLA_QK), MLA_Q_RANK ** -0.5),
        'kv_lat_norm_g': gain(ks[6], (DEPTH, MLA_KV_RANK)),
        'w_ukv': nrm(ks[7], (DEPTH, MLA_KV_RANK, MLA_HEADS * (MLA_NOPE + MLA_V)), MLA_KV_RANK ** -0.5),
        'mla_q_norm_g': gain(ks[8], (DEPTH, MLA_QK)),
        'mla_k_norm_g': gain(ks[9], (DEPTH, MLA_QK)),
        'diff_q_norm_g': gain(ks[10], (DEPTH, DIFF_QK)),
        'diff_k_norm_g': gain(ks[11], (DEPTH, DIFF_QK)),
        'lambda_q1': nrm(ks[12], (DEPTH, DIFF_QK), 0.1),
        'lambda_k1': nrm(ks[13], (DEPTH, DIFF_QK), 0.1),
        'lambda_q2': nrm(ks[14], (DEPTH, DIFF_QK), 0.1),
        'lambda_k2': nrm(ks[15], (DEPTH, DIFF_QK), 0.1),
        'diff_out_norm_g': gain(ks[16], (DEPTH, DIFF_V)),
        'rel_bias': nrm(ks[17], (NUM_BUCKETS, DIFF_HEADS), 0.5),
        'w_out': nrm(ks[18], (DEPTH, MIX_WIDTH_2, D_MODEL), MIX_WIDTH_2 ** -0.5),
        'ffn_norm_g': gain(ks[19], (DEPTH, D_MODEL)),
        'w_gate': nrm(ks[20], (DEPTH, D_MODEL, D_FF_2), D_MODEL ** -0.5),
        'w_up': nrm(ks[21], (DEPTH, D_MODEL, D_FF_2), D_MODEL ** -0.5),
        'conv_w': nrm(ks[22], (DEPTH, CONV_WIDTH, D_FF_2), CONV_WIDTH ** -0.5),
        'conv_b': nrm(ks[23], (DEPTH, D_FF_2), 0.02),
        'w_down': nrm(ks[24], (DEPTH, D_FF_2, D_MODEL), D_FF_2 ** -0.5),
        'ple_norm_g': gain(ks[25], (DEPTH, D_MODEL)),
        'w_ple_gate': nrm(ks[26], (DEPTH, D_MODEL, D_MODEL), D_MODEL ** -0.5),
        'w_ple_proj': nrm(ks[27], (DEPTH, PLE_DIM, D_MODEL), PLE_DIM ** -0.5),
    }

def second_block(x, p, attn_norm_g, w_in, q_lat_norm_g, w_uq, kv_lat_norm_g, w_ukv,
              mla_q_norm_g, mla_k_norm_g, diff_q_norm_g, diff_k_norm_g,
              lambda_q1, lambda_k1, lambda_q2, lambda_k2, diff_out_norm_g, rel_bias,
              w_out, ffn_norm_g, w_gate, w_up, conv_w, conv_b, w_down,
              ple_norm_g, w_ple_gate, w_ple_proj):
    s = x.shape[1]
    pos = jnp.arange(s, dtype=jnp.int32)
    for i in range(DEPTH):
        h = rms_norm(x, attn_norm_g[i])
        z = h @ w_in[i]
        y_mla = mla_group(z[..., OFF_Q_LAT:OFF_KV_LAT], z[..., OFF_KV_LAT:OFF_K_ROPE],
                          z[..., OFF_K_ROPE:OFF_DIFF_Q], pos,
                          q_lat_norm_g[i], w_uq[i], kv_lat_norm_g[i], w_ukv[i],
                          mla_q_norm_g[i], mla_k_norm_g[i])
        y_diff = diff_group(z[..., OFF_DIFF_Q:OFF_DIFF_K], z[..., OFF_DIFF_K:OFF_DIFF_V],
                            z[..., OFF_DIFF_V:IN_COLS_2],
                            diff_q_norm_g[i], diff_k_norm_g[i],
                            lambda_q1[i], lambda_k1[i], lambda_q2[i], lambda_k2[i],
                            diff_out_norm_g[i], rel_bias, lambda_init(i))
        x = x + jnp.concatenate([y_mla, y_diff], axis=-1) @ w_out[i]
        x = x + conv_ffn(rms_norm(x, ffn_norm_g[i]), w_gate[i], w_up[i], conv_w[i], conv_b[i], w_down[i])
        gate = jax.nn.sigmoid(rms_norm(x, ple_norm_g[i]) @ w_ple_gate[i])
        x = x + gate * (p[i] @ w_ple_proj[i])
    return x


def setup_inputs(seed=0):
    out = dict(first_inputs(seed))
    for name, value in second_inputs(seed + 1).items():
        if name != "x":
            out[name + "_2"] = value
    return out


def reference(
    x, p, attn_pre_norm, w_in, hg_lower_gamma, hg_out_norm, sb_out_norm, w_out, attn_post_norm,
    ffn_pre_norm, w_gate_up, w_down, ffn_post_norm, ple_proj, ple_gate, p_2, attn_norm_g_2,
    w_in_2, q_lat_norm_g_2, w_uq_2, kv_lat_norm_g_2, w_ukv_2, mla_q_norm_g_2, mla_k_norm_g_2,
    diff_q_norm_g_2, diff_k_norm_g_2, lambda_q1_2, lambda_k1_2, lambda_q2_2, lambda_k2_2,
    diff_out_norm_g_2, rel_bias_2, w_out_2, ffn_norm_g_2, w_gate_2, w_up_2, conv_w_2, conv_b_2,
    w_down_2, ple_norm_g_2, w_ple_gate_2, w_ple_proj_2,
):
    x = first_block(
        x, p, attn_pre_norm, w_in, hg_lower_gamma, hg_out_norm, sb_out_norm, w_out,
        attn_post_norm, ffn_pre_norm, w_gate_up, w_down, ffn_post_norm, ple_proj, ple_gate,
    )
    return second_block(
        x, p_2, attn_norm_g_2, w_in_2, q_lat_norm_g_2, w_uq_2, kv_lat_norm_g_2, w_ukv_2,
        mla_q_norm_g_2, mla_k_norm_g_2, diff_q_norm_g_2, diff_k_norm_g_2, lambda_q1_2,
        lambda_k1_2, lambda_q2_2, lambda_k2_2, diff_out_norm_g_2, rel_bias_2, w_out_2,
        ffn_norm_g_2, w_gate_2, w_up_2, conv_w_2, conv_b_2, w_down_2, ple_norm_g_2,
        w_ple_gate_2, w_ple_proj_2,
    )


_drawn_inputs = setup_inputs


def setup_inputs(seed=0):
    import zlib

    import numpy as np

    out = dict(_drawn_inputs(seed))
    spreads = {}
    factors = {'q_lat_norm_g_2': 8.0,
     'kv_lat_norm_g_2': 7.899,
     'mla_q_norm_g_2': 8.0,
     'mla_k_norm_g_2': 8.0,
     'lambda_q2_2': 8.0,
     'lambda_k2_2': 8.0,
     'conv_b_2': 26.901,
     'ple_norm_g_2': 31.027,
     'diff_q_norm_g_2': 6.134,
     'diff_k_norm_g_2': 5.247,
     'lambda_q1_2': 5.697,
     'lambda_k1_2': 3.512,
     'diff_out_norm_g_2': 5.261,
     'ffn_norm_g_2': 3.408}
    for name, (base, spread) in spreads.items():
        noise = np.random.default_rng([zlib.crc32(name.encode()), seed]).standard_normal(out[name].shape)
        drawn = base * np.exp(spread * noise) if base else spread * noise
        out[name] = jnp.asarray(drawn.astype(out[name].dtype))
    for name, factor in factors.items():
        out[name] = (out[name] * factor).astype(out[name].dtype)
    return out
```

```python
import math
from contextlib import ExitStack, contextmanager

import numpy as np

import concourse.bass as bass
from concourse import mybir

F32 = mybir.dt.float32
F32R = mybir.dt.float32r
U8 = mybir.dt.uint8
ACT = mybir.ActivationFunctionType
ALU = mybir.AluOpType
AX = mybir.AxisListType

P = 128
T = 1024
D = 1024
KT = D // P
TT = T // P
HALF = 512
EPS = 1e-6

HG = 512
HGH = HG // P
SB_DH = 64
PAIRS = 512 // (2 * SB_DH)
FF_TILES = 2816 // P
MLA_H, MLA_NOPE, MLA_ROPE = 8, 64, 32
MLA_QK = MLA_NOPE + MLA_ROPE
DIFF_H = 4
NBUCKET = 32
LAM_INIT = 0.8 - 0.6 * math.exp(-0.3 * 0)
RING = 3
UNIT = 1024
LEVELS = [64, 32, 16, 8, 4, 2, 1]


class Count:

    def __init__(self, prog, name, by=1):
        self.sem = prog.ctx.enter_context(prog.nc.semaphore(name))
        self.name, self.by, self.const, self.rate, self.reg = name, by, 0, 0, None
        prog.counts[name] = self

    def inc(self, ins):
        ins.then_inc(self.sem, self.by)
        self.const += self.by
        return self.now()

    def now(self):
        return (self, self.const, self.rate, self.reg)


class Engine:

    def __init__(self, prog, e, name):
        self.e, self.name = e, name
        self.count = Count(prog, "done_" + name)
        self.seen = {}

    def need(self, *tickets):
        waited = False
        for t in tickets:
            if t is None:
                continue
            if isinstance(t, (list)):
                self.need(*t)
                continue
            c, const, rate, reg = t
            if rate == 0:
                if const <= 0 or self.seen.get(c.name, 0) >= const:
                    continue
                self.seen[c.name] = const
                self.e.wait_ge(c.sem, const)
            else:
                assert const >= 1, (c.name, const)
                if self.seen.get((c.name, rate), 0) >= const:
                    continue
                self.seen[(c.name, rate)] = const
                self.e.wait_ge(c.sem, reg * rate + const)
                waited = True
        if waited and self.name in ("act", "dve", "sp"):
            self.e.nop(nofuse=True)

    def did(self, ins):
        return self.count.inc(ins)


class Prog:
    def __init__(self, nc, ctx, rates):
        self.nc, self.ctx, self.counts, self.rates = nc, ctx, {}, rates
        self.loops = 0
        self.pe = Engine(self, nc.tensor, "pe")
        self.act = Engine(self, nc.scalar, "act")
        self.dve = Engine(self, nc.vector, "dve")
        self.pool = Engine(self, nc.gpsimd, "pool")
        self.sp = Engine(self, nc.sync, "sp")
        self.engines = [self.pe, self.act, self.dve, self.pool, self.sp]
        self.compute = [self.pe, self.act, self.dve, self.pool]

    def meet(self, extra=()):
        t = [e.count.now() for e in self.compute] + [c.now() for c in extra]
        for e in self.engines:
            e.need(*t)

    @contextmanager
    def loop(self, n):
        key = self.loops
        self.loops += 1
        rate = self.rates.get(key, {})
        start = {k: c.const for k, c in self.counts.items()}
        with self.nc.Fori(0, n, 1) as i:
            for e in self.engines:
                e.seen = {}
            for k, c in self.counts.items():
                c.rate, c.reg = rate.get(k, 0), i
                if c.rate and c.const == 0:
                    pass
            yield i
        for e in self.engines:
            e.seen = {}
        got = {k: c.const - start.get(k, 0) for k, c in self.counts.items()}
        if key in self.rates:
            assert {k: v for k, v in got.items() if v} == {k: v for k, v in rate.items() if v}
        self.rates[key] = got
        for k, c in self.counts.items():
            c.const = start.get(k, 0) + n * got[k]
            c.rate, c.reg = 0, None


class Stream:

    def __init__(self, pr, dram, sb):
        self.pr, self.dram = pr, dram
        self.raw = [sb(f"w_raw{s}", [P, UNIT], F32) for s in range(RING)]
        self.hi = [sb(f"w_hi{s}", [P, UNIT], F32R) for s in range(RING)]
        self.lo = [sb(f"w_lo{s}", [P, UNIT], F32R) for s in range(RING)]
        self.loaded = [Count(pr, f"w_loaded{s}", 16) for s in range(RING)]
        self.hi_done = [Count(pr, f"w_hi_done{s}") for s in range(RING)]
        self.lo_done = [Count(pr, f"w_lo_done{s}") for s in range(RING)]
        self.used = [Count(pr, f"w_used{s}") for s in range(RING)]
        self.g = 0
        self.total = dram.shape[0]

    def load(self, s, index):
        pr = self.pr
        pr.sp.need(self.hi_done[s].now(), self.lo_done[s].now())
        self.loaded[s].inc(pr.sp.e.dma_start(self.raw[s][:], self.dram[index]))

    def split(self, s):
        pr = self.pr
        pr.act.need(self.loaded[s].now(), self.used[s].now())
        hi = self.hi_done[s].inc(pr.act.e.activation(self.hi[s][:], self.raw[s][:], ACT.Copy))
        pr.dve.need(self.loaded[s].now(), self.used[s].now(), hi)
        self.lo_done[s].inc(pr.dve.e.tensor_tensor(
            self.lo[s][:], self.raw[s][:], self.hi[s][:].bitcast(F32), ALU.subtract))

    def start(self):
        for s in range(RING):
            self.load(s, s)
            self.split(s)

    def take(self, index):
        s = self.g % RING
        self.g += 1
        self.load(s, index + RING)
        self.pr.pe.need(self.hi_done[s].now(), self.lo_done[s].now())
        return s

    def give(self, s, last):
        return self.used[s].inc(last)


class Kernel:
    def __init__(self, nc, rates, a, out):
        self.nc, self.a, self.out_ap = nc, a, out
        with ExitStack() as ctx:
            self.pr = Prog(nc, ctx, rates)
            self.build(ctx)

    def sb(self, ctx, name, shape, dt=F32):
        return ctx.enter_context(self.nc.sbuf_tensor(name, shape, dt))

    def dma(self, dst, src):
        self.n_dma += 1
        c = Count(self.pr, f"dma_{self.n_dma}", 16)
        return c.inc(self.pr.sp.e.dma_start(dst, src))

    def mm3(self, banks, lh, ll, rh, rl, first, last):
        e, n = self.pr.pe.e, len(banks)
        for i in range(n):
            ins = e.matmul(banks[i], lh, rh[i], start=first, stop=False)
        for i in range(n):
            ins = e.matmul(banks[i], lh, rl[i], start=False, stop=False)
        for i in range(n):
            ins = e.matmul(banks[i], ll, rh[i], start=False, stop=last)
        return ins

    def split_to(self, hi, lo, src, after=(), src_ps=None):
        pr = self.pr
        pr.act.need(*after)
        h = pr.act.did(pr.act.e.activation(hi, src, ACT.Copy))
        pr.dve.need(*after, h)
        return h, pr.dve.did(pr.dve.e.tensor_tensor(lo, src, hi.bitcast(F32), ALU.subtract))

    def rstd(self, tiles, dim, acc, sq, rows=P, after=()):
        pr = self.pr
        act, dve, pe = pr.act, pr.dve, pr.pe
        act.need(*after)
        dve.need(*after)
        pe.need(*after)
        added = [None, None]
        a = act.did(act.e.activation(acc[0:rows], tiles[0], ACT.Square))
        for k in range(1, len(tiles)):
            act.need(added[k % 2])
            q = act.did(act.e.activation(sq[k % 2][0:rows], tiles[k], ACT.Square))
            dve.need(q, a)
            a = added[k % 2] = dve.did(dve.e.tensor_tensor(
                acc[0:rows], acc[0:rows], sq[k % 2][0:rows], ALU.add))
        pe.need(a, self.free[3].now())
        for h in range(2):
            s = pe.did(pe.e.matmul(self.PS[:, 6 + h, :], self.ones[0:rows, :],
                                   acc[0:rows, h * HALF:(h + 1) * HALF], start=True, stop=True))
        act.need(s, added[0], added[1])
        r = self.free[3].inc(act.e.activation(sq[0], self.pair(3), ACT.Sqrt,
                                              scale=1.0 / dim, bias=self.eps[:, 0:1]))
        dve.need(r)
        return dve.did(dve.e.reciprocal(acc, sq[0]))

    def normed(self, src, gain, r, r_done, UH, UL, tmp, after=()):
        pr = self.pr
        act, dve = pr.act, pr.dve
        act.need(*after)
        dve.need(*after, r_done)
        busy = [None, None]
        for k in range(len(src)):
            t = tmp[k % 2]
            dve.need(busy[k % 2])
            m = dve.did(dve.e.scalar_tensor_tensor(t, src[k], gain[:, k:k + 1], r, ALU.mult, ALU.mult))
            act.need(m)
            h = act.did(act.e.activation(UH[:, k, :], t, ACT.Copy))
            dve.need(h, m)
            busy[k % 2] = dve.did(dve.e.tensor_tensor(UL[:, k, :], t, UH[:, k, :].bitcast(F32), ALU.subtract))

    def pair(self, p):
        return self.PS[:, 2 * p:2 * p + 2, :].rearrange("p a b -> p (a b)")

    def claim(self):
        p = self.turn % 4
        self.turn += 1
        self.pr.pe.need(self.free[p].now())
        return p

    def product(self, index, UH, UL, kt=KT, width=P, offset=0, stride=None):
        pr, st = self.pr, self.st
        s = st.take(index)
        p, last = self.channels(s, UH, UL, range(kt), lambda k: slice(k * P, k * P + width), width)
        return p, st.give(s, last), s

    def channels(self, s, UH, UL, ks, cols, width=P):
        p = self.claim()
        ks = list(ks)
        for n, k in enumerate(ks):
            last = self.mm3([self.PS[0:width, 2 * p + h, :] for h in range(2)],
                            self.st.hi[s][:, cols(k)], self.st.lo[s][:, cols(k)],
                            [UH[:, k, h * HALF:(h + 1) * HALF] for h in range(2)],
                            [UL[:, k, h * HALF:(h + 1) * HALF] for h in range(2)],
                            n == 0, n == len(ks) - 1)
        return p, last

    def project(self, n, UH, UL, dst):
        pr, st = self.pr, self.st
        g0 = st.g

        def step(j, index):
            p, done, s = self.product(index, UH, UL)
            pr.act.need(done)
            self.free[p].inc(pr.act.e.activation(dst(j), self.pair(p), ACT.Copy))
            st.split(s)

        rounds = n // RING
        if rounds > 1:
            with pr.loop(rounds) as i:
                self.turn = 0
                for j in range(RING):
                    step(i * RING + j, i * RING + (g0 + j))
            st.g = g0 + rounds * RING
        else:
            rounds = 0
        self.turn = 0
        for j in range(rounds * RING, n):
            step(j, g0 + j)

    def project_tokens(self, UH, UL, dst):
        pr, st = self.pr, self.st
        pr.pe.need(*[f.now() for f in self.free])
        for m in range(KT // 2):
            s = st.take(st.g)
            for t in range(TT):
                for j in range(2):
                    k = 2 * m + j
                    tok = slice(t * P, (t + 1) * P)
                    wh, wl = (w[s][:, j * 512:(j + 1) * 512] for w in (st.hi, st.lo))
                    first, last = k == 0, k == KT - 1
                    pr.pe.e.matmul(self.PS[:, t, :], UH[:, k, tok], wh, start=first, stop=False)
                    pr.pe.e.matmul(self.PS[:, t, :], UH[:, k, tok], wl, start=False, stop=False)
                    ins = pr.pe.e.matmul(self.PS[:, t, :], UL[:, k, tok], wh, start=False, stop=last)
            done = st.give(s, ins)
            st.split(s)
        pr.act.need(done)
        pr.dve.need(done)
        for t in range(TT):
            if t % 2:
                self.free[t // 2].inc(pr.dve.e.tensor_copy(dst[:, t, :], self.PS[:, t, :]))
            else:
                self.free[t // 2].inc(pr.act.e.activation(dst[:, t, :], self.PS[:, t, :], ACT.Copy))

    def build(self, ctx):
        nc, pr, a = self.nc, self.pr, self.a
        self.n_dma = 0
        self.turn = 0
        sb = lambda n, s, dt=F32: self.sb(ctx, n, s, dt)
        self.PS = ctx.enter_context(nc.psum_tensor("PS", [P, 8, HALF], F32))
        self.free = [Count(pr, f"psum_free{p}") for p in range(4)]
        self.st = Stream(pr, a["weights"], sb)
        self.H = sb("H", [P, KT, T])
        self.ones = sb("ones", [P, P])
        self.eps = sb("eps", [P, 1])
        self.ident = sb("ident", [P, P])
        self.gains = sb("gains", [P, a["gains"].shape[1]])
        for p in range(4):
            self.free[p].inc(nc.vector.memset(self.pair(p), 0.0))
        first = self.sb(ctx, "first_marks", [P, 2])
        ready = [pr.dve.did(nc.vector.memset(self.ones[:], 1.0)),
                 pr.pool.did(nc.gpsimd.memset(first[:, 0:1], 0.0)),
                 pr.dve.did(nc.vector.memset(self.eps[:], EPS))]
        ready.append(self.dma(self.ident[:], a["ident"]))
        ready.append(self.dma(self.gains[:], a["gains"]))
        self.x_in = [self.dma(self.H[:, k, :], a["x_t"][k]) for k in range(KT)]
        self.st.start()
        for e in pr.engines:
            e.need(*ready)
        self.program(ctx)

    def g(self, name):
        at, n = self.at[name]
        return self.gains[:, at:at + n]

    def program(self, ctx):
        with ExitStack() as c:
            self.first_mixer(c)
        self.first_output()
        self.feed_forward(conv=False)
        self.ple(self.a["p_t"], norm=None)
        self.second_mixer()
        self.feed_forward(conv=True)
        self.ple(self.a["p2_t"], norm="ple_norm_g_2")
        self.store()

    def operand(self, ctx, tag):
        return [self.sb(ctx, f"u_{x}_{tag}", [P, KT, T], F32R) for x in ("hi", "lo")]

    def first_mixer(self, ctx):
        pr, H = self.pr, self.H
        act, dve, pool, pe = pr.act, pr.dve, pr.pool, pr.pe
        big = self.sb(ctx, "mixer1", [P, 12, T])
        tok = lambda k: big[:, k:k + 4, :].rearrange("p a b -> p (a b)").rearrange(
            "p (t n) -> p t n", n=512)
        with ExitStack() as c:
            UH, UL = self.operand(c, "1")
            for e in (act, dve):
                e.need(*self.x_in)
            x = [H[:, k, :] for k in range(KT)]
            r = self.rstd(x, D, big[:, 0, :], [big[:, 1, :], big[:, 2, :]])
            self.normed(x, self.g("attn_pre_norm"), big[:, 0, :], r, UH, UL, [big[:, 1, :], big[:, 2, :]])
            pr.meet()
            self.project(8, UH, UL, lambda j: H[:, j, :])
            pr.meet()
            self.project(4, UH, UL, lambda j: big[:, j, :])
            self.project_tokens(UH, UL, tok(4))
            pr.meet(self.free)
            with ExitStack() as h:
                self.hgrn(h, big, tok(4))
            pr.meet(self.free)
            self.project(8, UH, UL, lambda j: big[:, j, :])
            self.project_tokens(UH, UL, tok(8))
            pr.meet(self.free)
        with ExitStack() as c:
            self.stick_breaking(c, big, tok(8))
        pr.meet(self.free)

    def hgrn(self, ctx, big, V):
        pr, H, PS = self.pr, self.H, self.PS
        act, dve, pool, pe = pr.act, pr.dve, pr.pool, pr.pe
        e_t = [big[:, 8, :], big[:, 9, :]]
        x_t = [big[:, 10, :], big[:, 11, :]]
        kk = self.sb(ctx, "hg_k", [P, T])
        b = self.sb(ctx, "hg_b", [P, T])
        scores = self.sb(ctx, "hg_scores", [P, TT, P])
        vj = self.sb(ctx, "hg_v", [P, TT, P])
        state = [self.sb(ctx, f"hg_state{i}", [P, P]) for i in range(2)]
        last_decay = self.sb(ctx, "hg_last", [P, TT, 1])
        lb = self.sb(ctx, "hg_lb", [P, HGH, 1])
        olb = self.sb(ctx, "hg_olb", [P, HGH, 1])
        tmp = self.sb(ctx, "hg_tmp", [P, HGH])
        masks = self.sb(ctx, "hg_masks", [P, len(LEVELS) + 1, P], U8)
        m_in = self.dma(kk[:].rearrange("p (a b) -> p a b", b=P), self.a["levels"])
        g0, g1 = self.g("gamma0"), self.g("gamma1")
        lb2, olb2 = lb[:].rearrange("p a b -> p (a b)"), olb[:].rearrange("p a b -> p (a b)")
        t = dve.did(dve.e.tensor_tensor(tmp[:], g0, g1, ALU.max))
        dve.need(t)
        dve.did(dve.e.tensor_tensor(lb2, g0, tmp[:], ALU.subtract))
        t = dve.did(dve.e.tensor_tensor(olb2, g1, tmp[:], ALU.subtract))
        act.need(t)
        act.did(act.e.activation(lb2, lb2, ACT.Exp))
        t = act.did(act.e.activation(olb2, olb2, ACT.Exp))
        dve.need(t)
        t = dve.did(dve.e.tensor_tensor(tmp[:], lb2, olb2, ALU.add))
        dve.need(t)
        t = dve.did(dve.e.reciprocal(tmp[:], tmp[:]))
        dve.need(t)
        dve.did(dve.e.tensor_tensor(lb2, lb2, tmp[:], ALU.mult))
        dve.did(dve.e.tensor_tensor(olb2, olb2, tmp[:], ALU.mult))
        dve.did(dve.e.memset(scores[:], 0.0))
        dve.need(m_in)
        dve.did(dve.e.tensor_copy(masks[:], kk[:].rearrange("p (a b) -> p a b", b=P)))
        flat = lambda x: x.rearrange("p a b -> p (a b)")

        with pr.loop(HGH) as j:
            pr.meet()
            q, z = H[:, j, :], H[:, j + 4, :]
            s = act.did(act.e.activation(x_t[0], q, ACT.Sigmoid))
            s1 = act.did(act.e.activation(e_t[0], z, ACT.Sigmoid))
            s2 = act.did(act.e.activation(e_t[1], z, ACT.Sigmoid, scale=-1.0))
            dve.need(s)
            q_done = dve.did(dve.e.tensor_tensor(q, q, x_t[0], ALU.mult))
            dve.need(s1, s2)
            f = dve.did(dve.e.tensor_scalar(z, e_t[0], olb[:, j, :], lb[:, j, :], ALU.mult, ALU.add))
            k_done = dve.did(dve.e.tensor_scalar(kk[:], e_t[1], olb[:, j, :], None, ALU.mult))
            dve.need(f)
            f = dve.did(dve.e.tensor_scalar(z, z, 1e-19, None, ALU.max))
            pool.e.tensor_copy(vj[:], V[:, :, bass.ds(j * P, P)]).then_inc(pool.count.sem, 1)
            pool.count.const += 1
            v_done = pool.count.now()
            act.need(f)
            lf = act.did(act.e.activation(z, z, ACT.Ln))
            dve.need(lf)
            for c in range(TT):
                ch = slice(c * P, (c + 1) * P)
                b_done = dve.did(dve.e.tensor_tensor_scan(
                    b[:, ch], H[:, j + 4, ch], H[:, j + 4, ch], 0.0, ALU.add, ALU.bypass))
            dve.need(b_done, q_done, k_done)
            pool.need(b_done, q_done, k_done)
            pe.need(k_done, q_done)

            def keep(level, ps_pair, prods):
                dve.need(prods)
                ps = self.pair(ps_pair).rearrange("p (a b) -> p a b", b=P)
                m = masks[:, level:level + 1, :].to_broadcast([P, TT, P])
                got = dve.did(dve.e.copy_predicated(scores[:], m, ps))
                return got

            used = [None, None]
            got = [None, None]
            kept = None
            for n, h in enumerate(LEVELS):
                w = n % 2
                blocks = lambda ap: ap.rearrange("p (n c) -> p n c", c=2 * h)
                bb, ee, xx = blocks(b[:]), blocks(e_t[w]), blocks(x_t[w])
                qq, k3 = blocks(q), blocks(kk[:])
                nb = T // (2 * h)
                dve.need(used[w])
                e = dve.did(dve.e.tensor_tensor(ee, bb, bb[:, :, h - 1:h].to_broadcast([P, nb, 2 * h]),
                                                ALU.subtract))
                act.need(e)
                up = act.did(act.e.activation(ee[:, :, h:], ee[:, :, h:], ACT.Exp))
                lo = act.did(act.e.activation(ee[:, :, :h], ee[:, :, :h], ACT.Exp, scale=-1.0))
                pool.need(lo, used[w])
                xl = pool.did(pool.e.tensor_tensor(xx[:, :, :h], k3[:, :, :h], ee[:, :, :h], ALU.mult))
                dve.need(up)
                xu = dve.did(dve.e.tensor_tensor(xx[:, :, h:], qq[:, :, h:], ee[:, :, h:], ALU.mult))
                pe.need(xl, xu, got[w])
                for c in range(TT):
                    ch = slice(c * P, (c + 1) * P)
                    mm = pe.did(pe.e.matmul(self.pair(w)[:, ch], x_t[w][:, ch], x_t[w][:, ch],
                                            start=True, stop=True))
                used[w] = [mm, xl, xu]
                if n:
                    dve.need(kept)
                    kept = got[1 - w] = keep(n - 1, 1 - w, prods)
                prods = mm
            dve.need(kept)
            kept = got[w] = keep(len(LEVELS) - 1, w, prods)
            w = 1 - w
            pe.need(got[w])
            for c in range(TT):
                ch = slice(c * P, (c + 1) * P)
                mm = pe.did(pe.e.matmul(self.pair(w)[:, ch], kk[:, ch], H[:, j, ch], start=True, stop=True))
            dve.need(kept)
            kept = keep(len(LEVELS), w, mm)
            b3, e3 = (t.rearrange("p (n c) -> p n c", c=P) for t in (b[:], e_t[1]))
            dve.need(used[0], used[1])
            e = dve.did(dve.e.tensor_tensor(e3, b3, b3[:, :, P - 1:P].to_broadcast([P, TT, P]), ALU.subtract))
            act.need(used[0], used[1])
            qe = act.did(act.e.activation(e_t[0], b[:], ACT.Exp))
            act.need(e)
            ke = act.did(act.e.activation(e_t[1], e_t[1], ACT.Exp, scale=-1.0))
            gl = act.did(act.e.activation(last_decay[:], b3[:, :, P - 1:P], ACT.Exp))
            dve.need(qe)
            qe = dve.did(dve.e.tensor_tensor(x_t[0], q, e_t[0], ALU.mult))
            pool.need(ke)
            ke = pool.did(pool.e.tensor_tensor(x_t[1], kk[:], e_t[1], ALU.mult))
            pe.need(ke, kept)
            for c in range(TT):
                ch = slice(c * P, (c + 1) * P)
                mm = pe.did(pe.e.transpose(self.pair(0)[:, ch], x_t[1][:, ch], self.ident[:]))
            act.need(mm, gl, qe)
            kt = act.did(act.e.activation(b[:], self.pair(0), ACT.Copy))
            pe.need(kt, v_done)
            for c in range(TT):
                ch = slice(c * P, (c + 1) * P)
                upd = pe.did(pe.e.matmul(self.pair(3)[:, ch], b[:, ch], vj[:, c, :], start=True, stop=True))
            st = None
            pe.need(qe)
            for c in range(TT):
                ch = slice(c * P, (c + 1) * P)
                o = pe.did(pe.e.matmul(self.pair(2)[:, ch], vj[:, c, :], scores[:, c, :],
                                       start=True, stop=c == 0))
                if c:
                    pe.need(st)
                    o = pe.did(pe.e.matmul(self.pair(2)[:, ch], state[c % 2][:], x_t[0][:, ch],
                                           start=False, stop=True))
                if c == TT - 1:
                    break
                dve.need(upd, st, o_prev if c else None)
                if c == 0:
                    st = dve.did(dve.e.tensor_copy(state[1][:], self.pair(3)[:, ch]))
                else:
                    st = dve.did(dve.e.scalar_tensor_tensor(
                        state[(c + 1) % 2][:], state[c % 2][:], last_decay[:, c, :], self.pair(3)[:, ch],
                        ALU.mult, ALU.add))
                o_prev = o
            act.need(o, qe)
            act.did(act.e.activation(H[:, j, :], self.pair(2), ACT.Copy))
        pr.meet()
        r = self.rstd([H[:, k, :] for k in range(HGH)], HG, kk[:], [x_t[0], x_t[1]])
        self.gated(H, big, self.g("hg_out_norm"), kk[:], r, e_t)

    def gated(self, H, big, gain, rr, r, tmp):
        pr = self.pr
        act, dve = pr.act, pr.dve
        busy = [None, None]
        for k in range(HGH):
            t = tmp[k % 2]
            act.need(busy[k % 2])
            s = act.did(act.e.activation(t, big[:, k, :], ACT.Sigmoid))
            dve.need(r)
            n = dve.did(dve.e.scalar_tensor_tensor(H[:, k, :], H[:, k, :], gain[:, k:k + 1], rr,
                                                   ALU.mult, ALU.mult))
            dve.need(s)
            m = dve.did(dve.e.tensor_tensor(t, t, big[:, k, :], ALU.mult))
            dve.need(m, n)
            busy[k % 2] = dve.did(dve.e.tensor_tensor(H[:, k, :], H[:, k, :], t, ALU.mult))

    def attend(self, items, width, scores, weigh, VH, VL, evac, at_hi, at_lo, a_buf):
        pr, PS = self.pr, self.PS
        act, dve, pe = pr.act, pr.dve, pr.pe
        N, depth = len(items), len(at_hi)
        ready, split, av, out = {}, {}, {}, {}
        turned = {}
        for step in range(N + 2):
            n = step
            if n < N:
                ready[n] = weigh(n, items[n], scores(n, items[n]), turned.get(n - 2))
            n = step - 1
            if 0 <= n < N:
                blocks = width(items[n])
                pe.need(ready[n], split.get(n - 1))
                for b in range(blocks):
                    mm = pe.e.transpose(self.pair(2)[:, b * P:(b + 1) * P],
                                        a_buf[n % 2][:, b * P:(b + 1) * P], self.ident[:])
                turned[n] = pe.did(mm)
            n = step - 2
            if 0 <= n < N:
                blocks, w = width(items[n]), n % depth
                bank = PS[:, 6 + n % 2, 0:P]
                pe.need(split[n], out.get(n - 2))
                for b in range(blocks):
                    cols = slice(b * P, (b + 1) * P)
                    mm = self.mm3([bank], VH[:, b, :], VL[:, b, :], [at_hi[w][:, cols]], [at_lo[w][:, cols]],
                                  b == 0, b == blocks - 1)
                av[n] = pe.did(mm)
                out[n] = evac(n, items[n], bank, av[n])
            n = step - 1
            if 0 <= n < N:
                w, cols = n % depth, slice(0, width(items[n]) * P)
                act.need(turned[n], av.get(n - depth))
                h = act.did(act.e.activation(at_hi[w][:, cols], self.pair(2)[:, cols], ACT.Copy))
                dve.need(turned[n], h, av.get(n - depth))
                lo = dve.did(dve.e.tensor_tensor(at_lo[w][:, cols], self.pair(2)[:, cols],
                                                 at_hi[w][:, cols].bitcast(F32), ALU.subtract))
                split[n] = [h, lo]

    def attention_tiles(self, ctx, tag):
        hi = [self.sb(ctx, f"{tag}_at_hi{i}", [P, T], F32R) for i in range(2)]
        lo = [self.sb(ctx, f"{tag}_at_lo{i}", [P, T], F32R) for i in range(2)]
        return hi, lo

    def banks_of(self, pair, cols):
        return [(self.PS[:, 2 * pair + h, 0:min(HALF, cols - h * HALF)], h * HALF, min(HALF, cols - h * HALF))
                for h in range(2) if cols > h * HALF]

    def score(self, pair, cols, qh, ql, kh, kl):
        for ps, c0, n in self.banks_of(pair, cols):
            mm = self.mm3([ps], qh, ql, [kh[:, c0:c0 + n]], [kl[:, c0:c0 + n]], True, True)
        return self.pr.pe.did(mm)

    def split_pair(self, i, V, VH, VL):
        return self.split_to(VH[:], VL[:], V[:, :, bass.ds(i * P, P)])

    def stick_breaking(self, ctx, big, V):
        pr, H, PS = self.pr, self.H, self.PS
        act, dve, pool, pe = pr.act, pr.dve, pr.pool, pr.pe
        sb = lambda n, s, dt=F32: self.sb(ctx, n, s, dt)
        QH, QL, KH, KL = (sb(f"sb_{n}", [P, T], F32R) for n in ("qh", "ql", "kh", "kl"))
        VH, VL = (sb(f"sb_{n}", [P, TT, P], F32R) for n in ("vh", "vl"))
        om = [sb(f"sb_om{i}", [P, T]) for i in range(2)]
        be = [sb(f"sb_beta{i}", [P, T]) for i in range(2)]
        rem = [sb(f"sb_rem{i}", [P, T + 1]) for i in range(2)]
        at_hi, at_lo = self.attention_tiles(ctx, "sb")
        strict, loose = sb("sb_strict", [P, P]), sb("sb_loose", [P, P])
        dve.need(self.dma(strict[:], self.a["strict"]))
        dve.did(dve.e.tensor_scalar(loose[:], strict[:], -1.0, 1.0, ALU.mult, ALU.add))
        scale = SB_DH ** -0.5
        with pr.loop(PAIRS) as i:
            pr.meet()
            ready = [self.split_to(QH[:], QL[:], big[:, i, :]), self.split_to(KH[:], KL[:], big[:, i + 4, :])]
            ready.append(self.split_pair(i, V, VH, VL))
            pe.need(*[list(r) for r in ready])
            items = [(hh, t) for hh in range(2) for t in range(TT)]
            read, scanned = {}, {}

            def scores(n, item):
                hh, t = item
                rows = slice(hh * SB_DH, (hh + 1) * SB_DH)
                pe.need(read.get(n - 2))
                tk = slice(t * P, (t + 1) * P)
                return self.score(n % 2, (t + 1) * P, QH[rows, tk], QL[rows, tk], KH[rows, :], KL[rows, :])

            def weigh(n, item, z, free):
                w, cols = n % 2, (item[1] + 1) * P
                diag = slice(cols - P, cols)
                ps = self.pair(w)[:, 0:cols]
                act.need(z, scanned.get(n - 2), free)
                o = act.did(act.e.activation(om[w][:, 0:cols], ps, ACT.Sigmoid, scale=-scale))
                b = read[n] = act.did(act.e.activation(be[w][:, 0:cols], ps, ACT.Sigmoid, scale=scale))
                dve.need(o, scanned.get(n - 2))
                one = dve.did(dve.e.memset(rem[w][:, cols:cols + 1], 1.0))
                m = dve.did(dve.e.tensor_tensor(om[w][:, diag], om[w][:, diag], loose[:], ALU.max))
                pool.need(b)
                m2 = pool.did(pool.e.tensor_tensor(be[w][:, diag], be[w][:, diag], strict[:], ALU.mult))
                dve.need(m)
                back = lambda ap: ap[:, 0:cols][:, ::-1]
                r = dve.did(dve.e.tensor_tensor_scan(back(rem[w]), back(om[w]), back(om[w]),
                                                     1.0, ALU.mult, ALU.bypass))
                pool.need(r, one, m2)
                a = scanned[n] = pool.did(pool.e.tensor_tensor(
                    be[w][:, 0:cols], be[w][:, 0:cols], rem[w][:, 1:cols + 1], ALU.mult))
                return a

            def evac(n, item, bank, done):
                hh, t = item
                rows = slice(hh * SB_DH, (hh + 1) * SB_DH)
                dve.need(done)
                return dve.did(dve.e.tensor_copy(H[rows, i + 4, t * P:(t + 1) * P], bank[rows, :]))

            self.attend(items, lambda it: it[1] + 1, scores, weigh, VH, VL, evac, at_hi, at_lo, be)

    def first_output(self):
        pr, H = self.pr, self.H
        act, dve = pr.act, pr.dve
        with ExitStack() as c:
            Y = self.sb(c, "mix1", [P, KT, T])
            UH, UL = self.operand(c, "o1")
            acc, s0, s1 = (self.sb(c, f"o1_t{k}", [P, T]) for k in range(3))
            sbo = [H[:, 4 + k, :] for k in range(4)]
            r = self.rstd(sbo, HG, acc[:], [s0[:], s1[:]])
            self.normed(sbo, self.g("sb_out_norm"), acc[:], r, UH[:, 4:8, :], UL[:, 4:8, :], [s0[:], s1[:]])
            for k in range(4):
                self.split_to(UH[:, k, :], UL[:, k, :], H[:, k, :])
            pr.meet()
            x_in = [self.dma(H[:, k, :], self.a["x_t"][k]) for k in range(KT)]
            self.project(8, UH, UL, lambda j: Y[:, j, :])
            pr.meet()
            for e in pr.compute:
                e.need(*x_in)
            self.add_normed(Y, self.g("attn_post_norm"), acc, s0, s1)
            pr.meet()

    def add_normed(self, Y, gain, acc, s0, s1):
        pr, H = self.pr, self.H
        dve, pool = pr.dve, pr.pool
        r = self.rstd([Y[:, k, :] for k in range(KT)], D, acc[:], [s0[:], s1[:]])
        for k in range(KT):
            dve.need(r)
            m = dve.did(dve.e.scalar_tensor_tensor(Y[:, k, :], Y[:, k, :], gain[:, k:k + 1], acc[:],
                                                   ALU.mult, ALU.mult))
            e = pool if k % 3 == 2 else dve
            e.need(m)
            e.did(e.e.tensor_tensor(H[:, k, :], H[:, k, :], Y[:, k, :], ALU.add))

    def feed_forward(self, conv):
        pr, H, st = self.pr, self.H, self.st
        act, dve, pool, pe = pr.act, pr.dve, pr.pool, pr.pe
        tag = "f2" if conv else "f1"
        with ExitStack() as c:
            UH, UL = self.operand(c, tag)
            Y = self.sb(c, f"{tag}_y", [P, KT, T]) if not conv else None
            AH, AL = (self.sb(c, f"{tag}_a{x}", [P, 2, T], F32R) for x in "hl")
            sg = self.sb(c, f"{tag}_gate", [P, T])
            prod = self.sb(c, f"{tag}_prod", [P, T])
            cw = self.sb(c, f"{tag}_cw", [P, 4]) if conv else None
            x = [H[:, k, :] for k in range(KT)]
            with ExitStack() as c2:
                acc = self.sb(c2, f"{tag}_acc", [P, T])
                r = self.rstd(x, D, acc[:], [sg[:], prod[:]])
                self.normed(x, self.g("ffn_norm_g_2" if conv else "ffn_pre_norm"), acc[:], r, UH, UL,
                            [sg[:], prod[:]])
                pr.meet()
            if conv:
                Y = H
            else:
                for k in range(KT):
                    pool.did(pool.e.memset(Y[:, k, :], 0.0))
            last = {}

            def gate(index, tile):
                p, done, s = self.product(index, UH, UL)
                if conv:
                    dve.need(pr.act.count.now(), pr.dve.count.now())
                    for n in range(4):
                        at, _ = self.at[f"conv_w{n}" if n < 3 else "conv_b"]
                        w = dve.did(dve.e.tensor_copy(cw[:, n:n + 1], self.gains[:, bass.ds(tile + at, 1)]))
                    act.need(done, w)
                    act.need(pr.dve.count.now())
                    g = act.did(act.e.activation(sg[:], self.pair(p), ACT.Identity,
                                                 scale=cw[:, 2:3], bias=cw[:, 3:4]))
                    for d, col in ((1, 1), (2, 0)):
                        dve.need(g)
                        g = dve.did(dve.e.scalar_tensor_tensor(
                            sg[:, d:], self.pair(p)[:, :T - d], cw[:, col:col + 1], sg[:, d:], ALU.mult, ALU.add))
                    act.need(g)
                    g = self.free[p].inc(act.e.activation(sg[:], sg[:], ACT.Silu))
                else:
                    act.need(done, pr.dve.count.now())
                    g = self.free[p].inc(act.e.activation(sg[:], self.pair(p), ACT.Silu))
                st.split(s)
                return g

            def up(index, j, g):
                p, done, s = self.product(index, UH, UL)
                dve.need(done, g, pr.act.count.now(), pr.dve.count.now())
                m = self.free[p].inc(dve.e.tensor_tensor(prod[:], sg[:], self.pair(p), ALU.mult))
                self.split_to(AH[:, j, :], AL[:, j, :], prod[:], after=(m, done))
                st.split(s)

            def down(index):
                s0, s1 = st.take(index), st.take(index + 1)
                pe.need(pr.act.count.now(), pr.dve.count.now())
                for n in range(KT):
                    p = self.claim()
                    for k, s in enumerate((s0, s1)):
                        mm = self.mm3([PS[:, 2 * p + h, :] for h in range(2)],
                                      st.hi[s][:, n * P:(n + 1) * P], st.lo[s][:, n * P:(n + 1) * P],
                                      [AH[:, k, h * HALF:(h + 1) * HALF] for h in range(2)],
                                      [AL[:, k, h * HALF:(h + 1) * HALF] for h in range(2)], k == 0, k == 1)
                        if n == KT - 1:
                            done = st.give(s, mm)
                        else:
                            done = pe.did(mm) if k else None
                    dve.need(done, self.free[p].now())
                    self.free[p].inc(dve.e.tensor_tensor(Y[:, n, :], Y[:, n, :], self.pair(p), ALU.add))
                st.split(s0)
                st.split(s1)

            PS = self.PS
            g0 = st.g
            pr.meet()
            self.turn = 0
            g = gate(g0, 0)
            up(g0 + 1, 0, g)
            g = gate(g0 + 2, 1)
            up(g0 + 3, 1, g)
            base = st.g
            with pr.loop(FF_TILES // 2 - 1) as i:
                self.turn = 0
                at = i * 6
                g = gate(at + base, i * 2 + 2)
                down(at + (base + 1))
                up(at + (base + 3), 0, g)
                g = gate(at + (base + 4), i * 2 + 3)
                up(at + (base + 5), 1, g)
            st.g = base + 6 * (FF_TILES // 2 - 1)
            self.turn = 1
            down(st.g)
            pr.meet(self.free)
            if not conv:
                self.add_normed(Y, self.g("ffn_post_norm"), sg, prod, self.sb(c, f"{tag}_last", [P, T]))
            pr.meet()

    def ple(self, p_dram, norm):
        pr, H, st = self.pr, self.H, self.st
        act, dve, pool, pe = pr.act, pr.dve, pr.pool, pr.pe
        tag = "p2" if norm else "p1"
        with ExitStack() as c:
            UH, UL = self.operand(c, tag)
            PP = self.sb(c, f"{tag}_pp", [P, KT, T])
            sg = [self.sb(c, f"{tag}_s{i}", [P, T]) for i in range(3)]
            raw = [self.dma(PP[:, k, :], p_dram[k]) for k in range(2)]
            x = [H[:, k, :] for k in range(KT)]
            ready = [list(self.split_to(UH[:, k, :], UL[:, k, :], PP[:, k, :], after=(raw[k],))) for k in range(2)]
            pe.need(*ready)
            act.need(*ready)
            self.turn = 0
            for half in range(2):
                s = st.take(st.g)
                for n in range(4):
                    p, mm = self.channels(s, UH, UL, range(2), lambda k: slice((2 * n + k) * P, (2 * n + k + 1) * P))
                    done = st.give(s, mm) if n == 3 else pe.did(mm)
                    act.need(done)
                    self.free[p].inc(act.e.activation(PP[:, 4 * half + n, :], self.pair(p), ACT.Copy))
                st.split(s)
            pr.meet(self.free)
            if norm:
                r = self.rstd(x, D, sg[2][:], [sg[0][:], sg[1][:]])
                self.normed(x, self.g(norm), sg[2][:], r, UH, UL, [sg[0][:], sg[1][:]])
            else:
                for k in range(KT):
                    self.split_to(UH[:, k, :], UL[:, k, :], x[k])
            pr.meet(self.free)
            g0 = st.g

            def step(j, index):
                p, done, s = self.product(index, UH, UL)
                act.need(done, pr.dve.count.now())
                g = self.free[p].inc(act.e.activation(sg[0][:], self.pair(p), ACT.Sigmoid))
                dve.need(g, pr.dve.count.now())
                m = dve.did(dve.e.tensor_tensor(sg[0][:], sg[0][:], PP[:, j, :], ALU.mult))
                dve.need(m)
                dve.did(dve.e.tensor_tensor(H[:, j, :], H[:, j, :], sg[0][:], ALU.add))
                st.split(s)

            with pr.loop(2) as i:
                self.turn = 0
                for j in range(RING):
                    step(i * RING + j, i * RING + (g0 + j))
            st.g = g0 + 2 * RING
            self.turn = 0
            for j in range(2 * RING, KT):
                step(j, g0 + j)
            pr.meet(self.free)

    def second_mixer(self):
        pr, H = self.pr, self.H
        act, dve, pool, pe = pr.act, pr.dve, pr.pool, pr.pe
        x = [H[:, k, :] for k in range(KT)]
        with ExitStack() as c:
            res = self.sb(c, "mixer2", [P, 16, T])
            tok = res[:, 8:12, :].rearrange("p a b -> p (a b)").rearrange("p (t n) -> p t n", n=512)
            with ExitStack() as cu:
                UH, UL = self.operand(cu, "2")
                r = self.rstd(x, D, res[:, 0, :], [res[:, 1, :], res[:, 2, :]])
                self.normed(x, self.g("attn_norm_g_2"), res[:, 0, :], r, UH, UL, [res[:, 1, :], res[:, 2, :]])
                pr.meet(self.free)
                self.project(4, UH, UL, lambda j: res[:, j + 12, :])
                pr.meet(self.free)
                self.project(8, UH, UL, lambda j: res[:, j, :])
                self.project_tokens(UH, UL, tok)
                pr.meet(self.free)
            with ExitStack() as cd:
                self.differential(cd, res, tok)
            pr.meet(self.free)
            with ExitStack() as cm:
                self.mla(cm, res)
            pr.meet(self.free)
            with ExitStack() as co:
                self.second_output(co, res)
            pr.meet(self.free)

    def second_output(self, ctx, res):
        pr, H, st = self.pr, self.H, self.st
        act, dve, pe = pr.act, pr.dve, pr.pe
        UH, UL = self.operand(ctx, "o2")
        for k in range(KT):
            self.split_to(UH[:, k, :], UL[:, k, :], res[:, k, :])
        pr.meet(self.free)
        g0 = st.g

        def step(j, index):
            p, done, s = self.product(index, UH, UL)
            dve.need(done)
            self.free[p].inc(dve.e.tensor_tensor(H[:, j, :], H[:, j, :], self.pair(p), ALU.add))
            st.split(s)

        with pr.loop(2) as i:
            self.turn = 0
            for j in range(RING):
                step(i * RING + j, i * RING + (g0 + j))
        st.g = g0 + 2 * RING
        self.turn = 0
        for j in range(2 * RING, KT):
            step(j, g0 + j)

    def group_rstd(self, src, rows, ones, dim, acc, sq):
        pr = self.pr
        act, dve, pe = pr.act, pr.dve, pr.pe
        q = act.did(act.e.activation(sq[0:rows], src, ACT.Square))
        pe.need(q)
        for h in range(2):
            s = pe.did(pe.e.matmul(self.PS[0:rows, 6 + h, :], ones[0:rows, 0:rows],
                                   sq[0:rows, h * HALF:(h + 1) * HALF], start=True, stop=True))
        act.need(s)
        t = act.did(act.e.activation(acc[0:rows], self.pair(3)[0:rows], ACT.Sqrt, scale=1.0 / dim,
                                     bias=self.eps[0:rows, 0:1]))
        dve.need(t)
        return dve.did(dve.e.reciprocal(acc[0:rows], acc[0:rows]))

    def differential(self, ctx, res, V):
        pr, PS = self.pr, self.PS
        act, dve, pool, pe = pr.act, pr.dve, pr.pool, pr.pe
        sb = lambda n, s, dt=F32: self.sb(ctx, n, s, dt)
        QH, QL, KH, KL = (sb(f"df_{n}", [P, T], F32R) for n in ("qh", "ql", "kh", "kl"))
        VH, VL = (sb(f"df_{n}", [P, TT, P], F32R) for n in ("vh", "vl"))
        toep = sb("df_bias", [P, T])
        pm = [sb(f"df_p{i}", [P, T]) for i in range(4)]
        at_hi, at_lo = self.attention_tiles(ctx, "df")
        small = sb("df_small", [P, 2, 8])
        ones2 = sb("df_ones2", [P, P])
        gq, lam2, nlam = sb("df_gq", [P, 1]), sb("df_lam2", [P, 2]), sb("df_nlam", [P, 1])
        gout = sb("df_gout", [P, 1])
        dve.did(dve.e.memset(ones2[:], 0.0))
        dve.need(dve.count.now())
        dve.did(dve.e.memset(ones2[0:64, 0:64], 1.0))
        dve.did(dve.e.memset(ones2[64:P, 64:P], 1.0))
        scale = 64 ** -0.5
        dve.did(dve.e.tensor_scalar(gq[:], self.g("diff_q_norm_g_2"), scale, None, ALU.mult))
        dve.did(dve.e.tensor_scalar(gout[:], self.g("diff_out_norm_g_2"), 1.0 - LAM_INIT, None, ALU.mult))
        for n in range(2):
            dve.did(dve.e.tensor_tensor(lam2[:, n:n + 1], self.g(f"lambda_q{n + 1}_2"), self.g(f"lambda_k{n + 1}_2"),
                                        ALU.mult))
        pe.need(dve.count.now())
        t = pe.did(pe.e.matmul(PS[:, 0, 0:2], self.ones[:], lam2[:], start=True, stop=True))
        act.need(t)
        t = act.did(act.e.activation(lam2[:], PS[:, 0, 0:2], ACT.Exp))
        dve.need(t)
        t = dve.did(dve.e.tensor_tensor(nlam[:], lam2[:, 1:2], lam2[:, 0:1], ALU.subtract))
        dve.need(t)
        dve.did(dve.e.tensor_scalar(nlam[:], nlam[:], -LAM_INIT, None, ALU.add))
        table, spread = sb("df_table", [NBUCKET, DIFF_H]), sb("df_spread", [NBUCKET, P])
        rest = BIAS_LEN - T
        bucket0, bucket1 = pm[0][0:NBUCKET, :], pm[1][0:NBUCKET, 0:rest]
        ins = [self.dma(table[:], self.a["rel_bias"]), self.dma(bucket0, self.a["bucket"][:, 0:T]),
               self.dma(bucket1, self.a["bucket"][:, T:BIAS_LEN])]
        lines = self.nc.dram_tensor("bias_lines", (DIFF_H, P, BIAS_LEN), F32)
        pe.need(*ins)
        dve.need(*ins)
        wrote = None
        for h in range(DIFF_H):
            dve.need(pe.count.now())
            t = dve.did(dve.e.tensor_scalar(spread[:], self.ones[0:NBUCKET, :], table[:, h:h + 1], None, ALU.mult))
            pe.need(t, act.count.now())
            pe.e.matmul(PS[:, 2, :], spread[:], bucket0[:, 0:HALF], start=True, stop=True)
            pe.e.matmul(PS[:, 3, :], spread[:], bucket0[:, HALF:T], start=True, stop=True)
            t = pe.did(pe.e.matmul(PS[:, 4, 0:rest], spread[:], bucket1, start=True, stop=True))
            act.need(t, wrote)
            act.did(act.e.activation(pm[2][:], self.pair(1), ACT.Copy))
            t = act.did(act.e.activation(pm[3][:, 0:rest], PS[:, 4, 0:rest], ACT.Copy))
            pr.sp.need(t)
            wrote = [self.dma(lines.ap()[h, :, 0:T], pm[2][:]),
                     self.dma(lines.ap()[h, :, T:BIAS_LEN], pm[3][:, 0:rest])]
            pr.sp.need(wrote)
        for e in (act, dve):
            e.need(wrote)
        bias_in = Count(pr, "df_bias_in", 16)
        toeplitz = bass.AP(lines, P - 1, [[P * BIAS_LEN, DIFF_H], [BIAS_LEN - 1, P], [1, T]])

        with pr.loop(DIFF_H) as h:
            pr.meet()
            b = bias_in.inc(pr.sp.e.dma_start(toep[:], toeplitz[h]))
            ready = []
            for src, gain, hi, lo in ((res[:, h, :], gq[:], QH, QL),
                                      (res[:, h + 4, :], self.g("diff_k_norm_g_2"), KH, KL)):
                r = self.group_rstd(src, P, ones2, 64, pm[0], pm[1])
                dve.need(r)
                m = dve.did(dve.e.scalar_tensor_tensor(pm[2][:], src, gain, pm[0][:], ALU.mult, ALU.mult))
                ready.append(list(self.split_to(hi[:], lo[:], pm[2][:], after=(m,))))
                for e in (act, dve):
                    e.need(*ready[-1])
            ready.append(list(self.split_pair(h, V, VH, VL)))
            pe.need(*ready)
            dve.need(b)
            read, weights = {}, {}

            def scores(n, t):
                out = []
                for m in range(2):
                    rows, tk = slice(64 * m, 64 * m + 64), slice(t * P, (t + 1) * P)
                    pe.need(read.get((n - 1, m)))
                    out.append(self.score(m, (t + 1) * P, QH[rows, tk], QL[rows, tk], KH[rows, :], KL[rows, :]))
                return out

            def weigh(n, t, z, free):
                cols = (t + 1) * P
                w = n % 2
                ms, ls = [], []
                for m in range(2):
                    pb = pm[w + 2 * m]
                    ps = self.pair(m)
                    dve.need(z[m], free, weights.get(n - 2))
                    t0 = dve.did(dve.e.memset(ps[0:64, cols - 64:cols], -1e30))
                    dve.need(t0)
                    t1 = read[(n, m)] = dve.did(dve.e.tensor_tensor(
                        pb[:, 0:cols], ps[:, 0:cols], toep[:, (TT - 1 - t) * P:T], ALU.add))
                    dve.need(t1)
                    t2 = dve.did(dve.e.tensor_reduce(small[:, w, m:m + 1], pb[:, 0:cols], AX.X, ALU.max,
                                                     negate=True))
                    act.need(t2)
                    ls.append(act.did(act.e.activation(pb[:, 0:cols], pb[:, 0:cols], ACT.Exp,
                                                       bias=small[:, w, m:m + 1],
                                                       accum_out=small[:, w, 2 + m:3 + m])))
                dve.need(*ls)
                t3 = dve.did(dve.e.reciprocal(small[:, w, 4:6], small[:, w, 2:4]))
                dve.need(t3)
                t4 = dve.did(dve.e.tensor_tensor(small[:, w, 6:7], small[:, w, 5:6], nlam[:], ALU.mult))
                dve.need(t4)
                t5 = dve.did(dve.e.tensor_scalar(pm[w + 2][:, 0:cols], pm[w + 2][:, 0:cols], small[:, w, 6:7], None,
                                                 ALU.mult))
                dve.need(t5)
                a = weights[n] = dve.did(dve.e.scalar_tensor_tensor(
                    pm[w][:, 0:cols], pm[w][:, 0:cols], small[:, w, 4:5], pm[w + 2][:, 0:cols],
                    ALU.mult, ALU.add))
                return a

            def evac(n, t, bank, done):
                dve.need(done)
                return dve.did(dve.e.tensor_copy(res[:, h, t * P:(t + 1) * P], bank))

            self.attend(list(range(TT)), lambda t: t + 1, scores, weigh, VH, VL, evac, at_hi, at_lo, pm)
            done = [dve.count.now(), pe.count.now(), act.count.now()]
            act.need(*done)
            dve.need(*done)
            r = self.group_rstd(res[:, h, :], P, self.ones, P, pm[0], pm[1])
            dve.need(r)
            dve.did(dve.e.scalar_tensor_tensor(res[:, h, :], res[:, h, :], gout[:], pm[0][:], ALU.mult, ALU.mult))

    def mla(self, ctx, res):
        pr, PS, st = self.pr, self.PS, self.st
        act, dve, pool, pe = pr.act, pr.dve, pr.pool, pr.pe
        kv = self.sb(ctx, "mla_kv", [P, 8, T])
        V = kv[:, 4:8, :].rearrange("p a b -> p (a b)").rearrange("p (t n) -> p t n", n=512)
        with ExitStack() as c:
            LH, LL = (self.sb(c, f"mla_l{x}", [P, 3, T], F32R) for x in "hl")
            t = [kv[:, k, :] for k in range(3)]
            for first, n, name in ((12, 2, "q_lat_norm_g_2"), (14, 1, "kv_lat_norm_g_2")):
                src = [res[:, first + k, :] for k in range(n)]
                r = self.rstd(src, n * P, t[0], [t[1], t[2]])
                at = first - 12
                self.normed(src, self.g(name), t[0], r, LH[:, at:at + n, :], LL[:, at:at + n, :], [t[1], t[2]])
                pr.meet(self.free)
            self.turn = 0
            for half in range(2):
                s = st.take(st.g)
                for n in range(4):
                    p, mm = self.channels(s, LH, LL, range(2),
                                          lambda k: slice((2 * n + k) * P, (2 * n + k + 1) * P))
                    done = st.give(s, mm) if n == 3 else pe.did(mm)
                    act.need(done)
                    self.free[p].inc(act.e.activation(res[0:MLA_QK, 4 + 4 * half + n, :],
                                                      self.pair(p)[0:MLA_QK, :], ACT.Copy))
                st.split(s)
            s = st.take(st.g)
            for n in range(4):
                p, mm = self.channels(s, LH[:, 2:3, :], LL[:, 2:3, :], range(1), lambda k: slice(n * P, (n + 1) * P))
                done = pe.did(mm)
                act.need(done)
                self.free[p].inc(act.e.activation(kv[:, n, :], self.pair(p), ACT.Copy))
            for n in range(4):
                p = self.claim()
                for h in range(2):
                    tk = slice((2 * n + h) * P, (2 * n + h + 1) * P)
                    mm = self.mm3([PS[:, 2 * p + h, :]], LH[:, 2, tk], LL[:, 2, tk],
                                  [st.hi[s][:, 512:1024]], [st.lo[s][:, 512:1024]], True, True)
                done = st.give(s, mm) if n == 3 else pe.did(mm)
                act.need(done)
                self.free[p].inc(act.e.activation(V[:, 2 * n:2 * n + 2, :], PS[:, 2 * p:2 * p + 2, :], ACT.Copy))
            st.split(s)
            pr.meet(self.free)

        sb = lambda n, s, dt=F32: self.sb(ctx, n, s, dt)
        QH, QL, KH, KL = (sb(f"mla_{n}", [P, T], F32R) for n in ("qh", "ql", "kh", "kl"))
        VH, VL = (sb(f"mla_{n}", [P, TT, P], F32R) for n in ("vh", "vl"))
        pm = [res[:, 12, :], res[:, 13, :]]
        krope = res[64:96, 14, :]
        act.did(act.e.activation(krope, res[0:MLA_ROPE, 15, :], ACT.Copy))
        at_hi = [sb("mla_at_hi", [P, T], F32R)]
        at_lo = [sb("mla_at_lo", [P, T], F32R)]
        rope = [sb(f"mla_rope{x}", [P, T]) for x in ("cos", "sin")]
        rotate = sb("mla_rotate", [P, P])
        small = sb("mla_small", [P, 2, 4])
        kfull = res[:, 15, :]
        ins = [self.dma(rope[k][:], self.a["rope"][:, k, :]) for k in range(2)]
        ins.append(self.dma(rotate[:], self.a["rotate"]))
        for e in pr.compute:
            e.need(*ins)
        scale = MLA_QK ** -0.5
        R = slice(0, MLA_QK)
        rp = slice(MLA_NOPE, MLA_QK)

        with pr.loop(PAIRS) as i:
            pr.meet()
            v_ready = list(self.split_pair(i, V, VH, VL))
            for hh in range(2):
                def normed_head(src, gain, hi, lo, after):
                    for e in (act, dve, pe):
                        e.need(*after)
                    r = self.group_rstd(src[R], MLA_QK, self.ones, MLA_QK, pm[0], pm[1])
                    dve.need(r)
                    m = dve.did(dve.e.scalar_tensor_tensor(src[R], src[R], gain[R], pm[0][R], ALU.mult, ALU.mult))
                    pe.need(m)
                    for h in range(2):
                        t = pe.did(pe.e.matmul(PS[0:MLA_QK, 4 + h, :], rotate[R, 0:MLA_QK],
                                               src[R, h * HALF:(h + 1) * HALF], start=True, stop=True))
                    dve.need(t, m)
                    a = dve.did(dve.e.tensor_tensor(pm[1][rp], self.pair(2)[rp], rope[1][rp], ALU.mult))
                    b = dve.did(dve.e.tensor_tensor(src[rp], src[rp], rope[0][rp], ALU.mult))
                    dve.need(a, b)
                    a = dve.did(dve.e.tensor_tensor(src[rp], src[rp], pm[1][rp], ALU.add))
                    return list(self.split_to(hi[R], lo[R], src[R], after=(a,)))

                now = [e.count.now() for e in pr.compute]
                q = res[:, i * 2 + (4 + hh), :]
                rq = normed_head(q, self.g("mla_q_norm_g_2"), QH, QL, now)
                act.need(*now)
                k1 = act.did(act.e.activation(kfull[0:64], kv[64 * hh:64 * hh + 64, i, :], ACT.Copy))
                k2 = act.did(act.e.activation(kfull[64:96], krope, ACT.Copy))
                rk = normed_head(kfull, self.g("mla_k_norm_g_2"), KH, KL, rq + [k1, k2])
                pe.need(*rq, *rk, *v_ready)
                act.need(*rk)
                dve.need(*rk)
                read, weights = {}, {}

                def scores(n, t):
                    pe.need(read.get(n - 2))
                    tk = slice(t * P, (t + 1) * P)
                    return self.score(n % 2, (t + 1) * P, QH[R, tk], QL[R, tk], KH[R, :], KL[R, :])

                def weigh(n, t, z, free):
                    cols, w = (t + 1) * P, n % 2
                    ps = self.pair(w)
                    dve.need(z)
                    t0 = dve.did(dve.e.memset(ps[0:64, cols - 64:cols], -1e30))
                    dve.need(t0, weights.get(n - 2))
                    mx = dve.did(dve.e.tensor_reduce(small[:, w, 0:1], ps[:, 0:cols], AX.X, ALU.max, negate=True))
                    dve.need(mx)
                    mx = dve.did(dve.e.tensor_scalar(small[:, w, 1:2], small[:, w, 0:1], scale, None, ALU.mult))
                    act.need(mx, free, weights.get(n - 2))
                    e = read[n] = act.did(act.e.activation(pm[w][:, 0:cols], ps[:, 0:cols], ACT.Exp, scale=scale,
                                                           bias=small[:, w, 1:2], accum_out=small[:, w, 2:3]))
                    dve.need(e)
                    l = dve.did(dve.e.reciprocal(small[:, w, 3:4], small[:, w, 2:3]))
                    dve.need(l)
                    a = weights[n] = dve.did(dve.e.tensor_scalar(pm[w][:, 0:cols], pm[w][:, 0:cols],
                                                                 small[:, w, 3:4], None, ALU.mult))
                    return a

                def evac(n, t, bank, done):
                    rows = slice(64 * hh, 64 * hh + 64)
                    dve.need(done)
                    return dve.did(dve.e.tensor_copy(res[rows, i + 4, t * P:(t + 1) * P], bank[rows, :]))

                self.attend(list(range(TT)), lambda t: t + 1, scores, weigh, VH, VL, evac, at_hi, at_lo, pm)

    def store(self):
        pr = self.pr
        for k in range(KT):
            t = self.dma(self.out_ap[k], self.H[:, k, :])
            pr.sp.need(t) if k == KT - 1 else self.pending.append(t)
        pr.sp.need(*self.pending)


BIAS_LEN = T + P - 1


def build_program(nc, rates, a, gains, out):
    k = Kernel.__new__(Kernel)
    k.at, k.pending = gains, []
    k.__init__(nc, rates, a, out)


GAINS = {}


def _lay(inp):
    def tiles(v):
        return np.ascontiguousarray(np.asarray(v).reshape(-1, P).T)

    def chan(w, c0, width=P):
        k = w.shape[0] // P
        u = np.zeros((P, k, P), w.dtype)
        u[:, :, :width] = w[:, c0:c0 + width].reshape(k, P, width).transpose(1, 0, 2)
        return [u.reshape(P, k * P)]

    def chans(w, cols):
        return [u for c in cols for u in chan(w, c)]

    def tokens(w):
        u = w.reshape(4, 2, P, 512).transpose(0, 2, 1, 3).reshape(4, P, 1024)
        return list(u)

    def rows(w, k):
        return [w[k * P:(k + 1) * P]]

    def small(w):
        u = w.reshape(2, P, 2, 4, P).transpose(2, 1, 3, 0, 4).reshape(2, P, 1024)
        return list(u)

    def ffn(gate, up, down):
        n, u = FF_TILES // 2, []
        for g in range(n):
            if g:
                u += chan(gate, 2 * g * P)
                u += rows(down, 2 * g - 2) + rows(down, 2 * g - 1)
            else:
                u += chan(gate, 0)
            u += chan(up, 2 * g * P) + chan(gate, (2 * g + 1) * P) + chan(up, (2 * g + 1) * P)
        return u + rows(down, 2 * n - 2) + rows(down, 2 * n - 1)

    w1 = np.asarray(inp["w_in"])[0]
    w2 = np.asarray(inp["w_in_2"])[0]
    gu = np.asarray(inp["w_gate_up"])[0]
    span = lambda c, n: [c + P * j for j in range(n)]
    units = chans(w1, span(0, 4) + span(512, 4) + span(1536, 4))
    units += tokens(w1[:, 1024:1536])
    units += chans(w1, span(2048, 8))
    units += tokens(w1[:, 3072:3584])
    units += chans(np.asarray(inp["w_out"])[0], span(0, 8))
    units += ffn(gu[:, :2816], gu[:, 2816:], np.asarray(inp["w_down"])[0])
    units += small(np.asarray(inp["ple_proj"])[0])
    units += chans(np.asarray(inp["ple_gate"])[0], span(0, 8))
    units += chans(w2, [0, 128, 256]) + chan(w2, 384, MLA_ROPE)
    units += chans(w2, span(416, 8)) + tokens(w2[:, 1440:1952])
    uq = np.asarray(inp["w_uq_2"])[0].reshape(2, P, MLA_H, MLA_QK)
    for g in range(2):
        u = np.zeros((P, 4, 2, P), w1.dtype)
        u[:, :, :, :MLA_QK] = uq[:, :, 4 * g:4 * g + 4].transpose(1, 2, 0, 3)
        units.append(u.reshape(P, 1024))
    ukv = np.asarray(inp["w_ukv_2"])[0].reshape(P, MLA_H, 2, 64)
    units.append(ukv.transpose(0, 2, 1, 3).reshape(P, 1024))
    wo = np.asarray(inp["w_out_2"])[0]
    wo = np.concatenate([wo[512:], wo[:512]])
    units += chans(wo, span(0, 8))
    units += ffn(np.asarray(inp["w_gate_2"])[0], np.asarray(inp["w_up_2"])[0], np.asarray(inp["w_down_2"])[0])
    units += small(np.asarray(inp["w_ple_proj_2"])[0])
    units += chans(np.asarray(inp["w_ple_gate_2"])[0], span(0, 8))
    units += [np.zeros((P, UNIT), w1.dtype)] * RING
    arrays = {"weights": np.stack(units)}

    def flat(w):
        return np.asarray(w)[0].T.reshape(-1, P, T)

    arrays["x_t"] = np.ascontiguousarray(np.asarray(inp["x"])[0].T).reshape(KT, P, T)
    arrays["p_t"] = np.ascontiguousarray(np.asarray(inp["p"])[0, 0].T).reshape(2, P, T)
    arrays["p2_t"] = np.ascontiguousarray(np.asarray(inp["p_2"])[0, 0].T).reshape(2, P, T)

    cols, at = [], 0
    GAINS.clear()

    def put(name, m):
        nonlocal at
        z = np.zeros((P, m.shape[1]), np.float32)
        z[:m.shape[0]] = m
        cols.append(z)
        GAINS[name] = (at, m.shape[1])
        at += m.shape[1]

    for name in ("attn_pre_norm", "hg_out_norm", "sb_out_norm", "attn_post_norm", "ffn_pre_norm",
                 "ffn_post_norm", "attn_norm_g_2", "q_lat_norm_g_2", "kv_lat_norm_g_2",
                 "diff_out_norm_g_2", "ffn_norm_g_2", "ple_norm_g_2"):
        put(name, tiles(np.asarray(inp[name])[0]))
    for name in ("mla_q_norm_g_2", "mla_k_norm_g_2", "lambda_q1_2", "lambda_k1_2", "lambda_q2_2", "lambda_k2_2"):
        put(name, np.asarray(inp[name])[0][:, None])
    for name in ("diff_q_norm_g_2", "diff_k_norm_g_2"):
        g = np.asarray(inp[name])[0]
        put(name, np.concatenate([g, g])[:, None])
    g = np.asarray(inp["hg_lower_gamma"])
    put("gamma0", tiles(g[0]))
    put("gamma1", tiles(g[1]))
    cw = np.asarray(inp["conv_w_2"])[0]
    for j in range(3):
        put(f"conv_w{j}", tiles(cw[j]))
    put("conv_b", tiles(np.asarray(inp["conv_b_2"])[0]))
    arrays["gains"] = np.concatenate(cols, axis=1)
    arrays["rel_bias"] = np.ascontiguousarray(np.asarray(inp["rel_bias_2"]))
    arrays.update(_constants())
    return arrays


def _constants():
    c = {"ident": np.eye(P, dtype=np.float32)}
    s, t = np.arange(P)[:, None], np.arange(P)[None, :]
    masks = [(s // (2 * h) == t // (2 * h)) & (s % (2 * h) < h) & (t % (2 * h) >= h) for h in LEVELS]
    masks.append(s == t)
    c["levels"] = np.stack(masks, axis=1).astype(np.float32)
    c["strict"] = (t < s).astype(np.float32)
    half = MLA_ROPE // 2
    ang = (np.arange(T, dtype=np.float32)[:, None]
           * (np.float32(10000.0) ** (-np.arange(half, dtype=np.float32) / half)).astype(np.float32)[None, :])
    cos, sin = np.ones((P, T), np.float32), np.zeros((P, T), np.float32)
    for b in range(2):
        cos[MLA_NOPE + b * half:MLA_NOPE + (b + 1) * half] = np.cos(ang).T
        sin[MLA_NOPE + b * half:MLA_NOPE + (b + 1) * half] = np.sin(ang).T
    c["rope"] = np.stack([cos, sin], axis=1)
    rot = np.zeros((P, P), np.float32)
    for j in range(half):
        rot[MLA_NOPE + half + j, MLA_NOPE + j] = -1.0
        rot[MLA_NOPE + j, MLA_NOPE + half + j] = 1.0
    c["rotate"] = rot
    rel = np.arange(BIAS_LEN) - (T - 1)
    n = np.abs(rel)
    large = 8 + (np.log(np.maximum(n, 1).astype(np.float32) / 8) / math.log(1024 / 8) * 8).astype(np.int32)
    bucket = np.where(rel > 0, 16, 0) + np.where(n < 8, n, np.minimum(large, 15))
    c["bucket"] = (np.arange(NBUCKET)[:, None] == bucket[None, :]).astype(np.float32)
    return c


def kernel(**inputs):
    import concourse.bacc as _bacc
    from concourse.bass_utils import run_bass_kernel_spmd as _run

    arrays = _lay(inputs)
    gains = dict(GAINS)
    rates = {}
    for _ in range(2):
        nc = _bacc.Bacc("TRN2", target_bir_lowering=False, num_devices=1)
        aps = {n: nc.dram_tensor("in_" + n, v.shape, mybir.dt.from_np(v.dtype), kind="ExternalInput").ap()
               for n, v in arrays.items()}
        out = nc.dram_tensor("out_t", (KT, P, T), F32, kind="ExternalOutput").ap()
        build_program(nc, rates, aps, gains, out)
    r = _run(nc, [{"in_" + n: v for n, v in arrays.items()}], core_ids=[0])
    return np.ascontiguousarray(r.results[0]["out_t"].reshape(D, T).T).reshape(1, T, D)
```

```python
import math
from contextlib import ExitStack, contextmanager

import numpy as np

import concourse.bass as bass
from concourse import mybir

F32 = mybir.dt.float32
F32R = mybir.dt.float32r
U8 = mybir.dt.uint8
ACT = mybir.ActivationFunctionType
ALU = mybir.AluOpType
AX = mybir.AxisListType

P = 128
T = 1024
D = 1024
KT = D // P
TT = T // P
HALF = 512
EPS = 1e-6

HG = 512
HGH = HG // P
SB_DH = 64
PAIRS = 512 // (2 * SB_DH)
FF_TILES = 2816 // P
MLA_H, MLA_NOPE, MLA_ROPE = 8, 64, 32
MLA_QK = MLA_NOPE + MLA_ROPE
DIFF_H = 4
NBUCKET = 32
LAM_INIT = 0.8 - 0.6 * math.exp(-0.3 * 0)
RING = 3
UNIT = 1024
LEVELS = [64, 32, 16, 8, 4, 2, 1]


class Count:

    def __init__(self, prog, name, by=1):
        self.sem = prog.ctx.enter_context(prog.nc.semaphore(name))
        self.name, self.by, self.const, self.rate, self.reg = name, by, 0, 0, None
        prog.counts[name] = self

    def inc(self, ins):
        ins.then_inc(self.sem, self.by)
        self.const += self.by
        return self.now()

    def now(self):
        return (self, self.const, self.rate, self.reg)


class Engine:

    def __init__(self, prog, e, name):
        self.e, self.name = e, name
        self.count = Count(prog, "done_" + name)
        self.seen = {}

    def need(self, *tickets):
        waited = False
        for t in tickets:
            if t is None:
                continue
            if isinstance(t, (list)):
                self.need(*t)
                continue
            c, const, rate, reg = t
            if rate == 0:
                if const <= 0 or self.seen.get(c.name, 0) >= const:
                    continue
                self.seen[c.name] = const
                self.e.wait_ge(c.sem, const)
            else:
                assert const >= 1, (c.name, const)
                if self.seen.get((c.name, rate), 0) >= const:
                    continue
                self.seen[(c.name, rate)] = const
                self.e.wait_ge(c.sem, reg * rate + const)
                waited = True
                if self.name == "sp":
                    self.e.nop(nofuse=True)
        if waited and self.name in ("act", "dve"):
            self.e.nop(nofuse=True)

    def did(self, ins):
        return self.count.inc(ins)


class Prog:
    def __init__(self, nc, ctx, rates):
        self.nc, self.ctx, self.counts, self.rates = nc, ctx, {}, rates
        self.loops = 0
        self.pe = Engine(self, nc.tensor, "pe")
        self.act = Engine(self, nc.scalar, "act")
        self.dve = Engine(self, nc.vector, "dve")
        self.pool = Engine(self, nc.gpsimd, "pool")
        self.sp = Engine(self, nc.sync, "sp")
        self.engines = [self.pe, self.act, self.dve, self.pool, self.sp]
        self.compute = [self.pe, self.act, self.dve, self.pool]

    def meet(self, extra=()):
        t = [e.count.now() for e in self.compute] + [c.now() for c in extra]
        for e in self.engines:
            e.need(*t)

    @contextmanager
    def loop(self, n):
        key = self.loops
        self.loops += 1
        rate = self.rates.get(key, {})
        start = {k: c.const for k, c in self.counts.items()}
        with self.nc.Fori(0, n, 1) as i:
            for e in self.engines:
                e.seen = {}
            for k, c in self.counts.items():
                c.rate, c.reg = rate.get(k, 0), i
                if c.rate and c.const == 0:
                    pass
            yield i
        for e in self.engines:
            e.seen = {}
        got = {k: c.const - start.get(k, 0) for k, c in self.counts.items()}
        if key in self.rates:
            assert {k: v for k, v in got.items() if v} == {k: v for k, v in rate.items() if v}
        self.rates[key] = got
        for k, c in self.counts.items():
            c.const = start.get(k, 0) + n * got[k]
            c.rate, c.reg = 0, None


class Stream:

    def __init__(self, pr, dram, sb):
        self.pr, self.dram = pr, dram
        self.raw = [sb(f"w_raw{s}", [P, UNIT], F32) for s in range(RING)]
        self.hi = [sb(f"w_hi{s}", [P, UNIT], F32R) for s in range(RING)]
        self.lo = [sb(f"w_lo{s}", [P, UNIT], F32R) for s in range(RING)]
        self.loaded = [Count(pr, f"w_loaded{s}", 16) for s in range(RING)]
        self.hi_done = [Count(pr, f"w_hi_done{s}") for s in range(RING)]
        self.lo_done = [Count(pr, f"w_lo_done{s}") for s in range(RING)]
        self.used = [Count(pr, f"w_used{s}") for s in range(RING)]
        self.g = 0
        self.total = dram.shape[0]

    def load(self, s, index):
        pr = self.pr
        pr.sp.need(self.hi_done[s].now(), self.lo_done[s].now())
        self.loaded[s].inc(pr.sp.e.dma_start(self.raw[s][:], self.dram[index]))

    def split(self, s):
        pr = self.pr
        pr.act.need(self.loaded[s].now(), self.used[s].now())
        hi = self.hi_done[s].inc(pr.act.e.activation(self.hi[s][:], self.raw[s][:], ACT.Copy))
        pr.dve.need(self.loaded[s].now(), self.used[s].now(), hi)
        self.lo_done[s].inc(pr.dve.e.tensor_tensor(
            self.lo[s][:], self.raw[s][:], self.hi[s][:].bitcast(F32), ALU.subtract))

    def start(self):
        for s in range(RING):
            self.load(s, s)
            self.split(s)

    def take(self, index):
        s = self.g % RING
        self.g += 1
        self.load(s, index + RING)
        self.pr.pe.need(self.hi_done[s].now(), self.lo_done[s].now())
        return s

    def give(self, s, last):
        return self.used[s].inc(last)


class Kernel:
    def __init__(self, nc, rates, a, out):
        self.nc, self.a, self.out_ap = nc, a, out
        with ExitStack() as ctx:
            self.pr = Prog(nc, ctx, rates)
            self.build(ctx)

    def sb(self, ctx, name, shape, dt=F32):
        return ctx.enter_context(self.nc.sbuf_tensor(name, shape, dt))

    def dma(self, dst, src):
        self.n_dma += 1
        c = Count(self.pr, f"dma_{self.n_dma}", 16)
        return c.inc(self.pr.sp.e.dma_start(dst, src))

    def mm3(self, banks, lh, ll, rh, rl, first, last):
        e, n = self.pr.pe.e, len(banks)
        for i in range(n):
            ins = e.matmul(banks[i], lh, rh[i], start=first, stop=False)
        for i in range(n):
            ins = e.matmul(banks[i], lh, rl[i], start=False, stop=False)
        for i in range(n):
            ins = e.matmul(banks[i], ll, rh[i], start=False, stop=last)
        return ins

    def split_to(self, hi, lo, src, after=(), src_ps=None):
        pr = self.pr
        pr.act.need(*after)
        h = pr.act.did(pr.act.e.activation(hi, src, ACT.Copy))
        pr.dve.need(*after, h)
        return h, pr.dve.did(pr.dve.e.tensor_tensor(lo, src, hi.bitcast(F32), ALU.subtract))

    def token_sums(self, k, n, sq):
        e = self.pr.pe.e
        for t in range(TT):
            ins = e.matmul(self.PS[:, 7, t:t + 1], sq[:, t * P:(t + 1) * P], self.ones[:, 0:1],
                           start=k == 0 and t == 0, stop=k == n - 1 and t == TT - 1, skip_group_check=True)
        return self.pr.pe.did(ins)

    def token_rstd(self, r, sums, dim, after):
        pr = self.pr
        pr.act.need(*after)
        t = pr.act.did(pr.act.e.activation(r, sums, ACT.Sqrt, scale=1.0 / dim, bias=self.eps[:, 0:1]))
        pr.dve.need(t)
        return pr.dve.did(pr.dve.e.reciprocal(r, r))

    def spread_rows(self, r, r_done, diag, out):
        pr = self.pr
        pe, dve, act = pr.pe, pr.dve, pr.act
        pe.need(self.free[2].now())
        used = [None, None]
        for t in range(TT):
            d = diag[t % 2]
            dve.need(r_done, used[t % 2])
            g = dve.did(dve.e.tensor_scalar(d, self.ident[:], r[:, t:t + 1], None, ALU.mult))
            pe.need(g)
            used[t % 2] = pe.did(pe.e.matmul(self.pair(2)[:, t * P:(t + 1) * P], self.ones[:], d,
                                             start=True, stop=True))
        act.need(used[0], used[1])
        return self.free[2].inc(act.e.activation(out, self.pair(2), ACT.Copy))

    def prepare(self, src, gain, UH, UL, sq=None, after=()):
        pr = self.pr
        act, dve, pe = pr.act, pr.dve, pr.pe
        n = len(src)
        used = [None, None]
        s = None
        if sq:
            pe.need(self.free[3].now())
        for k in range(n):
            for e in (act, dve):
                e.need(after[k] if after else None)
            if sq:
                q = sq[k % 2]
                if k % 2:
                    dve.need(used[1])
                    m = dve.did(dve.e.tensor_tensor(q, src[k], src[k], ALU.mult))
                else:
                    act.need(used[0])
                    m = act.did(act.e.activation(q, src[k], ACT.Square))
                pe.need(m)
                s = used[k % 2] = self.token_sums(k, n, q)
            g = 1.0 if gain is None else gain[:, k:k + 1]
            h = act.did(act.e.activation(UH[:, k, :], src[k], ACT.Copy, scale=g))
            dve.need(h)
            if gain is None:
                dve.did(dve.e.tensor_tensor(UL[:, k, :], src[k], UH[:, k, :].bitcast(F32), ALU.subtract))
            else:
                dve.did(dve.e.scalar_tensor_tensor(UL[:, k, :], src[k], g, UH[:, k, :].bitcast(F32),
                                                   ALU.mult, ALU.subtract))
        return s

    def statistics(self, s, dim, out=None):
        r = self.token_rstd(self.rt[:], self.PS[:, 7, 0:TT], dim, (s,))
        if out is not None:
            self.spread_rows(self.rt, r, [self.diag[:, 0:P], self.diag[:, P:2 * P]], out)
        return r

    def pair(self, p):
        return self.PS[:, 2 * p:2 * p + 2, :].rearrange("p a b -> p (a b)")

    def claim(self):
        p = self.turn % 4
        self.turn += 1
        self.pr.pe.need(self.free[p].now())
        return p

    def product(self, index, UH, UL, kt=KT, width=P):
        pr, st = self.pr, self.st
        s = st.take(index)
        p, last = self.channels(s, UH, UL, range(kt), lambda k: slice(k * P, k * P + width), width)
        return p, st.give(s, last), s

    def channels(self, s, UH, UL, ks, cols, width=P):
        p = self.claim()
        ks = list(ks)
        for n, k in enumerate(ks):
            last = self.mm3([self.PS[0:width, 2 * p + h, :] for h in range(2)],
                            self.st.hi[s][:, cols(k)], self.st.lo[s][:, cols(k)],
                            [UH[:, k, h * HALF:(h + 1) * HALF] for h in range(2)],
                            [UL[:, k, h * HALF:(h + 1) * HALF] for h in range(2)],
                            n == 0, n == len(ks) - 1)
        return p, last

    def project(self, n, UH, UL, dst, rows):
        pr, st = self.pr, self.st
        g0 = st.g

        def step(j, index):
            p, done, s = self.product(index, UH, UL)
            if rows is None:
                pr.act.need(done)
                self.free[p].inc(pr.act.e.activation(dst(j), self.pair(p), ACT.Copy))
            else:
                pr.dve.need(done)
                self.free[p].inc(pr.dve.e.tensor_tensor(dst(j), self.pair(p), rows, ALU.mult))
            st.split(s)

        rounds = n // RING
        if rounds > 1:
            with pr.loop(rounds) as i:
                self.turn = 0
                for j in range(RING):
                    step(i * RING + j, i * RING + (g0 + j))
            st.g = g0 + rounds * RING
        else:
            rounds = 0
        self.turn = 0
        for j in range(rounds * RING, n):
            step(j, g0 + j)

    def project_tokens(self, UH, UL, dst):
        pr, st = self.pr, self.st
        pr.pe.need(*[f.now() for f in self.free])
        for m in range(KT // 2):
            s = st.take(st.g)
            for t in range(TT):
                for j in range(2):
                    k = 2 * m + j
                    tok = slice(t * P, (t + 1) * P)
                    wh, wl = (w[s][:, j * 512:(j + 1) * 512] for w in (st.hi, st.lo))
                    first, last = k == 0, k == KT - 1
                    pr.pe.e.matmul(self.PS[:, t, :], UH[:, k, tok], wh, start=first, stop=False)
                    pr.pe.e.matmul(self.PS[:, t, :], UH[:, k, tok], wl, start=False, stop=False)
                    ins = pr.pe.e.matmul(self.PS[:, t, :], UL[:, k, tok], wh, start=False, stop=last)
            done = st.give(s, ins)
            st.split(s)
        pr.act.need(done)
        pr.dve.need(done)
        for t in range(TT):
            to = dst[:, :, t * P:(t + 1) * P]
            ps = self.PS[:, t, :].rearrange("p (k c) -> p k c", c=P)
            if t % 2:
                self.free[t // 2].inc(pr.dve.e.tensor_scalar(to, ps, self.rt[:, t:t + 1], None, ALU.mult))
            else:
                self.free[t // 2].inc(pr.act.e.activation(to, ps, ACT.Copy, scale=self.rt[:, t:t + 1]))

    def build(self, ctx):
        nc, pr, a = self.nc, self.pr, self.a
        self.n_dma = 0
        self.turn = 0
        sb = lambda n, s, dt=F32: self.sb(ctx, n, s, dt)
        self.PS = ctx.enter_context(nc.psum_tensor("PS", [P, 8, HALF], F32))
        self.free = [Count(pr, f"psum_free{p}") for p in range(4)]
        self.st = Stream(pr, a["weights"], sb)
        self.H = sb("H", [P, KT, T])
        self.ones = sb("ones", [P, P])
        self.eps = sb("eps", [P, 1])
        self.rt = sb("r_tokens", [P, TT])
        self.rt2 = sb("r_tokens2", [P, TT])
        self.sums = sb("token_sums", [P, TT])
        self.gout8 = sb("mixer2_out_gains", [P, KT])
        self.diag = sb("diag", [P, 2 * P])
        self.ident = sb("ident", [P, P])
        self.gains = sb("gains", [P, a["gains"].shape[1]])
        for p in range(4):
            self.free[p].inc(nc.vector.memset(self.pair(p), 0.0))
        first = self.sb(ctx, "first_marks", [P, 2])
        ready = [pr.dve.did(nc.vector.memset(self.ones[:], 1.0)),
                 pr.pool.did(nc.gpsimd.memset(first[:, 0:1], 0.0)),
                 pr.dve.did(nc.vector.memset(self.eps[:], EPS))]
        ready.append(self.dma(self.ident[:], a["ident"]))
        ready.append(self.dma(self.gains[:], a["gains"]))
        self.x_in = [self.dma(self.H[:, k, :], a["x_t"][k]) for k in range(KT)]
        self.st.start()
        for e in pr.engines:
            e.need(*ready)
        self.program(ctx)

    def g(self, name):
        at, n = self.at[name]
        return self.gains[:, at:at + n]

    def program(self, ctx):
        with ExitStack() as c:
            self.first_mixer(c)
        self.first_output()
        self.feed_forward(conv=False)
        self.ple(self.a["p_t"], norm=None)
        self.second_mixer()
        self.feed_forward(conv=True)
        self.ple(self.a["p2_t"], norm="ple_norm_g_2")
        self.store()

    def operand(self, ctx, tag):
        return [self.sb(ctx, f"u_{x}_{tag}", [P, KT, T], F32R) for x in ("hi", "lo")]

    def normed_input(self, gain, UH, UL, scratch, rows, after=None):
        pr = self.pr
        x = [self.H[:, k, :] for k in range(KT)]
        s = self.prepare(x, self.g(gain), UH, UL, sq=scratch, after=after)
        self.statistics(s, D, rows)
        pr.meet(self.free)

    def first_mixer(self, ctx):
        pr, H = self.pr, self.H
        big = self.sb(ctx, "mixer1", [P, 12, T])
        rows = self.sb(ctx, "mixer1_rows", [P, T])
        with ExitStack() as c:
            UH, UL = self.operand(c, "1")
            self.normed_input("attn_pre_norm", UH, UL, [big[:, 0, :], big[:, 1, :]], rows[:], after=self.x_in)
            self.project(8, UH, UL, lambda j: H[:, j, :], rows[:])
            self.project_tokens(UH, UL, big[:, 0:4, :])
            self.project_tokens(UH, UL, big[:, 4:8, :])
            pr.meet(self.free)
            with ExitStack() as h:
                self.hgrn(h, big)
            pr.meet(self.free)
            self.project(8, UH, UL, lambda j: big[:, j, :], rows[:])
            self.project_tokens(UH, UL, big[:, 8:12, :])
            pr.meet(self.free)
        with ExitStack() as c:
            self.stick_breaking(c, big)
        pr.meet(self.free)

    def hgrn(self, ctx, big):
        pr, H, PS = self.pr, self.H, self.PS
        act, dve, pool, pe = pr.act, pr.dve, pr.pool, pr.pe
        e_t = [big[:, 8, :], big[:, 9, :]]
        x_t = [big[:, 10, :], big[:, 11, :]]
        kk = self.sb(ctx, "hg_k", [P, T])
        b = self.sb(ctx, "hg_b", [P, T])
        scores = self.sb(ctx, "hg_scores", [P, TT, P])
        last_decay = self.sb(ctx, "hg_last", [P, TT, 1])
        lb = self.sb(ctx, "hg_lb", [P, HGH, 1])
        olb = self.sb(ctx, "hg_olb", [P, HGH, 1])
        tmp = self.sb(ctx, "hg_tmp", [P, HGH])
        masks = self.sb(ctx, "hg_masks", [P, len(LEVELS) + 1, P], U8)
        m_in = self.dma(kk[:].rearrange("p (a b) -> p a b", b=P), self.a["levels"])
        g0, g1 = self.g("gamma0"), self.g("gamma1")
        lb2, olb2 = lb[:].rearrange("p a b -> p (a b)"), olb[:].rearrange("p a b -> p (a b)")
        t = dve.did(dve.e.tensor_tensor(tmp[:], g0, g1, ALU.max))
        dve.need(t)
        dve.did(dve.e.tensor_tensor(lb2, g0, tmp[:], ALU.subtract))
        t = dve.did(dve.e.tensor_tensor(olb2, g1, tmp[:], ALU.subtract))
        act.need(t)
        act.did(act.e.activation(lb2, lb2, ACT.Exp))
        t = act.did(act.e.activation(olb2, olb2, ACT.Exp))
        dve.need(t)
        t = dve.did(dve.e.tensor_tensor(tmp[:], lb2, olb2, ALU.add))
        dve.need(t)
        t = dve.did(dve.e.reciprocal(tmp[:], tmp[:]))
        dve.need(t)
        dve.did(dve.e.tensor_tensor(lb2, lb2, tmp[:], ALU.mult))
        dve.did(dve.e.tensor_tensor(olb2, olb2, tmp[:], ALU.mult))
        dve.did(dve.e.memset(scores[:], 0.0))
        dve.need(m_in)
        dve.did(dve.e.tensor_copy(masks[:], kk[:].rearrange("p (a b) -> p a b", b=P)))
        chunks = [slice(c * P, (c + 1) * P) for c in range(TT)]

        with pr.loop(HGH) as j:
            pr.meet()
            q, z, v = H[:, j, :], H[:, j + 4, :], lambda c: big[:, j + 4, chunks[c]]
            s1 = act.did(act.e.activation(e_t[0], z, ACT.Sigmoid))
            s2 = act.did(act.e.activation(e_t[1], z, ACT.Sigmoid, scale=-1.0))
            s = act.did(act.e.activation(x_t[0], q, ACT.Sigmoid))
            dve.need(s1, s2)
            f = dve.did(dve.e.tensor_scalar(z, e_t[0], olb[:, j, :], lb[:, j, :], ALU.mult, ALU.add))
            dve.need(f)
            f = dve.did(dve.e.tensor_scalar(z, z, 1e-19, None, ALU.max))
            k_done = dve.did(dve.e.tensor_scalar(kk[:], e_t[1], olb[:, j, :], None, ALU.mult))
            act.need(f)
            lf = act.did(act.e.activation(z, z, ACT.Ln))
            dve.need(s)
            q_done = dve.did(dve.e.tensor_tensor(q, q, x_t[0], ALU.mult))
            dve.need(lf)
            for ch in chunks:
                b_done = dve.did(dve.e.tensor_tensor_scan(
                    b[:, ch], H[:, j + 4, ch], H[:, j + 4, ch], 0.0, ALU.add, ALU.bypass))
            dve.need(b_done, q_done, k_done)
            pool.need(b_done, q_done, k_done)
            pe.need(k_done, q_done)

            def keep(level, ps_pair, prods, kept):
                dve.need(prods, kept)
                ps = self.pair(ps_pair).rearrange("p (a b) -> p a b", b=P)
                m = masks[:, level:level + 1, :].to_broadcast([P, TT, P])
                return dve.did(dve.e.copy_predicated(scores[:], m, ps))

            scaled = [None, None]
            read = [None, None]
            got = [None, None]
            exps = {}

            def exponents(n):
                h, w = LEVELS[n], n % 2
                blocks = lambda ap: ap.rearrange("p (n c) -> p n c", c=2 * h)
                bb, ee = blocks(b[:]), blocks(e_t[w])
                dve.need(scaled[w])
                e = dve.did(dve.e.tensor_tensor(
                    ee, bb, bb[:, :, h - 1:h].to_broadcast([P, T // (2 * h), 2 * h]), ALU.subtract))
                act.need(e)
                lo = act.did(act.e.activation(ee[:, :, :h], ee[:, :, :h], ACT.Exp, scale=-1.0))
                up = act.did(act.e.activation(ee[:, :, h:], ee[:, :, h:], ACT.Exp))
                exps[n] = lo, up

            exponents(0)
            kept = prods = None
            for n, h in enumerate(LEVELS):
                w = n % 2
                if n + 1 < len(LEVELS):
                    exponents(n + 1)
                blocks = lambda ap: ap.rearrange("p (n c) -> p n c", c=2 * h)
                ee, xx, qq, k3 = blocks(e_t[w]), blocks(x_t[w]), blocks(q), blocks(kk[:])
                lo, up = exps[n]
                pool.need(lo, read[w])
                xl = pool.did(pool.e.tensor_tensor(xx[:, :, :h], k3[:, :, :h], ee[:, :, :h], ALU.mult))
                dve.need(up, read[w])
                xu = dve.did(dve.e.tensor_tensor(xx[:, :, h:], qq[:, :, h:], ee[:, :, h:], ALU.mult))
                scaled[w] = [xl, xu]
                if n:
                    kept = got[1 - w] = keep(n - 1, 1 - w, prods, kept)
                pe.need(xl, xu, got[w])
                for ch in chunks:
                    mm = pe.e.matmul(self.pair(w)[:, ch], x_t[w][:, ch], x_t[w][:, ch], start=True, stop=True)
                prods = read[w] = pe.did(mm)
            pe.need(got[1 - w])
            for ch in chunks:
                mm = pe.e.matmul(self.pair(1 - w)[:, ch], kk[:, ch], H[:, j, ch], start=True, stop=True)
            diagonal = pe.did(mm)
            b3, e3 = (t.rearrange("p (n c) -> p n c", c=P) for t in (b[:], e_t[1]))
            dve.need(scaled[1])
            e = dve.did(dve.e.tensor_tensor(e3, b3, b3[:, :, P - 1:P].to_broadcast([P, TT, P]), ALU.subtract))
            kept = got[w] = keep(len(LEVELS) - 1, w, prods, kept)
            act.need(e)
            ke = act.did(act.e.activation(e_t[1], e_t[1], ACT.Exp, scale=-1.0))
            act.need(scaled[0])
            qe = act.did(act.e.activation(e_t[0], b[:], ACT.Exp))
            gl = act.did(act.e.activation(last_decay[:], b3[:, :, P - 1:P], ACT.Exp))
            dve.need(ke, read[1])
            ke = dve.did(dve.e.tensor_tensor(x_t[1], kk[:], e_t[1], ALU.mult))
            pool.need(qe, read[0])
            qe = pool.did(pool.e.tensor_tensor(x_t[0], q, e_t[0], ALU.mult))
            kept = keep(len(LEVELS), 1 - w, diagonal, kept)
            pe.need(ke, kept)
            for ch in chunks:
                mm = pe.e.transpose(self.pair(0)[:, ch], x_t[1][:, ch], self.ident[:])
            mm = pe.did(mm)
            act.need(mm, gl, qe)
            kt = act.did(act.e.activation(b[:], self.pair(0), ACT.Copy))
            for c, ch in enumerate(chunks):
                pe.e.matmul(self.pair(2)[:, ch], scores[:, c, :], v(c),
                            start=c % 4 == 0, stop=False, skip_group_check=True)
            pe.need(kt)
            for c, ch in enumerate(chunks[:-1]):
                mm = pe.e.matmul(self.pair(3)[:, ch], b[:, ch], v(c), start=True, stop=True)
            upd = pe.did(mm)
            dve.need(upd, diagonal, ke, gl, scaled[0])
            st = dve.did(dve.e.tensor_copy(kk[:, chunks[0]], self.pair(3)[:, chunks[0]]))
            pe.need(qe)
            for c in range(1, TT):
                if c > 1:
                    dve.need(st)
                    st = dve.did(dve.e.scalar_tensor_tensor(
                        kk[:, chunks[c - 1]], kk[:, chunks[c - 2]], last_decay[:, c - 1, :],
                        self.pair(3)[:, chunks[c - 1]], ALU.mult, ALU.add))
                pe.need(st)
                mm = pe.e.matmul(self.pair(2)[:, chunks[c]], x_t[0][:, chunks[c]], kk[:, chunks[c - 1]],
                                 start=False, stop=c == TT - 1, skip_group_check=True)
            o = pe.did(mm)
            act.need(o, diagonal, qe)
            act.did(act.e.activation(H[:, j, :], self.pair(2), ACT.Copy))
        pr.meet()
        for t, tk in enumerate(chunks):
            tile = e_t[t % 2][:, 0:HALF].rearrange("p (k c) -> p k c", c=P)
            act.need(act.count.now())
            s = act.did(act.e.activation(tile, H[:, 0:4, tk], ACT.Square, accum_out=self.sums[:, t:t + 1]))
        s = self.token_rstd(self.rt2[:], self.sums[:], HG, (s,))
        used = [None, None]
        for k in range(HGH):
            act.need(used[k % 2])
            gate = act.did(act.e.activation(x_t[k % 2], big[:, k, :], ACT.Silu))
            dve.need(gate, s)
            for t, tk in enumerate(chunks):
                m = dve.did(dve.e.scalar_tensor_tensor(H[:, k, tk], H[:, k, tk], self.rt2[:, t:t + 1],
                                                       x_t[k % 2][:, tk], ALU.mult, ALU.mult))
            used[k % 2] = m

    def attend(self, items, blocks, scores, before, after, v, evac, a_buf, at_buf, wide=P, copier=None):
        pr, PS = self.pr, self.PS
        act, dve, pe = pr.act, pr.dve, pr.pe
        N, na, nt = len(items), len(a_buf), len(at_buf)
        mid, ready, turned, copied, av, out = {}, {}, {}, {}, {}, {}
        for step in range(N + 3):
            n = step
            if n < N:
                z = scores(n, items[n])
            n = step - 2
            if 0 <= n < N:
                pe.need(ready[n], copied.get(n - 1))
                for b in range(blocks(items[n])):
                    cols = slice(b * P, (b + 1) * P)
                    mm = pe.e.transpose(self.pair(2)[:, cols], a_buf[n % na][:, cols], self.ident[:])
                turned[n] = pe.did(mm)
            n = step - 3
            if 0 <= n < N:
                bank = PS[:, 6 + n % 2, 0:wide]
                nb = blocks(items[n])
                pe.need(copied[n], out.get(n - 2))
                for b in range(nb):
                    mm = pe.e.matmul(bank, at_buf[n % nt][:, b * P:(b + 1) * P], v(items[n], b),
                                     start=b == 0, stop=b == nb - 1)
                av[n] = pe.did(mm)
            n = step - 1
            if 0 <= n < N:
                ready[n] = after(n, items[n], mid[n])
            n = step - 2
            if 0 <= n < N:
                cols = slice(0, blocks(items[n]) * P)
                e = copier(n) if copier else act
                e.need(turned[n], av.get(n - nt))
                if e is act:
                    i = e.e.activation(at_buf[n % nt][:, cols], self.pair(2)[:, cols], ACT.Copy)
                else:
                    i = e.e.tensor_copy(at_buf[n % nt][:, cols], self.pair(2)[:, cols])
                copied[n] = e.did(i)
            n = step
            if n < N:
                mid[n] = before(n, items[n], z, turned.get(n - na))
            n = step - 3
            if 0 <= n < N:
                out[n] = evac(n, items[n], bank, av[n])

    def banks_of(self, pair, cols):
        return [(self.PS[:, 2 * pair + h, 0:min(HALF, cols - h * HALF)], h * HALF, min(HALF, cols - h * HALF))
                for h in range(2) if cols > h * HALF]

    def score(self, pair, cols, qh, ql, kh, kl):
        for ps, c0, n in self.banks_of(pair, cols):
            mm = self.mm3([ps], qh, ql, [kh[:, c0:c0 + n]], [kl[:, c0:c0 + n]], True, True)
        return self.pr.pe.did(mm)

    def stick_breaking(self, ctx, big):
        pr, H, PS = self.pr, self.H, self.PS
        act, dve, pool, pe = pr.act, pr.dve, pr.pool, pr.pe
        sb = lambda n, s, dt=F32: self.sb(ctx, n, s, dt)
        QH, QL, KH, KL = (sb(f"sb_{n}", [P, T], F32R) for n in ("qh", "ql", "kh", "kl"))
        om = [sb(f"sb_om{i}", [P, T]) for i in range(2)]
        be = [sb(f"sb_beta{i}", [P, T]) for i in range(4)]
        rem = [sb(f"sb_rem{i}", [P, T + 1]) for i in range(2)]
        at_buf = [sb(f"sb_at{i}", [P, T]) for i in range(2)]
        strict, loose = sb("sb_strict", [P, P]), sb("sb_loose", [P, P])
        dve.need(self.dma(strict[:], self.a["strict"]))
        dve.did(dve.e.tensor_scalar(loose[:], strict[:], -1.0, 1.0, ALU.mult, ALU.add))
        scale = SB_DH ** -0.5
        with pr.loop(PAIRS) as i:
            pr.meet()
            ready = [self.split_to(QH[:], QL[:], big[:, i, :]), self.split_to(KH[:], KL[:], big[:, i + 4, :])]
            pe.need(*[list(r) for r in ready])
            items = [(hh, t) for hh in range(2) for t in range(TT)]
            read, scanned, weighed = {}, {}, {}

            def scores(n, item):
                hh, t = item
                rows = slice(hh * SB_DH, (hh + 1) * SB_DH)
                pe.need(read.get(n - 2))
                tk = slice(t * P, (t + 1) * P)
                return self.score(n % 2, (t + 1) * P, QH[rows, tk], QL[rows, tk], KH[rows, :], KL[rows, :])

            def before(n, item, z, free):
                w, cols = n % 2, (item[1] + 1) * P
                bt = be[n % 4]
                diag = slice(cols - P, cols)
                ps = self.pair(w)[:, 0:cols]
                act.need(z, scanned.get(n - 2), free)
                o = act.did(act.e.activation(om[w][:, 0:cols], ps, ACT.Sigmoid, scale=-scale))
                b = read[n] = act.did(act.e.activation(bt[:, 0:cols], ps, ACT.Sigmoid, scale=scale))
                pool.need(o, weighed.get(n - 2))
                o = pool.did(pool.e.tensor_tensor(om[w][:, diag], om[w][:, diag], strict[:], ALU.mult))
                pool.need(b, o)
                pool.did(pool.e.tensor_tensor(om[w][:, diag], om[w][:, diag], loose[:], ALU.add))
                pool.did(pool.e.tensor_tensor(bt[:, diag], bt[:, diag], strict[:], ALU.mult))
                return pool.did(pool.e.memset(rem[w][:, cols:cols + 1], 1.0))

            def after(n, item, masked):
                w, cols = n % 2, (item[1] + 1) * P
                bt = be[n % 4]
                dve.need(masked, weighed.get(n - 2))
                back = lambda ap: ap[:, 0:cols][:, ::-1]
                r = scanned[n] = dve.did(dve.e.tensor_tensor_scan(
                    back(rem[w]), back(om[w]), back(om[w]), 1.0, ALU.mult, ALU.bypass))
                e = pool if n % 3 == 0 else dve
                e.need(r, masked)
                weighed[n] = e.did(e.e.tensor_tensor(
                    bt[:, 0:cols], bt[:, 0:cols], rem[w][:, 1:cols + 1], ALU.mult))
                return weighed[n]

            def v(item, b):
                return big[:, i + 8, b * P + item[0] * SB_DH:b * P + (item[0] + 1) * SB_DH]

            def evac(n, item, bank, done):
                hh, t = item
                dve.need(done)
                return dve.did(dve.e.tensor_copy(H[:, i + 4, t * P + hh * SB_DH:t * P + (hh + 1) * SB_DH], bank))

            self.attend(items, lambda it: it[1] + 1, scores, before, after, v, evac, be, at_buf, wide=SB_DH)

    def first_output(self):
        pr, H = self.pr, self.H
        act, dve = pr.act, pr.dve
        with ExitStack() as c:
            Y = self.sb(c, "mix1", [P, KT, T])
            UH, UL = self.operand(c, "o1")
            rows, s0, s1 = (self.sb(c, f"o1_t{k}", [P, T]) for k in range(3))
            for t in range(TT):
                tk = slice(t * P, (t + 1) * P)
                act.need(act.count.now())
                s = act.did(act.e.activation(s0[:, 0:HALF].rearrange("p (k c) -> p k c", c=P), H[:, 4:8, tk],
                                             ACT.Square, accum_out=self.sums[:, t:t + 1]))
            r = self.token_rstd(self.rt[:], self.sums[:], HG, (s,))
            dve.need(r)
            scaled = []
            for k in range(4, 8):
                for t in range(TT):
                    tk = slice(t * P, (t + 1) * P)
                    m = dve.did(dve.e.tensor_scalar(H[:, k, tk], H[:, k, tk], self.rt[:, t:t + 1], None, ALU.mult))
                scaled.append(m)
            self.to_channels([H[:, k, :] for k in range(KT)], self.g("hg_sb_out_norm"), UH, UL,
                             [None] * 4 + scaled)
            pr.meet(self.free)
            x_in = [self.dma(H[:, k, :], self.a["x_t"][k]) for k in range(KT)]
            self.project(8, UH, UL, lambda j: Y[:, j, :], None)
            pr.meet(self.free)
            for e in pr.compute:
                e.need(*x_in)
            self.add_normed(Y, self.g("attn_post_norm"), rows, s0, s1)
            pr.meet(self.free)

    def to_channels(self, slots, gain, UH, UL, after):
        pr = self.pr
        act, dve, pe = pr.act, pr.dve, pr.pe
        for k, src in enumerate(slots):
            p = self.claim()
            pe.need(after[k])
            for t in range(TT):
                tk = slice(t * P, (t + 1) * P)
                mm = pe.e.transpose(self.pair(p)[:, tk], src[:, tk], self.ident[:])
            mm = pe.did(mm)
            self.scaled_parts(UH[:, k, :], UL[:, k, :], self.pair(p), 1.0 if gain is None else gain[:, k:k + 1],
                              mm, self.free[p])

    def scaled_parts(self, hi, lo, src, gain, after, free=None):
        pr = self.pr
        act, dve = pr.act, pr.dve
        act.need(after)
        h = act.did(act.e.activation(hi, src, ACT.Copy, scale=gain))
        dve.need(h, after)
        i = dve.e.scalar_tensor_tensor(lo, src, gain, hi.bitcast(F32), ALU.mult, ALU.subtract)
        return [h, free.inc(i) if free else dve.did(i)]

    def add_normed(self, Y, gain, rows, s0, s1):
        pr, H = self.pr, self.H
        act, dve, pool, pe = pr.act, pr.dve, pr.pool, pr.pe
        sq, used = [s0[:], s1[:]], [None, None]
        for k in range(KT):
            q = sq[k % 2]
            if k % 2:
                dve.need(used[1])
                m = dve.did(dve.e.tensor_tensor(q, Y[:, k, :], Y[:, k, :], ALU.mult))
            else:
                act.need(used[0])
                m = act.did(act.e.activation(q, Y[:, k, :], ACT.Square))
            pe.need(m)
            s = used[k % 2] = self.token_sums(k, KT, q)
        self.statistics(s, D, rows[:])
        r = self.free[2].now()
        busy = [None, None]
        for k in range(KT):
            dve.need(r)
            m = dve.did(dve.e.scalar_tensor_tensor(Y[:, k, :], Y[:, k, :], gain[:, k:k + 1], rows[:],
                                                   ALU.mult, ALU.mult))
            e = pool if k % 3 == 0 else dve
            e.need(m)
            e.did(e.e.tensor_tensor(H[:, k, :], H[:, k, :], Y[:, k, :], ALU.add))

    def feed_forward(self, conv):
        pr, H, st, PS = self.pr, self.H, self.st, self.PS
        act, dve, pool, pe = pr.act, pr.dve, pr.pool, pr.pe
        tag = "f2" if conv else "f1"
        with ExitStack() as c:
            UH, UL = self.operand(c, tag)
            Y = H if conv else self.sb(c, f"{tag}_y", [P, KT, T])
            AH, AL = (self.sb(c, f"{tag}_a{x}", [P, 2, T], F32R) for x in "hl")
            sg = self.sb(c, f"{tag}_gate", [P, T])
            prod = self.sb(c, f"{tag}_prod", [P, T])
            rows = self.sb(c, f"{tag}_rows", [P, T])
            cw = self.sb(c, f"{tag}_cw", [P, 4]) if conv else None
            cg = self.sb(c, f"{tag}_conv_in", [P, T]) if conv else None
            if not conv:
                for k in range(KT):
                    pool.did(pool.e.memset(Y[:, k, :], 0.0))
            self.normed_input("ffn_norm_g_2" if conv else "ffn_pre_norm", UH, UL, [sg[:], prod[:]], rows[:])

            def gate(index, tile):
                p, done, s = self.product(index, UH, UL)
                if conv:
                    dve.need(act.count.now(), dve.count.now())
                    w = dve.did(dve.e.tensor_copy(cw[:], self.gains[:, bass.ds(tile * 4 + self.at["conv"][0], 4)]))
                    dve.need(done)
                    g = self.free[p].inc(dve.e.tensor_tensor(cg[:], self.pair(p), rows[:], ALU.mult))
                    act.need(g, w)
                    g = act.did(act.e.activation(sg[:], cg[:], ACT.Identity, scale=cw[:, 2:3], bias=cw[:, 3:4]))
                    for d, col in ((1, 1), (2, 0)):
                        dve.need(g)
                        g = dve.did(dve.e.scalar_tensor_tensor(
                            sg[:, d:], cg[:, :T - d], cw[:, col:col + 1], sg[:, d:], ALU.mult, ALU.add))
                else:
                    dve.need(done, dve.count.now(), act.count.now())
                    g = self.free[p].inc(dve.e.tensor_tensor(sg[:], self.pair(p), rows[:], ALU.mult))
                act.need(g)
                g = act.did(act.e.activation(sg[:], sg[:], ACT.Silu))
                st.split(s)
                return g

            def up(index, j, g):
                p, done, s = self.product(index, UH, UL)
                dve.need(done, act.count.now(), dve.count.now())
                m = self.free[p].inc(dve.e.tensor_tensor(prod[:], self.pair(p), rows[:], ALU.mult))
                dve.need(g, m)
                m = dve.did(dve.e.tensor_tensor(prod[:], prod[:], sg[:], ALU.mult))
                self.split_to(AH[:, j, :], AL[:, j, :], prod[:], after=(m, done))
                st.split(s)

            def down(index):
                s0, s1 = st.take(index), st.take(index + 1)
                pe.need(*self.a_ready)
                for n in range(KT):
                    p = self.claim()
                    for k, s in enumerate((s0, s1)):
                        mm = self.mm3([PS[:, 2 * p + h, :] for h in range(2)],
                                      st.hi[s][:, n * P:(n + 1) * P], st.lo[s][:, n * P:(n + 1) * P],
                                      [AH[:, k, h * HALF:(h + 1) * HALF] for h in range(2)],
                                      [AL[:, k, h * HALF:(h + 1) * HALF] for h in range(2)], k == 0, k == 1)
                        if n == KT - 1:
                            done = st.give(s, mm)
                        else:
                            done = pe.did(mm) if k else None
                    dve.need(done, self.free[p].now())
                    self.free[p].inc(dve.e.tensor_tensor(Y[:, n, :], Y[:, n, :], self.pair(p), ALU.add))
                st.split(s0)
                st.split(s1)

            g0 = st.g
            self.turn = 0
            g = gate(g0, 0)
            up(g0 + 1, 0, g)
            g = gate(g0 + 2, 1)
            up(g0 + 3, 1, g)
            base = st.g
            pr.meet(self.free)
            with pr.loop(FF_TILES // 2 - 1) as i:
                self.turn = 0
                at = i * 6
                self.a_ready = [act.count.now(), dve.count.now()]
                g = gate(at + base, i * 2 + 2)
                down(at + (base + 1))
                up(at + (base + 3), 0, g)
                g = gate(at + (base + 4), i * 2 + 3)
                up(at + (base + 5), 1, g)
            st.g = base + 6 * (FF_TILES // 2 - 1)
            self.turn = 1
            self.a_ready = [act.count.now(), dve.count.now()]
            down(st.g)
            pr.meet(self.free)
            if not conv:
                self.add_normed(Y, self.g("ffn_post_norm"), rows, sg, prod)
                pr.meet(self.free)

    def ple(self, p_dram, norm):
        pr, H, st = self.pr, self.H, self.st
        act, dve, pool, pe = pr.act, pr.dve, pr.pool, pr.pe
        tag = "p2" if norm else "p1"
        with ExitStack() as c:
            UH, UL = self.operand(c, tag)
            PP = self.sb(c, f"{tag}_pp", [P, KT, T])
            sg = [self.sb(c, f"{tag}_s{i}", [P, T]) for i in range(2)]
            rows = self.sb(c, f"{tag}_rows", [P, T]) if norm else None
            raw = [self.dma(PP[:, k, :], p_dram[k]) for k in range(2)]
            ready = [list(self.split_to(UH[:, 6 + k, :], UL[:, 6 + k, :], PP[:, k, :], after=(raw[k],)))
                     for k in range(2)]
            pe.need(*ready)
            act.need(*ready)
            self.turn = 0
            for half in range(2):
                s = st.take(st.g)
                for n in range(4):
                    p, mm = self.channels(s, UH[:, 6:8, :], UL[:, 6:8, :], range(2),
                                          lambda k: slice((2 * n + k) * P, (2 * n + k + 1) * P))
                    done = st.give(s, mm) if n == 3 else pe.did(mm)
                    act.need(done)
                    self.free[p].inc(act.e.activation(PP[:, 4 * half + n, :], self.pair(p), ACT.Copy))
                st.split(s)
            if norm:
                pr.meet(self.free)
                self.normed_input(norm, UH, UL, [sg[0][:], sg[1][:]], rows[:])
            else:
                self.prepare([H[:, k, :] for k in range(KT)], None, UH, UL,
                             after=[None] * 6 + [done, done])
                pr.meet(self.free)
            g0 = st.g

            def step(j, w, index):
                p, done, s = self.product(index, UH, UL)
                t = sg[w][:]
                if norm:
                    dve.need(done, act.count.now(), dve.count.now())
                    m = self.free[p].inc(dve.e.tensor_tensor(t, self.pair(p), rows[:], ALU.mult))
                    act.need(m)
                    g = act.did(act.e.activation(t, t, ACT.Sigmoid))
                else:
                    act.need(done, dve.count.now())
                    g = self.free[p].inc(act.e.activation(t, self.pair(p), ACT.Sigmoid))
                dve.need(g)
                m = dve.did(dve.e.tensor_tensor(t, t, PP[:, j, :], ALU.mult))
                dve.need(m)
                done = dve.did(dve.e.tensor_tensor(H[:, j, :], H[:, j, :], t, ALU.add))
                st.split(s)
                return done

            with pr.loop(2) as i:
                self.turn = 0
                for j in range(RING):
                    step(i * RING + j, j % 2, i * RING + (g0 + j))
            st.g = g0 + 2 * RING
            self.turn = 0
            for j in range(2 * RING, KT):
                step(j, j % 2, g0 + j)
            pr.meet(self.free)

    def second_mixer(self):
        pr, H = self.pr, self.H
        with ExitStack() as c:
            res = self.sb(c, "mixer2", [P, 16, T])
            with ExitStack() as cu:
                UH, UL = self.operand(cu, "2")
                rows = self.sb(cu, "mixer2_rows", [P, T])
                self.normed_input("attn_norm_g_2", UH, UL, [res[:, 0, :], res[:, 1, :]], rows[:])
                self.project(4, UH, UL, lambda j: res[:, j + 12, :], rows[:])
                for first in (0, 4, 8):
                    self.project_tokens(UH, UL, res[:, first:first + 4, :])
                pr.meet(self.free)
            with ExitStack() as cd:
                self.differential(cd, res)
            pr.meet(self.free)
            with ExitStack() as cm:
                self.mla(cm, res)
            pr.meet(self.free)
            with ExitStack() as co:
                self.second_output(co, res)
            pr.meet(self.free)

    def second_output(self, ctx, res):
        pr, H, st = self.pr, self.H, self.st
        dve = pr.dve
        UH, UL = self.operand(ctx, "o2")
        self.turn = 0
        self.to_channels([res[:, k, :] for k in range(KT)], self.gout8, UH, UL, [None] * KT)
        pr.meet(self.free)
        g0 = st.g

        def step(j, index):
            p, done, s = self.product(index, UH, UL)
            dve.need(done)
            self.free[p].inc(dve.e.tensor_tensor(H[:, j, :], H[:, j, :], self.pair(p), ALU.add))
            st.split(s)

        with pr.loop(2) as i:
            self.turn = 0
            for j in range(RING):
                step(i * RING + j, i * RING + (g0 + j))
        st.g = g0 + 2 * RING
        self.turn = 0
        for j in range(2 * RING, KT):
            step(j, g0 + j)

    def head_parts(self, src, d, hi, lo, gain, after, p):
        pr = self.pr
        pe = pr.pe
        pe.need(after, self.free[p].now())
        for t in range(TT):
            mm = pe.e.transpose(self.pair(p)[0:d, t * P:(t + 1) * P], src[:, t * d:(t + 1) * d], self.ident[:])
        mm = pe.did(mm)
        return self.scaled_parts(hi, lo, self.pair(p)[0:d], gain, mm, self.free[p])

    def differential(self, ctx, res):
        pr, PS = self.pr, self.PS
        act, dve, pool, pe = pr.act, pr.dve, pr.pool, pr.pe
        sb = lambda n, s, dt=F32: self.sb(ctx, n, s, dt)
        QH, QL, KH, KL = (sb(f"df_{n}", [P, T], F32R) for n in ("qh", "ql", "kh", "kl"))
        toep = sb("df_bias", [P, T])
        pm = [sb(f"df_p{i}", [P, T]) for i in range(6)]
        at_buf = [sb(f"df_at{i}", [P, T]) for i in range(2)]
        small = sb("df_small", [P, 4, 8])
        norms = sb("df_norms", [P, 2, 2 * TT])
        gq, lam2, nlam = sb("df_gq", [P, 1]), sb("df_lam2", [P, 2]), sb("df_nlam", [P, 1])
        scale = 64 ** -0.5
        dve.did(dve.e.tensor_scalar(gq[:], self.g("diff_q_norm_g_2"), scale, None, ALU.mult))
        dve.did(dve.e.memset(self.gout8[:], 1.0))
        dve.need(dve.count.now())
        dve.did(dve.e.tensor_scalar(self.gout8[:, 0:DIFF_H], self.g("diff_out_norm_g_2").to_broadcast([P, DIFF_H]),
                                    1.0 - LAM_INIT, None, ALU.mult))
        for n in range(2):
            dve.did(dve.e.tensor_tensor(lam2[:, n:n + 1], self.g(f"lambda_q{n + 1}_2"), self.g(f"lambda_k{n + 1}_2"),
                                        ALU.mult))
        pe.need(dve.count.now())
        t = pe.did(pe.e.matmul(PS[:, 0, 0:2], self.ones[:], lam2[:], start=True, stop=True))
        act.need(t)
        t = act.did(act.e.activation(lam2[:], PS[:, 0, 0:2], ACT.Exp))
        dve.need(t)
        t = dve.did(dve.e.tensor_tensor(nlam[:], lam2[:, 1:2], lam2[:, 0:1], ALU.subtract))
        dve.need(t)
        dve.did(dve.e.tensor_scalar(nlam[:], nlam[:], -LAM_INIT, None, ALU.add))
        table, spread = sb("df_table", [NBUCKET, DIFF_H]), sb("df_spread", [NBUCKET, P])
        rest = BIAS_LEN - T
        bucket0, bucket1 = pm[0][0:NBUCKET, :], pm[1][0:NBUCKET, 0:rest]
        ins = [self.dma(table[:], self.a["rel_bias"]), self.dma(bucket0, self.a["bucket"][:, 0:T]),
               self.dma(bucket1, self.a["bucket"][:, T:BIAS_LEN])]
        lines = self.nc.dram_tensor("bias_lines", (DIFF_H, P, BIAS_LEN), F32)
        pe.need(*ins)
        dve.need(*ins)
        wrote = []
        for h in range(DIFF_H):
            dve.need(pe.count.now())
            t = dve.did(dve.e.tensor_scalar(spread[:], self.ones[0:NBUCKET, :], table[:, h:h + 1], None, ALU.mult))
            pe.need(t, act.count.now())
            pe.e.matmul(PS[:, 2, :], spread[:], bucket0[:, 0:HALF], start=True, stop=True)
            pe.e.matmul(PS[:, 3, :], spread[:], bucket0[:, HALF:T], start=True, stop=True)
            t = pe.did(pe.e.matmul(PS[:, 4, 0:rest], spread[:], bucket1, start=True, stop=True))
            w = 2 + 2 * (h % 2)
            act.need(t, wrote[h - 2] if h > 1 else None)
            act.did(act.e.activation(pm[w][:], self.pair(1), ACT.Copy))
            t = act.did(act.e.activation(pm[w + 1][:, 0:rest], PS[:, 4, 0:rest], ACT.Copy))
            pr.sp.need(t)
            wrote.append([self.dma(lines.ap()[h, :, 0:T], pm[w][:]),
                          self.dma(lines.ap()[h, :, T:BIAS_LEN], pm[w + 1][:, 0:rest])])
        for e in (act, dve, pr.sp):
            e.need(*wrote)
        bias_in = Count(pr, "df_bias_in", 16)
        toeplitz = bass.AP(lines, P - 1, [[P * BIAS_LEN, DIFF_H], [BIAS_LEN - 1, P], [1, T]])

        with pr.loop(DIFF_H) as h:
            pr.meet(self.free)
            bias = bias_in.inc(pr.sp.e.dma_start(toep[:], toeplitz[h]))
            for n, (src, gain, hi, lo) in enumerate(((res[:, h, :], gq[:], QH, QL),
                                                     (res[:, h + 4, :], self.g("diff_k_norm_g_2"), KH, KL))):
                sq, x = pm[2 * n], pm[2 * n + 1]
                groups = lambda ap: ap.rearrange("p (g c) -> p g c", c=64)
                t = act.did(act.e.activation(sq[:], src, ACT.Square))
                dve.need(t)
                t = dve.did(dve.e.tensor_reduce(norms[:, n, :], groups(sq[:]), AX.X, ALU.add))
                r = self.token_rstd(norms[:, n, :], norms[:, n, :], 64, (t,))
                dve.need(r)
                rb = norms[:, n, :].unsqueeze(2).to_broadcast([P, 2 * TT, 64])
                m = dve.did(dve.e.tensor_tensor(groups(x[:]), groups(src), rb, ALU.mult))
                parts = self.head_parts(x[:], P, hi[:], lo[:], gain, m, n)
                pe.need(*parts)
                act.need(*parts)
                dve.need(*parts)
            dve.need(bias)
            read, weights = {}, {}

            def scores(n, t):
                out = []
                for m in range(2):
                    rows, tk = slice(64 * m, 64 * m + 64), slice(t * P, (t + 1) * P)
                    pe.need(read.get((n - 1, m)))
                    out.append(self.score(m, (t + 1) * P, QH[rows, tk], QL[rows, tk], KH[rows, :], KL[rows, :]))
                return out

            def before(n, t, z, free):
                cols, w, s = (t + 1) * P, n % 3, n % 4
                ls = []
                for m in range(2):
                    pb = pm[2 * w + m]
                    ps = self.pair(m)
                    dve.need(z[m], free, weights.get(n - 3))
                    t0 = dve.did(dve.e.memset(ps[0:64, cols - 64:cols], -1e30))
                    dve.need(t0)
                    t1 = read[(n, m)] = dve.did(dve.e.tensor_tensor(
                        pb[:, 0:cols], ps[:, 0:cols], toep[:, (TT - 1 - t) * P:T], ALU.add))
                    dve.need(t1)
                    t2 = dve.did(dve.e.tensor_reduce(small[:, s, m:m + 1], pb[:, 0:cols], AX.X, ALU.max,
                                                     negate=True))
                    act.need(t2)
                    ls.append(act.did(act.e.activation(pb[:, 0:cols], pb[:, 0:cols], ACT.Exp,
                                                       bias=small[:, s, m:m + 1],
                                                       accum_out=small[:, s, 2 + m:3 + m])))
                return ls

            def after(n, t, ls):
                cols, w, s = (t + 1) * P, n % 3, n % 4
                p0, p1 = pm[2 * w], pm[2 * w + 1]
                dve.need(*ls)
                t3 = dve.did(dve.e.reciprocal(small[:, s, 4:6], small[:, s, 2:4]))
                dve.need(t3)
                t4 = dve.did(dve.e.tensor_scalar(small[:, s, 6:7], small[:, s, 5:6], nlam[:], small[:, s, 2:3],
                                                 ALU.mult, ALU.mult))
                dve.need(t4)
                weights[n] = dve.did(dve.e.scalar_tensor_tensor(
                    p0[:, 0:cols], p1[:, 0:cols], small[:, s, 6:7], p0[:, 0:cols], ALU.mult, ALU.add))
                return weights[n]

            def evac(n, t, bank, done):
                dve.need(done, self.q_done)
                return dve.did(dve.e.tensor_scalar(res[:, h, t * P:(t + 1) * P], bank, small[:, n % 4, 4:5], None,
                                                   ALU.mult))

            self.q_done = parts
            self.attend(list(range(TT)), lambda t: t + 1, scores, before, after,
                        lambda t, b: res[:, h + 8, b * P:(b + 1) * P], evac,
                        [pm[0], pm[2], pm[4]], at_buf)
            dve.need(dve.count.now())
            act.need(dve.count.now(), act.count.now())
            t = act.did(act.e.activation(pm[1][:], res[:, h, :], ACT.Square))
            dve.need(t)
            t = dve.did(dve.e.tensor_reduce(norms[:, 0, 0:TT], pm[1][:].rearrange("p (g c) -> p g c", c=P),
                                            AX.X, ALU.add))
            r = self.token_rstd(norms[:, 0, 0:TT], norms[:, 0, 0:TT], P, (t,))
            dve.need(r)
            o3 = res[:, h, :].rearrange("p (g c) -> p g c", c=P)
            dve.did(dve.e.tensor_tensor(o3, o3, norms[:, 0, 0:TT].unsqueeze(2).to_broadcast([P, TT, P]), ALU.mult))

    def mla(self, ctx, res):
        pr, PS, st = self.pr, self.PS, self.st
        act, dve, pool, pe = pr.act, pr.dve, pr.pool, pr.pe
        sb = lambda n, s, dt=F32: self.sb(ctx, n, s, dt)
        W = TT * MLA_QK
        HALF_R = MLA_ROPE // 2
        V = res[:, 8:12, :]
        qt = sb("mla_q", [P, MLA_H, W])
        kt = sb("mla_k", [P, MLA_H, TT * MLA_NOPE])
        kr = sb("mla_kr", [P, TT, MLA_ROPE])
        krope_sq = sb("mla_kr_sq", [P, TT])
        rope = sb("mla_rope", [P, 2, TT, HALF_R])
        rg = sb("mla_rope_gain", [P, 2, MLA_ROPE])
        ngain = sb("mla_nope_gain", [P, 2])
        small = sb("mla_small", [P, 4, 4])
        norms = sb("mla_norms", [P, 2, TT])
        rt = sb("mla_latent_r", [P, 2, TT])
        tmp = sb("mla_tmp", [P, 2, TT, MLA_ROPE])
        ins = [self.dma(rope[:].rearrange("p a b c -> p (a b c)"), self.a["rope"]),
               self.dma(rg[:].rearrange("p a b -> p (a b)"), self.a["rope_gain"].partition_broadcast(P))]
        for e in (act, dve, pool):
            e.need(*ins)
        dve.did(dve.e.memset(ngain[:], 1.0))
        dve.need(dve.count.now())
        dve.did(dve.e.tensor_copy(ngain[0:MLA_NOPE, 0:1], self.g("mla_q_norm_g_2")[0:MLA_NOPE]))
        dve.did(dve.e.tensor_copy(ngain[0:MLA_NOPE, 1:2], self.g("mla_k_norm_g_2")[0:MLA_NOPE]))
        with ExitStack() as c:
            LH, LL = (self.sb(c, f"mla_l{x}", [P, 3, T], F32R) for x in "hl")
            sq = [res[:, 4, :], res[:, 5, :]]
            for n, (first, count, name) in enumerate(((0, 2, "q_lat_norm_g_2"), (2, 1, "kv_lat_norm_g_2"))):
                src = [res[:, 12 + first + k, :] for k in range(count)]
                s = self.prepare(src, self.g(name), LH[:, first:first + count, :], LL[:, first:first + count, :],
                                 sq=sq)
                self.token_rstd(rt[:, n, :], PS[:, 7, 0:TT], count * P, (s,))
                pr.meet(self.free)
            for t in range(TT):
                mm = pe.e.transpose(PS[:, 6, t * MLA_ROPE:(t + 1) * MLA_ROPE],
                                    res[0:MLA_ROPE, 15, t * P:(t + 1) * P], self.ident[0:MLA_ROPE, 0:MLA_ROPE])
            mm = pe.did(mm)
            act.need(mm)
            act.did(act.e.activation(kr[:].rearrange("p a b -> p (a b)"), PS[:, 6, 0:TT * MLA_ROPE], ACT.Copy))
            pr.meet(self.free)
            s0, s1 = st.take(st.g), st.take(st.g)
            for t in range(TT):
                tk = slice(t * P, (t + 1) * P)
                p = self.claim()
                for b in range(2):
                    for k, s in enumerate((s0, s1)):
                        cols = slice(b * 384, (b + 1) * 384)
                        wh, wl, out = st.hi[s][:, cols], st.lo[s][:, cols], PS[:, 2 * p + b, 0:384]
                        pe.e.matmul(out, LH[:, k, tk], wh, start=k == 0, stop=False)
                        pe.e.matmul(out, LH[:, k, tk], wl, start=False, stop=False)
                        mm = pe.e.matmul(out, LL[:, k, tk], wh, start=False, stop=k == 1)
                        if t == TT - 1 and b == 1:
                            done = st.give(s, mm)
                if t < TT - 1:
                    done = pe.did(mm)
                act.need(done)
                for b in range(2):
                    i = act.e.activation(qt[:, 4 * b:4 * b + 4, t * MLA_QK:(t + 1) * MLA_QK],
                                         PS[:, 2 * p + b, 0:384].rearrange("p (h c) -> p h c", c=MLA_QK),
                                         ACT.Copy, scale=rt[:, 0, t:t + 1])
                    self.free[p].inc(i) if b else act.did(i)
            st.split(s0)
            st.split(s1)
            s = st.take(st.g)
            for t in range(TT):
                tk = slice(t * P, (t + 1) * P)
                p = self.claim()
                for b in range(2):
                    cols, out = slice(b * 512, (b + 1) * 512), PS[:, 2 * p + b, :]
                    pe.e.matmul(out, LH[:, 2, tk], st.hi[s][:, cols], start=True, stop=False)
                    pe.e.matmul(out, LH[:, 2, tk], st.lo[s][:, cols], start=False, stop=False)
                    mm = pe.e.matmul(out, LL[:, 2, tk], st.hi[s][:, cols], start=False, stop=True)
                done = st.give(s, mm) if t == TT - 1 else pe.did(mm)
                act.need(done)
                act.did(act.e.activation(kt[:, :, t * MLA_NOPE:(t + 1) * MLA_NOPE],
                                         PS[:, 2 * p, :].rearrange("p (h c) -> p h c", c=MLA_NOPE),
                                         ACT.Copy, scale=rt[:, 1, t:t + 1]))
                self.free[p].inc(act.e.activation(V[:, :, tk], PS[:, 2 * p + 1, :].rearrange(
                    "p (k c) -> p k c", c=P), ACT.Copy, scale=rt[:, 1, t:t + 1]))
            st.split(s)
            pr.meet(self.free)

        QH, QL, KH, KL = (sb(f"mla_{n}", [P, T], F32R) for n in ("qh", "ql", "kh", "kl"))
        pm = [res[:, 12, :], res[:, 13, :], res[:, 14, :]]
        at_buf = [res[:, 15, :], sb("mla_at", [P, T])[:]]
        scale = MLA_QK ** -0.5
        R = slice(0, MLA_QK)

        def rotate(e, x, gain):
            a, b = slice(0, HALF_R), slice(HALF_R, MLA_ROPE)
            cos, sin = rope[:, 0], rope[:, 1]
            e.need(e.count.now())
            t = e.did(e.e.tensor_tensor(x, x, gain.unsqueeze(1).to_broadcast([P, TT, MLA_ROPE]), ALU.mult))
            e.need(t)
            e.did(e.e.tensor_tensor(tmp[:, 0, :, a], x[:, :, b], sin, ALU.mult))
            e.did(e.e.tensor_tensor(tmp[:, 0, :, b], x[:, :, a], sin, ALU.mult))
            e.did(e.e.tensor_tensor(tmp[:, 1, :, a], x[:, :, a], cos, ALU.mult))
            t = e.did(e.e.tensor_tensor(tmp[:, 1, :, b], x[:, :, b], cos, ALU.mult))
            e.need(t)
            e.did(e.e.tensor_tensor(x[:, :, a], tmp[:, 1, :, a], tmp[:, 0, :, a], ALU.subtract))
            return e.did(e.e.tensor_tensor(x[:, :, b], tmp[:, 1, :, b], tmp[:, 0, :, b], ALU.add))

        t = act.did(act.e.activation(tmp[:, 0], kr[:], ACT.Square))
        dve.need(t)
        dve.did(dve.e.tensor_reduce(krope_sq[:], tmp[:, 0], AX.X, ALU.add))
        rotate(dve, kr[:], rg[:, 1])

        with pr.loop(MLA_H // 2) as i:
            for hh in range(2):
                pr.meet(self.free)
                q3 = qt[:, i * 2 + hh, :].rearrange("p (g c) -> p g c", c=MLA_QK)
                k3 = kt[:, i * 2 + hh, :].rearrange("p (g c) -> p g c", c=MLA_NOPE)
                sq = [pm[0].rearrange("p (g c) -> p g c", c=P)[:, :, 0:MLA_QK],
                      pm[1].rearrange("p (g c) -> p g c", c=P)[:, :, 0:MLA_NOPE]]
                x = [pm[2][:, 0:W].rearrange("p (g c) -> p g c", c=MLA_QK),
                     at_buf[0][:, 0:W].rearrange("p (g c) -> p g c", c=MLA_QK)]
                sk = act.did(act.e.activation(sq[1], k3, ACT.Square))
                sq_ = act.did(act.e.activation(sq[0], q3, ACT.Square))
                dve.need(sk)
                t = dve.did(dve.e.tensor_reduce(norms[:, 1, :], sq[1], AX.X, ALU.add))
                dve.need(t)
                t = dve.did(dve.e.tensor_tensor(norms[:, 1, :], norms[:, 1, :], krope_sq[:], ALU.add))
                dve.need(sq_)
                tq = dve.did(dve.e.tensor_reduce(norms[:, 0, :], sq[0], AX.X, ALU.add))
                r = self.token_rstd(norms[:], norms[:], MLA_QK, (t, tq))
                dve.need(r)
                rb = lambda n, d: norms[:, n, :].unsqueeze(2).to_broadcast([P, TT, d])
                dve.did(dve.e.tensor_tensor(x[1][:, :, 0:MLA_NOPE], k3, rb(1, MLA_NOPE), ALU.mult))
                m = dve.did(dve.e.tensor_tensor(x[1][:, :, MLA_NOPE:MLA_QK], kr[:], rb(1, MLA_ROPE), ALU.mult))
                kp = self.head_parts(at_buf[0], MLA_QK, KH[R], KL[R], ngain[R, 1:2], m, 1)
                mq = dve.did(dve.e.tensor_tensor(x[0], q3, rb(0, MLA_QK), ALU.mult))
                dve.need(mq)
                m = rotate(dve, x[0][:, :, MLA_NOPE:MLA_QK], rg[:, 0])
                qp = self.head_parts(pm[2], MLA_QK, QH[R], QL[R], ngain[R, 0:1], m, 0)
                for e in (pe, act, dve):
                    e.need(*kp, *qp)
                read = {}

                def scores(n, t):
                    pe.need(read.get(n - 2))
                    tk = slice(t * P, (t + 1) * P)
                    return self.score(n % 2, (t + 1) * P, QH[R, tk], QL[R, tk], KH[R, :], KL[R, :])

                def before(n, t, z, free):
                    cols, w = (t + 1) * P, n % 4
                    ps = self.pair(n % 2)
                    dve.need(z)
                    t0 = dve.did(dve.e.memset(ps[0:64, cols - 64:cols], -1e30))
                    dve.need(t0)
                    mx = dve.did(dve.e.tensor_reduce(small[:, w, 0:1], ps[:, 0:cols], AX.X, ALU.max, negate=True))
                    dve.need(mx)
                    mx = dve.did(dve.e.tensor_scalar(small[:, w, 1:2], small[:, w, 0:1], scale, None, ALU.mult))
                    act.need(mx, free)
                    read[n] = act.did(act.e.activation(pm[n % 3][:, 0:cols], ps[:, 0:cols], ACT.Exp, scale=scale,
                                                       bias=small[:, w, 1:2], accum_out=small[:, w, 2:3]))
                    return read[n]

                def after(n, t, e):
                    dve.need(e)
                    w = n % 4
                    return dve.did(dve.e.reciprocal(small[:, w, 3:4], small[:, w, 2:3]))

                def evac(n, t, bank, done):
                    dve.need(done)
                    return dve.did(dve.e.tensor_scalar(
                        res[:, i + 4, t * P + hh * 64:t * P + (hh + 1) * 64], bank, small[:, n % 4, 3:4], None,
                        ALU.mult))

                self.attend(list(range(TT)), lambda t: t + 1, scores, before, after,
                            lambda t, b: V[:, i, b * P + hh * 64:b * P + (hh + 1) * 64], evac, pm, at_buf, wide=64,
                            copier=lambda n: dve if n % 2 else act)

    def store(self):
        pr = self.pr
        pr.sp.need(*[self.dma(self.out_ap[k], self.H[:, k, :]) for k in range(KT)])


BIAS_LEN = T + P - 1


def build_program(nc, rates, a, gains, out):
    k = Kernel.__new__(Kernel)
    k.at = gains
    k.__init__(nc, rates, a, out)


GAINS = {}


def _lay(inp):
    def tiles(v):
        return np.ascontiguousarray(np.asarray(v).reshape(-1, P).T)

    def chan(w, c0, width=P):
        k = w.shape[0] // P
        u = np.zeros((P, k, P), w.dtype)
        u[:, :, :width] = w[:, c0:c0 + width].reshape(k, P, width).transpose(1, 0, 2)
        return [u.reshape(P, k * P)]

    def chans(w, cols):
        return [u for c in cols for u in chan(w, c)]

    def tokens(w):
        u = w.reshape(4, 2, P, 512).transpose(0, 2, 1, 3).reshape(4, P, 1024)
        return list(u)

    def rows(w, k):
        return [w[k * P:(k + 1) * P]]

    def small(w):
        u = w.reshape(2, P, 2, 4, P).transpose(2, 1, 3, 0, 4).reshape(2, P, 1024)
        return list(u)

    def ffn(gate, up, down):
        n, u = FF_TILES // 2, []
        for g in range(n):
            if g:
                u += chan(gate, 2 * g * P)
                u += rows(down, 2 * g - 2) + rows(down, 2 * g - 1)
            else:
                u += chan(gate, 0)
            u += chan(up, 2 * g * P) + chan(gate, (2 * g + 1) * P) + chan(up, (2 * g + 1) * P)
        return u + rows(down, 2 * n - 2) + rows(down, 2 * n - 1)

    w1 = np.asarray(inp["w_in"])[0]
    w2 = np.asarray(inp["w_in_2"])[0]
    gu = np.asarray(inp["w_gate_up"])[0]
    span = lambda c, n: [c + P * j for j in range(n)]
    units = chans(w1, span(0, 8))
    units += tokens(w1[:, 1536:2048]) + tokens(w1[:, 1024:1536])
    units += chans(w1, span(2048, 8)) + tokens(w1[:, 3072:3584])
    units += chans(np.asarray(inp["w_out"])[0], span(0, 8))
    units += ffn(gu[:, :2816], gu[:, 2816:], np.asarray(inp["w_down"])[0])
    units += small(np.asarray(inp["ple_proj"])[0])
    units += chans(np.asarray(inp["ple_gate"])[0], span(0, 8))
    units += chans(w2, [0, 128, 256]) + chan(w2, 384, MLA_ROPE)
    for c in (416, 928, 1440):
        units += tokens(w2[:, c:c + 512])
    uq = np.asarray(inp["w_uq_2"])[0]
    for k in range(2):
        u = np.zeros((P, UNIT), w1.dtype)
        u[:, :uq.shape[1]] = uq[k * P:(k + 1) * P]
        units.append(u)
    ukv = np.asarray(inp["w_ukv_2"])[0].reshape(P, MLA_H, 2, 64)
    units.append(ukv.transpose(0, 2, 1, 3).reshape(P, 1024))
    wo = np.asarray(inp["w_out_2"])[0]
    wo = np.concatenate([wo[512:], wo[:512]])
    units += chans(wo, span(0, 8))
    units += ffn(np.asarray(inp["w_gate_2"])[0], np.asarray(inp["w_up_2"])[0], np.asarray(inp["w_down_2"])[0])
    units += small(np.asarray(inp["w_ple_proj_2"])[0])
    units += chans(np.asarray(inp["w_ple_gate_2"])[0], span(0, 8))
    units += [np.zeros((P, UNIT), w1.dtype)] * RING
    arrays = {"weights": np.stack(units)}

    def flat(w):
        return np.asarray(w)[0].T.reshape(-1, P, T)

    arrays["x_t"] = np.ascontiguousarray(np.asarray(inp["x"])[0].T).reshape(KT, P, T)
    arrays["p_t"] = np.ascontiguousarray(np.asarray(inp["p"])[0, 0].T).reshape(2, P, T)
    arrays["p2_t"] = np.ascontiguousarray(np.asarray(inp["p_2"])[0, 0].T).reshape(2, P, T)

    cols, at = [], 0
    GAINS.clear()

    def put(name, m):
        nonlocal at
        z = np.zeros((P, m.shape[1]), np.float32)
        z[:m.shape[0]] = m
        cols.append(z)
        GAINS[name] = (at, m.shape[1])
        at += m.shape[1]

    put("hg_sb_out_norm", tiles(np.concatenate([np.asarray(inp["hg_out_norm"])[0],
                                                np.asarray(inp["sb_out_norm"])[0]])))
    for name in ("attn_pre_norm", "attn_post_norm", "ffn_pre_norm",
                 "ffn_post_norm", "attn_norm_g_2", "q_lat_norm_g_2", "kv_lat_norm_g_2",
                 "diff_out_norm_g_2", "ffn_norm_g_2", "ple_norm_g_2"):
        put(name, tiles(np.asarray(inp[name])[0]))
    for name in ("mla_q_norm_g_2", "mla_k_norm_g_2", "lambda_q1_2", "lambda_k1_2", "lambda_q2_2", "lambda_k2_2"):
        put(name, np.asarray(inp[name])[0][:, None])
    for name in ("diff_q_norm_g_2", "diff_k_norm_g_2"):
        g = np.asarray(inp[name])[0]
        put(name, np.concatenate([g, g])[:, None])
    g = np.asarray(inp["hg_lower_gamma"])
    put("gamma0", tiles(g[0]))
    put("gamma1", tiles(g[1]))
    cw = np.asarray(inp["conv_w_2"])[0]
    taps = np.concatenate([cw, np.asarray(inp["conv_b_2"])])
    put("conv", taps.reshape(4, FF_TILES, P).transpose(2, 1, 0).reshape(P, 4 * FF_TILES))
    arrays["rope_gain"] = np.concatenate([np.asarray(inp["mla_q_norm_g_2"])[0, MLA_NOPE:],
                                          np.asarray(inp["mla_k_norm_g_2"])[0, MLA_NOPE:]])
    arrays["gains"] = np.concatenate(cols, axis=1)
    arrays["rel_bias"] = np.ascontiguousarray(np.asarray(inp["rel_bias_2"]))
    arrays.update(_constants())
    return arrays


def _constants():
    c = {"ident": np.eye(P, dtype=np.float32)}
    s, t = np.arange(P)[:, None], np.arange(P)[None, :]
    masks = [(s // (2 * h) == t // (2 * h)) & (s % (2 * h) < h) & (t % (2 * h) >= h) for h in LEVELS]
    masks.append(s == t)
    c["levels"] = np.stack(masks, axis=1).astype(np.float32)
    c["strict"] = (t < s).astype(np.float32)
    half = MLA_ROPE // 2
    ang = (np.arange(T, dtype=np.float32)[:, None]
           * (np.float32(10000.0) ** (-np.arange(half, dtype=np.float32) / half)).astype(np.float32)[None, :])
    tables = np.stack([np.cos(ang), np.sin(ang)]).astype(np.float32)
    c["rope"] = np.ascontiguousarray(tables.reshape(2, TT, P, half).transpose(2, 0, 1, 3)).reshape(P, -1)
    rel = np.arange(BIAS_LEN) - (T - 1)
    n = np.abs(rel)
    large = 8 + (np.log(np.maximum(n, 1).astype(np.float32) / 8) / math.log(1024 / 8) * 8).astype(np.int32)
    bucket = np.where(rel > 0, 16, 0) + np.where(n < 8, n, np.minimum(large, 15))
    c["bucket"] = (np.arange(NBUCKET)[:, None] == bucket[None, :]).astype(np.float32)
    return c


def kernel(**inputs):
    import concourse.bacc as _bacc
    from concourse.bass_utils import run_bass_kernel_spmd as _run

    arrays = _lay(inputs)
    gains = dict(GAINS)
    rates = {}
    for _ in range(2):
        nc = _bacc.Bacc("TRN2", target_bir_lowering=False, num_devices=1)
        aps = {n: nc.dram_tensor("in_" + n, v.shape, mybir.dt.from_np(v.dtype), kind="ExternalInput").ap()
               for n, v in arrays.items()}
        out = nc.dram_tensor("out_t", (KT, P, T), F32, kind="ExternalOutput").ap()
        build_program(nc, rates, aps, gains, out)
    r = _run(nc, [{"in_" + n: v for n, v in arrays.items()}], core_ids=[0])
    return np.ascontiguousarray(r.results[0]["out_t"].reshape(D, T).T).reshape(1, T, D)
```

```python
import math
from contextlib import ExitStack, contextmanager

import numpy as np

import concourse.bass as bass
from concourse import mybir

F32 = mybir.dt.float32
F32R = mybir.dt.float32r
U8 = mybir.dt.uint8
ACT = mybir.ActivationFunctionType
ALU = mybir.AluOpType
AX = mybir.AxisListType

P = 128
T = 1024
D = 1024
KT = D // P
TT = T // P
HALF = 512
EPS = 1e-6

HG = 512
HGH = HG // P
SB_DH = 64
PAIRS = 512 // (2 * SB_DH)
FF_TILES = 2816 // P
MLA_H, MLA_NOPE, MLA_ROPE = 8, 64, 32
MLA_QK = MLA_NOPE + MLA_ROPE
DIFF_H = 4
NBUCKET = 32
LAM_INIT = 0.8 - 0.6 * math.exp(-0.3 * 0)
RING = 3
UNIT = 1024
LEVELS = [64, 32, 16, 8, 4, 2, 1]
FILL = [4, 3, 2, 4, 3, 2, 1]


class Count:

    def __init__(self, prog, name, by=1):
        self.sem = prog.ctx.enter_context(prog.nc.semaphore(name))
        self.name, self.by, self.const, self.rate, self.reg = name, by, 0, 0, None
        prog.counts[name] = self

    def inc(self, ins):
        ins.then_inc(self.sem, self.by)
        self.const += self.by
        return self.now()

    def now(self):
        return (self, self.const, self.rate, self.reg)


class Engine:

    def __init__(self, prog, e, name):
        self.e, self.name = e, name
        self.count = Count(prog, "done_" + name)
        self.seen = {}

    def need(self, *tickets):
        waited = False
        for t in tickets:
            if t is None:
                continue
            if isinstance(t, list):
                self.need(*t)
                continue
            c, const, rate, reg = t
            if rate == 0:
                if const <= 0 or self.seen.get(c.name, 0) >= const:
                    continue
                self.seen[c.name] = const
                self.e.wait_ge(c.sem, const)
            else:
                assert const >= 1, (c.name, const)
                if self.seen.get((c.name, rate), 0) >= const:
                    continue
                self.seen[(c.name, rate)] = const
                self.e.wait_ge(c.sem, reg * rate + const)
                waited = True
                if self.name == "sp":
                    self.e.nop(nofuse=True)
        if waited and self.name in ("act", "dve"):
            self.e.nop(nofuse=True)

    def did(self, ins):
        return self.count.inc(ins)


class Prog:
    def __init__(self, nc, ctx, rates):
        self.nc, self.ctx, self.counts, self.rates = nc, ctx, {}, rates
        self.loops = 0
        self.pe = Engine(self, nc.tensor, "pe")
        self.act = Engine(self, nc.scalar, "act")
        self.dve = Engine(self, nc.vector, "dve")
        self.pool = Engine(self, nc.gpsimd, "pool")
        self.sp = Engine(self, nc.sync, "sp")
        self.engines = [self.pe, self.act, self.dve, self.pool, self.sp]
        self.compute = [self.pe, self.act, self.dve, self.pool]

    def meet(self, extra=()):
        t = [e.count.now() for e in self.compute] + [c.now() for c in extra]
        for e in self.engines:
            e.need(*t)

    @contextmanager
    def loop(self, n):
        key = self.loops
        self.loops += 1
        rate = self.rates.get(key, {})
        start = {k: c.const for k, c in self.counts.items()}
        with self.nc.Fori(0, n, 1) as i:
            for e in self.engines:
                e.seen = {}
            for k, c in self.counts.items():
                c.rate, c.reg = rate.get(k, 0), i
            yield i
        for e in self.engines:
            e.seen = {}
        got = {k: c.const - start.get(k, 0) for k, c in self.counts.items()}
        if key in self.rates:
            assert {k: v for k, v in got.items() if v} == {k: v for k, v in rate.items() if v}
        self.rates[key] = got
        for k, c in self.counts.items():
            c.const = start.get(k, 0) + n * got[k]
            c.rate, c.reg = 0, None


class Stream:

    def __init__(self, pr, dram, sb):
        self.pr, self.dram = pr, dram
        self.raw = [sb(f"w_raw{s}", [P, UNIT], F32) for s in range(RING)]
        self.hi = [sb(f"w_hi{s}", [P, UNIT], F32R) for s in range(RING)]
        self.lo = [sb(f"w_lo{s}", [P, UNIT], F32R) for s in range(RING)]
        self.loaded = [Count(pr, f"w_loaded{s}", 16) for s in range(RING)]
        self.hi_done = [Count(pr, f"w_hi_done{s}") for s in range(RING)]
        self.lo_done = [Count(pr, f"w_lo_done{s}") for s in range(RING)]
        self.used = [Count(pr, f"w_used{s}") for s in range(RING)]
        self.g = 0
        self.total = dram.shape[0]

    def load(self, s, index):
        pr = self.pr
        pr.sp.need(self.hi_done[s].now(), self.lo_done[s].now())
        self.loaded[s].inc(pr.sp.e.dma_start(self.raw[s][:], self.dram[index]))

    def split(self, s):
        pr = self.pr
        pr.act.need(self.loaded[s].now(), self.used[s].now())
        hi = self.hi_done[s].inc(pr.act.e.activation(self.hi[s][:], self.raw[s][:], ACT.Copy))
        pr.dve.need(self.loaded[s].now(), self.used[s].now(), hi)
        self.lo_done[s].inc(pr.dve.e.tensor_tensor(
            self.lo[s][:], self.raw[s][:], self.hi[s][:].bitcast(F32), ALU.subtract))

    def start(self):
        for s in range(RING):
            self.load(s, s)
            self.split(s)

    def take(self, index):
        s = self.g % RING
        self.g += 1
        self.load(s, index + RING)
        self.pr.pe.need(self.hi_done[s].now(), self.lo_done[s].now())
        return s

    def give(self, s, last):
        return self.used[s].inc(last)


class Kernel:
    def __init__(self, nc, rates, a, out):
        self.nc, self.a, self.out_ap = nc, a, out
        with ExitStack() as ctx:
            self.pr = Prog(nc, ctx, rates)
            self.build(ctx)

    def sb(self, ctx, name, shape, dt=F32):
        return ctx.enter_context(self.nc.sbuf_tensor(name, shape, dt))

    def dma(self, dst, src):
        self.n_dma += 1
        c = Count(self.pr, f"dma_{self.n_dma}", 16)
        return c.inc(self.pr.sp.e.dma_start(dst, src))

    def mm3(self, banks, lh, ll, rh, rl, first, last):
        e, n = self.pr.pe.e, len(banks)
        for i in range(n):
            ins = e.matmul(banks[i], lh, rh[i], start=first, stop=False)
        for i in range(n):
            ins = e.matmul(banks[i], lh, rl[i], start=False, stop=False)
        for i in range(n):
            ins = e.matmul(banks[i], ll, rh[i], start=False, stop=last)
        return ins

    def split_to(self, hi, lo, src, after=()):
        pr = self.pr
        pr.act.need(*after)
        h = pr.act.did(pr.act.e.activation(hi, src, ACT.Copy))
        pr.dve.need(*after, h)
        return h, pr.dve.did(pr.dve.e.tensor_tensor(lo, src, hi.bitcast(F32), ALU.subtract))

    def token_sums(self, k, n, sq):
        e = self.pr.pe.e
        for t in range(TT):
            ins = e.matmul(self.PS[:, 7, t:t + 1], sq[:, t * P:(t + 1) * P], self.ones[:, 0:1],
                           start=k == 0 and t == 0, stop=k == n - 1 and t == TT - 1, skip_group_check=True)
        return self.pr.pe.did(ins)

    def token_rstd(self, r, sums, dim, after):
        pr = self.pr
        pr.act.need(*after)
        t = pr.act.did(pr.act.e.activation(r, sums, ACT.Sqrt, scale=1.0 / dim, bias=self.eps[:, 0:1]))
        pr.dve.need(t)
        return pr.dve.did(pr.dve.e.reciprocal(r, r))

    def spread_rows(self, r, r_done, diag, out):
        pr = self.pr
        pe, dve, act = pr.pe, pr.dve, pr.act
        pe.need(self.free[2].now())
        used = [None, None]
        for t in range(TT):
            d = diag[t % 2]
            dve.need(r_done, used[t % 2])
            g = dve.did(dve.e.tensor_scalar(d, self.ident[:], r[:, t:t + 1], None, ALU.mult))
            pe.need(g)
            used[t % 2] = pe.did(pe.e.matmul(self.pair(2)[:, t * P:(t + 1) * P], self.ones[:], d,
                                             start=True, stop=True))
        act.need(used[0], used[1])
        return self.free[2].inc(act.e.activation(out, self.pair(2), ACT.Copy))

    def prepare(self, src, gain, UH, UL, sq):
        pr = self.pr
        act, dve, pe = pr.act, pr.dve, pr.pe
        used = [None, None]
        pe.need(self.free[3].now())
        for k in range(len(src)):
            q = sq[k % 2]
            act.need(used[k % 2])
            m = act.did(act.e.activation(q, src[k], ACT.Square))
            pe.need(m)
            used[k % 2] = self.token_sums(k, len(src), q)
            self.scaled_parts(UH[:, k, :], UL[:, k, :], src[k], gain[:, k:k + 1], None)
        return used[(len(src) - 1) % 2]

    def statistics(self, s, dim, out=None):
        r = self.token_rstd(self.rt[:], self.PS[:, 7, 0:TT], dim, (s,))
        if out is not None:
            self.rows_done = self.spread_rows(self.rt, r, [self.diag[:, 0:P], self.diag[:, P:2 * P]], out)
        return r

    def pair(self, p):
        return self.PS[:, 2 * p:2 * p + 2, :].rearrange("p a b -> p (a b)")

    def claim(self):
        p = self.turn % self.pairs
        self.turn += 1
        self.pr.pe.need(self.free[p].now())
        return p

    def product(self, index, UH, UL, ready=None, between=None):
        pr, st = self.pr, self.st
        s = st.take(index)
        p, last = self.channels(s, UH, UL, range(KT), lambda k: slice(k * P, (k + 1) * P), ready=ready,
                                between=between)
        done = st.give(s, last)
        if between:
            self.after_last()
        return p, done, s

    def first_products(self, src, gain, UH, UL, sq=None, after=None, rows=None):
        pr, st = self.pr, self.st
        act, dve, pe = pr.act, pr.dve, pr.pe
        ready = []
        for k in range(KT):
            t = after(k) if after else None
            ready.append(self.scaled_parts(UH[:, k, :], UL[:, k, :], src[k], 1.0 if gain is None else gain[:, k:k + 1],
                                           t))
        self.turn = 0
        first = self.product(st.g, UH, UL, ready=ready)
        if not sq:
            return [first, self.product(st.g, UH, UL)]
        used = [None, None]
        pe.need(self.free[3].now())

        def sums(k):
            q = sq[k % 2]
            if k % 2:
                dve.need(used[1])
                m = dve.did(dve.e.tensor_tensor(q, src[k], src[k], ALU.mult))
            else:
                act.need(used[0])
                m = act.did(act.e.activation(q, src[k], ACT.Square))
            pe.need(m)
            used[k % 2] = self.token_sums(k, KT, q)

        second = self.product(st.g, UH, UL, between=sums)
        self.statistics(used[1], D, rows)
        dve.need(self.rows_done)
        return [first, second]

    def channels(self, s, UH, UL, ks, cols, ready=None, between=None):
        p = self.claim()
        ks = list(ks)
        for n, k in enumerate(ks):
            if ready:
                self.pr.pe.need(ready[k])
            last = self.mm3([self.PS[:, 2 * p + h, :] for h in range(2)],
                            self.st.hi[s][:, cols(k)], self.st.lo[s][:, cols(k)],
                            [UH[:, k, h * HALF:(h + 1) * HALF] for h in range(2)],
                            [UL[:, k, h * HALF:(h + 1) * HALF] for h in range(2)],
                            n == 0, n == len(ks) - 1)
            if between:
                if n == len(ks) - 1:
                    self.after_last = lambda k=k: between(k)
                else:
                    between(k)
        return p, last

    def project(self, n, UH, UL, dst, rows, first=()):
        pr, st = self.pr, self.st

        def step(j, index, out=None):
            p, done, s = out or self.product(index, UH, UL)
            pr.dve.need(done)
            self.free[p].inc(pr.dve.e.tensor_tensor(dst(j), self.pair(p), rows, ALU.mult))
            st.split(s)

        for j, out in enumerate(first):
            step(j, None, out)
        begin = len(first)
        g0 = st.g
        rounds = (n - begin) // RING
        if rounds > 1:
            with pr.loop(rounds) as i:
                self.turn = 0
                for j in range(RING):
                    step(i * RING + (j + begin), i * RING + (g0 + j))
            st.g = g0 + rounds * RING
            begin += rounds * RING
            self.turn = 0
        for j in range(begin, n):
            step(j, st.g)

    def project_tokens(self, UH, UL, dst):
        pr, st = self.pr, self.st
        pr.pe.need(*[f.now() for f in self.free])
        for m in range(KT // 2):
            s = st.take(st.g)
            for t in range(TT):
                for j in range(2):
                    k = 2 * m + j
                    tok = slice(t * P, (t + 1) * P)
                    wh, wl = (w[s][:, j * 512:(j + 1) * 512] for w in (st.hi, st.lo))
                    first, last = k == 0, k == KT - 1
                    pr.pe.e.matmul(self.PS[:, t, :], UH[:, k, tok], wh, start=first, stop=False)
                    pr.pe.e.matmul(self.PS[:, t, :], UH[:, k, tok], wl, start=False, stop=False)
                    ins = pr.pe.e.matmul(self.PS[:, t, :], UL[:, k, tok], wh, start=False, stop=last)
            done = st.give(s, ins)
            st.split(s)
        pr.act.need(done)
        pr.dve.need(done)
        for t in range(TT):
            to = dst[:, :, t * P:(t + 1) * P]
            ps = self.PS[:, t, :].rearrange("p (k c) -> p k c", c=P)
            if t % 2:
                self.free[t // 2].inc(pr.dve.e.tensor_scalar(to, ps, self.rt[:, t:t + 1], None, ALU.mult))
            else:
                self.free[t // 2].inc(pr.act.e.activation(to, ps, ACT.Copy, scale=self.rt[:, t:t + 1]))

    def build(self, ctx):
        nc, pr, a = self.nc, self.pr, self.a
        self.n_dma = 0
        self.turn = 0
        self.pairs = 4
        sb = lambda n, s, dt=F32: self.sb(ctx, n, s, dt)
        self.PS = ctx.enter_context(nc.psum_tensor("PS", [P, 8, HALF], F32))
        self.free = [Count(pr, f"psum_free{p}") for p in range(4)]
        self.st = Stream(pr, a["weights"], sb)
        self.H = sb("H", [P, KT, T])
        self.ones = sb("ones", [P, P])
        self.eps = sb("eps", [P, 1])
        self.rt = sb("r_tokens", [P, TT])
        self.rt2 = sb("r_tokens2", [P, TT])
        self.sums = sb("token_sums", [P, TT])
        self.gout8 = sb("mixer2_out_gains", [P, KT])
        self.diag = sb("diag", [P, 2 * P])
        self.ident = sb("ident", [P, P])
        self.gains = sb("gains", [P, a["gains"].shape[1]])
        for p in range(4):
            self.free[p].inc(nc.vector.memset(self.pair(p), 0.0))
        first = self.sb(ctx, "first_marks", [P, 2])
        ready = [pr.dve.did(nc.vector.memset(self.ones[:], 1.0)),
                 pr.pool.did(nc.gpsimd.memset(first[:, 0:1], 0.0)),
                 pr.dve.did(nc.vector.memset(self.eps[:], EPS))]
        ready.append(self.dma(self.ident[:], a["ident"]))
        ready.append(self.dma(self.gains[:], a["gains"]))
        self.x_in = [self.dma(self.H[:, k, :], a["x_t"][k]) for k in range(KT)]
        self.st.start()
        for e in pr.engines:
            e.need(*ready)
        self.program(ctx)

    def g(self, name):
        at, n = self.at[name]
        return self.gains[:, at:at + n]

    def program(self, ctx):
        with ExitStack() as c:
            self.first_mixer(c)
        with ExitStack() as c:
            Y = self.sb(c, "Y", [P, KT, T])
            rows = self.sb(c, "Y_rows", [P, T])
            self.y_rows = rows[:]
            self.first_output(Y, rows)
            self.feed_forward(conv=False, Y=Y, add=self.adder(Y, self.g("attn_post_norm"), rows))
            self.ple(self.a["p_t"], norm=None, add=self.adder(Y, self.g("ffn_post_norm"), rows),
                     sg=[Y[:, k, :] for k in range(2)])
        self.second_mixer()
        self.feed_forward(conv=True)
        self.stored = Count(self.pr, "out_stored", 16)
        self.ple(self.a["p2_t"], norm="ple_norm_g_2", out=self.out_ap)
        self.pr.sp.need(self.stored.now())

    def operand(self, ctx, tag):
        return [self.sb(ctx, f"u_{x}_{tag}", [P, KT, T], F32R) for x in ("hi", "lo")]

    def first_mixer(self, ctx):
        pr, H = self.pr, self.H
        big = self.sb(ctx, "mixer1", [P, 12, T])
        rows = self.sb(ctx, "mixer1_rows", [P, T])
        with ExitStack() as c:
            UH, UL = self.operand(c, "1")
            first = self.first_products([H[:, k, :] for k in range(KT)], self.g("attn_pre_norm"), UH, UL,
                                        [big[:, 0, :], big[:, 1, :]], lambda k: self.x_in[k], rows[:])
            self.project(8, UH, UL, lambda j: H[:, j, :], rows[:], first)
            self.project_tokens(UH, UL, big[:, 0:4, :])
            self.project_tokens(UH, UL, big[:, 4:8, :])
            pr.meet(self.free)
            kept = self.nc.dram_tensor("stick_kept", (3 * PAIRS, P, T), F32).ap()
            with ExitStack() as h:
                back = self.hgrn(h, big, UH, UL, rows, kept)
            pr.meet(self.free)
        with ExitStack() as c:
            self.stick_breaking(c, big, back)
        pr.meet(self.free)

    def along(self, index, UH, UL, rows, stage, kept, at, stored):
        pr, st = self.pr, self.st
        pe, dve, sp = pr.pe, pr.dve, pr.sp
        for m in range(RING):
            s, p = st.take(index + m), 2 + m % 2
            pe.need(self.free[p].now())
            for k in range(KT):
                last = self.mm3([self.PS[:, 2 * p + h, :] for h in range(2)],
                                st.hi[s][:, k * P:(k + 1) * P], st.lo[s][:, k * P:(k + 1) * P],
                                [UH[:, k, h * HALF:(h + 1) * HALF] for h in range(2)],
                                [UL[:, k, h * HALF:(h + 1) * HALF] for h in range(2)], k == 0, k == KT - 1)
                if k == KT - 1:
                    done = st.give(s, last)
                yield
            dve.need(done, stored.now())
            t = self.free[p].inc(dve.e.tensor_tensor(stage[:], self.pair(p), rows[:], ALU.mult))
            sp.need(t)
            stored.inc(sp.e.dma_start(kept[at + m], stage[:]))
            st.split(s)
        yield

    def hgrn(self, ctx, big, UH, UL, rows, spill):
        pr, H, PS = self.pr, self.H, self.PS
        act, dve, pool, pe = pr.act, pr.dve, pr.pool, pr.pe
        e_t = [big[:, 8, :], big[:, 9, :]]
        x_t = [big[:, 10, :], big[:, 11, :]]
        kk = self.sb(ctx, "hg_k", [P, T])
        b = self.sb(ctx, "hg_b", [P, T])
        scores = self.sb(ctx, "hg_scores", [P, TT, P])
        last_decay = self.sb(ctx, "hg_last", [P, TT, 1])
        lb = self.sb(ctx, "hg_lb", [P, HGH, 1])
        olb = self.sb(ctx, "hg_olb", [P, HGH, 1])
        tmp = self.sb(ctx, "hg_tmp", [P, HGH])
        masks = self.sb(ctx, "hg_masks", [P, len(LEVELS) + 1, P], U8)
        m_in = self.dma(kk[:].rearrange("p (a b) -> p a b", b=P), self.a["levels"])
        g0, g1 = self.g("gamma0"), self.g("gamma1")
        lb2, olb2 = lb[:].rearrange("p a b -> p (a b)"), olb[:].rearrange("p a b -> p (a b)")
        t = dve.did(dve.e.tensor_tensor(tmp[:], g0, g1, ALU.max))
        dve.need(t)
        dve.did(dve.e.tensor_tensor(lb2, g0, tmp[:], ALU.subtract))
        t = dve.did(dve.e.tensor_tensor(olb2, g1, tmp[:], ALU.subtract))
        act.need(t)
        act.did(act.e.activation(lb2, lb2, ACT.Exp))
        t = act.did(act.e.activation(olb2, olb2, ACT.Exp))
        dve.need(t)
        t = dve.did(dve.e.tensor_tensor(tmp[:], lb2, olb2, ALU.add))
        dve.need(t)
        t = dve.did(dve.e.reciprocal(tmp[:], tmp[:]))
        dve.need(t)
        dve.did(dve.e.tensor_tensor(lb2, lb2, tmp[:], ALU.mult))
        dve.did(dve.e.tensor_tensor(olb2, olb2, tmp[:], ALU.mult))
        dve.did(dve.e.memset(scores[:], 0.0))
        dve.need(m_in)
        dve.did(dve.e.tensor_copy(masks[:], kk[:].rearrange("p (a b) -> p a b", b=P)))
        chunks = [slice(c * P, (c + 1) * P) for c in range(TT)]
        stage = self.sb(ctx, "stick_stage", [P, T])
        stored = Count(pr, "stick_stored", 16)
        stored.inc(pr.sp.e.dma_start(spill[0], big[:, 0, :]))
        g0 = self.st.g

        with pr.loop(HGH) as j:
            pr.meet(self.free + [stored])
            along = self.along(j * RING + g0, UH, UL, rows, stage, spill, j * RING, stored)

            def fill(n):
                for _ in range(n):
                    next(along, None)

            q, z, v = H[:, j, :], H[:, j + 4, :], lambda c: big[:, j + 4, chunks[c]]
            s1 = act.did(act.e.activation(e_t[0], z, ACT.Sigmoid))
            s2 = act.did(act.e.activation(e_t[1], z, ACT.Sigmoid, scale=-1.0))
            s = act.did(act.e.activation(x_t[0], q, ACT.Sigmoid))
            dve.need(s1, s2)
            f = dve.did(dve.e.tensor_scalar(z, e_t[0], olb[:, j, :], lb[:, j, :], ALU.mult, ALU.add))
            dve.need(f)
            f = dve.did(dve.e.tensor_scalar(z, z, 1e-19, None, ALU.max))
            k_done = dve.did(dve.e.tensor_scalar(kk[:], e_t[1], olb[:, j, :], None, ALU.mult))
            act.need(f)
            lf = act.did(act.e.activation(z, z, ACT.Ln))
            dve.need(s)
            q_done = dve.did(dve.e.tensor_tensor(q, q, x_t[0], ALU.mult))
            dve.need(lf)
            for ch in chunks:
                b_done = dve.did(dve.e.tensor_tensor_scan(
                    b[:, ch], H[:, j + 4, ch], H[:, j + 4, ch], 0.0, ALU.add, ALU.bypass))
            dve.need(b_done, q_done, k_done)
            pool.need(b_done, q_done, k_done)
            fill(KT)
            pe.need(k_done, q_done)

            def keep(level, ps_pair, prods, kept):
                dve.need(prods, kept)
                ps = self.pair(ps_pair).rearrange("p (a b) -> p a b", b=P)
                m = masks[:, level:level + 1, :].to_broadcast([P, TT, P])
                return dve.did(dve.e.copy_predicated(scores[:], m, ps))

            scaled = [None, None]
            read = [None, None]
            got = [None, None]
            exps = {}

            def exponents(n):
                h, w = LEVELS[n], n % 2
                blocks = lambda ap: ap.rearrange("p (n c) -> p n c", c=2 * h)
                bb, ee = blocks(b[:]), blocks(e_t[w])
                dve.need(scaled[w])
                e = dve.did(dve.e.tensor_tensor(
                    ee, bb, bb[:, :, h - 1:h].to_broadcast([P, T // (2 * h), 2 * h]), ALU.subtract))
                act.need(e)
                lo = act.did(act.e.activation(ee[:, :, :h], ee[:, :, :h], ACT.Exp, scale=-1.0))
                up = act.did(act.e.activation(ee[:, :, h:], ee[:, :, h:], ACT.Exp))
                exps[n] = lo, up

            exponents(0)
            kept = prods = None
            for n, h in enumerate(LEVELS):
                w = n % 2
                if n + 1 < len(LEVELS):
                    exponents(n + 1)
                blocks = lambda ap: ap.rearrange("p (n c) -> p n c", c=2 * h)
                ee, xx, qq, k3 = blocks(e_t[w]), blocks(x_t[w]), blocks(q), blocks(kk[:])
                lo, up = exps[n]
                pool.need(lo, read[w])
                xl = pool.did(pool.e.tensor_tensor(xx[:, :, :h], k3[:, :, :h], ee[:, :, :h], ALU.mult))
                dve.need(up, read[w])
                xu = dve.did(dve.e.tensor_tensor(xx[:, :, h:], qq[:, :, h:], ee[:, :, h:], ALU.mult))
                scaled[w] = [xl, xu]
                if n:
                    kept = got[1 - w] = keep(n - 1, 1 - w, prods, kept)
                pe.need(xl, xu, got[w])
                for ch in chunks:
                    mm = pe.e.matmul(self.pair(w)[:, ch], x_t[w][:, ch], x_t[w][:, ch], start=True, stop=True)
                prods = read[w] = pe.did(mm)
                fill(FILL[n])
            pe.need(got[1 - w])
            for ch in chunks:
                mm = pe.e.matmul(self.pair(1 - w)[:, ch], kk[:, ch], H[:, j, ch], start=True, stop=True)
            diagonal = pe.did(mm)
            for _ in along:
                pass
            b3, e3 = (t.rearrange("p (n c) -> p n c", c=P) for t in (b[:], e_t[1]))
            dve.need(scaled[1])
            e = dve.did(dve.e.tensor_tensor(e3, b3, b3[:, :, P - 1:P].to_broadcast([P, TT, P]), ALU.subtract))
            kept = got[w] = keep(len(LEVELS) - 1, w, prods, kept)
            act.need(e)
            ke = act.did(act.e.activation(e_t[1], e_t[1], ACT.Exp, scale=-1.0))
            act.need(scaled[0])
            qe = act.did(act.e.activation(e_t[0], b[:], ACT.Exp))
            gl = act.did(act.e.activation(last_decay[:], b3[:, :, P - 1:P], ACT.Exp))
            dve.need(ke, read[1])
            ke = dve.did(dve.e.tensor_tensor(x_t[1], kk[:], e_t[1], ALU.mult))
            pool.need(qe, read[0])
            qe = pool.did(pool.e.tensor_tensor(x_t[0], q, e_t[0], ALU.mult))
            kept = keep(len(LEVELS), 1 - w, diagonal, kept)
            pe.need(ke, kept)
            for ch in chunks:
                mm = pe.e.transpose(self.pair(0)[:, ch], x_t[1][:, ch], self.ident[:])
            mm = pe.did(mm)
            act.need(mm, gl, qe)
            kt = act.did(act.e.activation(b[:], self.pair(0), ACT.Copy))
            pe.need(self.free[2].now(), self.free[3].now())
            for c, ch in enumerate(chunks):
                pe.e.matmul(self.pair(2)[:, ch], scores[:, c, :], v(c),
                            start=c % 4 == 0, stop=False, skip_group_check=True)
            pe.need(kt)
            for c, ch in enumerate(chunks[:-1]):
                mm = pe.e.matmul(self.pair(3)[:, ch], b[:, ch], v(c), start=True, stop=True)
            upd = pe.did(mm)
            dve.need(upd, diagonal, ke, gl, scaled[0])
            st = dve.did(dve.e.tensor_copy(kk[:, chunks[0]], self.pair(3)[:, chunks[0]]))
            pe.need(qe)
            for c in range(1, TT):
                if c > 1:
                    dve.need(st)
                    st = dve.did(dve.e.scalar_tensor_tensor(
                        kk[:, chunks[c - 1]], kk[:, chunks[c - 2]], last_decay[:, c - 1, :],
                        self.pair(3)[:, chunks[c - 1]], ALU.mult, ALU.add))
                pe.need(st)
                mm = pe.e.matmul(self.pair(2)[:, chunks[c]], x_t[0][:, chunks[c]], kk[:, chunks[c - 1]],
                                 start=False, stop=c == TT - 1, skip_group_check=True)
            o = pe.did(mm)
            act.need(o, diagonal, qe)
            act.did(act.e.activation(H[:, j, :], self.pair(2), ACT.Copy))
        self.st.g = g0 + HGH * RING
        pr.meet(self.free + [stored])
        load = lambda m, pair: self.dma(big[:, m * PAIRS + pair, :], spill[pair * 3 + m])
        back = {}
        for pair in range(2):
            for m in (1, 2):
                back[m, pair] = load(m, pair)
        squares, silu = [kk, b], [scores[:].rearrange("p a b -> p (a b)"), stage[:]]
        s = None
        for t, tk in enumerate(chunks):
            tile = squares[t % 2][:, 0:HALF].rearrange("p (k c) -> p k c", c=P)
            act.need(s)
            s = act.did(act.e.activation(tile, H[:, 0:4, tk], ACT.Square, accum_out=self.sums[:, t:t + 1]))
        s = self.token_rstd(self.rt2[:], self.sums[:], HG, (s,))
        used = [None, None]
        for k in range(HGH):
            act.need(used[k % 2])
            gate = act.did(act.e.activation(silu[k % 2], big[:, k, :], ACT.Silu))
            dve.need(gate, s)
            for t, tk in enumerate(chunks):
                m = dve.did(dve.e.scalar_tensor_tensor(H[:, k, tk], H[:, k, tk], self.rt2[:, t:t + 1],
                                                       silu[k % 2][:, tk], ALU.mult, ALU.mult))
            used[k % 2] = m
            pr.sp.need(gate)
            back[0, k] = load(0, k)
            if k >= 2:
                back[1, k], back[2, k] = load(1, k), load(2, k)
        return back

    def attend(self, items, blocks, scores, before, after, v, evac, a_buf, at_buf, wide=P, side=()):
        pr, PS = self.pr, self.PS
        act, dve, pe = pr.act, pr.dve, pr.pe
        N, na, nt = len(items), len(a_buf), len(at_buf)
        bank = PS[:, 6, 0:wide]
        mid, ready, turned, copied, av, out = {}, {}, {}, {}, {}, {}
        side = iter(side)
        for step in range(N + 3):
            n = step
            if n < N:
                z = scores(n, items[n])
            n = step - 2
            if 0 <= n < N:
                pe.need(ready[n], copied.get(n - 1))
                for b in range(blocks(items[n])):
                    cols = slice(b * P, (b + 1) * P)
                    mm = pe.e.transpose(self.pair(2)[:, cols], a_buf[n % na][:, cols], self.ident[:])
                turned[n] = pe.did(mm)
            n = step - 3
            if 0 <= n < N:
                nb = blocks(items[n])
                pe.need(copied[n], out.get(n - 1))
                for b in range(nb):
                    mm = pe.e.matmul(bank, at_buf[n % nt][:, b * P:(b + 1) * P], v(items[n], b),
                                     start=b == 0, stop=b == nb - 1)
                av[n] = pe.did(mm)
            n = step - 1
            if 0 <= n < N:
                ready[n] = after(n, items[n], mid[n])
            n = step - 2
            if 0 <= n < N:
                cols = slice(0, blocks(items[n]) * P)
                act.need(turned[n], av.get(n - nt))
                copied[n] = act.did(act.e.activation(at_buf[n % nt][:, cols], self.pair(2)[:, cols], ACT.Copy))
            n = step
            if n < N:
                mid[n] = before(n, items[n], z, turned.get(n - na))
            n = step - 3
            if 0 <= n < N:
                out[n] = evac(n, items[n], bank, av[n])
            next(side, None)
        for _ in side:
            pass

    def banks_of(self, pair, cols):
        return [(self.PS[:, 2 * pair + h, 0:min(HALF, cols - h * HALF)], h * HALF, min(HALF, cols - h * HALF))
                for h in range(2) if cols > h * HALF]

    def score(self, pair, cols, qh, ql, kh, kl):
        for ps, c0, n in self.banks_of(pair, cols):
            mm = self.mm3([ps], qh, ql, [kh[:, c0:c0 + n]], [kl[:, c0:c0 + n]], True, True)
        return self.pr.pe.did(mm)

    def bias_lines(self, table, spread, buckets, rows):
        pr, PS = self.pr, self.PS
        act, dve, pe = pr.act, pr.dve, pr.pe
        rest = BIAS_LEN - T
        bucket0, bucket1 = buckets[0][0:NBUCKET, :], buckets[1][0:NBUCKET, 0:rest]
        ins = [self.dma(table, self.a["rel_bias"]), self.dma(bucket0, self.a["bucket"][:, 0:T]),
               self.dma(bucket1, self.a["bucket"][:, T:BIAS_LEN])]
        self.lines = self.nc.dram_tensor("bias_lines", (DIFF_H, P, BIAS_LEN), F32)
        to = self.lines.ap()
        pe.need(*ins)
        dve.need(*ins)
        wrote = []
        for h in range(DIFF_H):
            dve.need(pe.count.now())
            t = dve.did(dve.e.tensor_scalar(spread, self.ones[0:NBUCKET, :], table[:, h:h + 1], None, ALU.mult))
            pe.need(t, act.count.now())
            pe.e.matmul(PS[:, 2, :], spread, bucket0[:, 0:HALF], start=True, stop=True)
            pe.e.matmul(PS[:, 3, :], spread, bucket0[:, HALF:T], start=True, stop=True)
            t = pe.did(pe.e.matmul(PS[:, 4, 0:rest], spread, bucket1, start=True, stop=True))
            w = rows[h % 2]
            act.need(t, wrote[h - 2] if h > 1 else None)
            act.did(act.e.activation(w[0], self.pair(1), ACT.Copy))
            t = act.did(act.e.activation(w[1][:, 0:rest], PS[:, 4, 0:rest], ACT.Copy))
            pr.sp.need(t)
            wrote.append([self.dma(to[h, :, 0:T], w[0]), self.dma(to[h, :, T:BIAS_LEN], w[1][:, 0:rest])])
        return [pe.count.now(), act.count.now(), *ins, *wrote]

    def stick_breaking(self, ctx, big, back):
        pr, H, PS = self.pr, self.H, self.PS
        act, dve, pool, pe = pr.act, pr.dve, pr.pool, pr.pe
        sb = lambda n, s, dt=F32: self.sb(ctx, n, s, dt)
        parts = [[sb(f"sb_{n}{s}", [P, T], F32R) for n in ("qh", "ql", "kh", "kl")] for s in range(2)]
        om = [sb(f"sb_om{i}", [P, T]) for i in range(2)]
        be = [sb(f"sb_beta{i}", [P, T]) for i in range(4)]
        rem = [sb(f"sb_rem{i}", [P, T + 1]) for i in range(2)]
        at_buf = [sb(f"sb_at{i}", [P, T]) for i in range(2)]
        v_in = sb("sb_v_in", [P, T])
        strict, loose = sb("sb_strict", [P, P]), sb("sb_loose", [P, P])
        dve.need(self.dma(strict[:], self.a["strict"]))
        dve.did(dve.e.tensor_scalar(loose[:], strict[:], -1.0, 1.0, ALU.mult, ALU.add))
        table, spread = sb("df_table", [NBUCKET, DIFF_H]), sb("df_spread", [NBUCKET, P])
        lines_done = self.bias_lines(table[:], spread[:], [om[0][:], om[1][:]],
                                     [[be[0][:], be[1][:]], [be[2][:], be[3][:]]])
        scale = SB_DH ** -0.5
        ready, scored = {}, {}

        def prepare(pair, s):
            v = big[:, pair + 8, :]
            qh, ql, kh, kl = parts[s]
            free = scored.get(s)
            q = self.split_to(qh[:], ql[:], big[:, pair, :], after=(free,))
            yield
            k = self.split_to(kh[:], kl[:], big[:, pair + 4, :], after=(free,))
            dve.need(turned[1])
            c = dve.did(dve.e.tensor_copy(v_in[:], v))
            yield
            for half in range(2):
                cols = slice(half * HALF, (half + 1) * HALF)
                pe.need(turned[0], c)
                for t in range(4):
                    mm = pe.e.transpose(PS[:, 7, t * P:(t + 1) * P],
                                        v_in[:, (4 * half + t) * P:(4 * half + t + 1) * P], self.ident[:])
                turned[1] = pe.did(mm)
                act.need(turned[1])
                turned[0] = act.did(act.e.activation(v[:, cols], PS[:, 7, :], ACT.Copy))
                yield
            ready[s] = [*q, *k, turned[0]]

        turned = [None, None]
        for e in (pe, act, dve):
            e.need(*[back[m, 0] for m in range(3)])
        for _ in prepare(0, 0):
            pass
        for e in (pe, act, dve):
            e.need(*back.values())
        act.need(*lines_done)
        with pr.loop(PAIRS // 2) as i:
            pr.meet()
            ready.clear()
            scored.clear()
            turned[:] = [None, None]
            items = [(s, hh, t) for s in range(2) for hh in range(2) for t in range(TT)]
            read, scanned, weighed = {}, {}, {}

            def side():
                yield from prepare(i * 2 + 1, 1)
                for _ in range(2 * TT):
                    yield
                yield from prepare(2 - i * 2, 0)

            def scores(n, item):
                s, hh, t = item
                qh, ql, kh, kl = parts[s]
                rows = slice(hh * SB_DH, (hh + 1) * SB_DH)
                pe.need(read.get(n - 2), ready.get(s))
                tk = slice(t * P, (t + 1) * P)
                scored[s] = self.score(n % 2, (t + 1) * P, qh[rows, tk], ql[rows, tk], kh[rows, :], kl[rows, :])
                return scored[s]

            def before(n, item, z, free):
                w, cols = n % 2, (item[2] + 1) * P
                bt = be[n % 4]
                diag = slice(cols - P, cols)
                ps = self.pair(w)[:, 0:cols]
                act.need(z, scanned.get(n - 2), free)
                o = act.did(act.e.activation(om[w][:, 0:cols], ps, ACT.Sigmoid, scale=-scale))
                b = read[n] = act.did(act.e.activation(bt[:, 0:cols], ps, ACT.Sigmoid, scale=scale))
                pool.need(o, weighed.get(n - 2))
                o = pool.did(pool.e.tensor_tensor(om[w][:, diag], om[w][:, diag], strict[:], ALU.mult))
                pool.need(b, o)
                pool.did(pool.e.tensor_tensor(om[w][:, diag], om[w][:, diag], loose[:], ALU.add))
                pool.did(pool.e.tensor_tensor(bt[:, diag], bt[:, diag], strict[:], ALU.mult))
                return pool.did(pool.e.memset(rem[w][:, cols:cols + 1], 1.0))

            def after(n, item, masked):
                w, cols = n % 2, (item[2] + 1) * P
                bt = be[n % 4]
                dve.need(masked, weighed.get(n - 2))
                back = lambda ap: ap[:, 0:cols][:, ::-1]
                r = scanned[n] = dve.did(dve.e.tensor_tensor_scan(
                    back(rem[w]), back(om[w]), back(om[w]), 1.0, ALU.mult, ALU.bypass))
                e = pool if n % 3 == 0 else dve
                e.need(r, masked)
                weighed[n] = e.did(e.e.tensor_tensor(
                    bt[:, 0:cols], bt[:, 0:cols], rem[w][:, 1:cols + 1], ALU.mult))
                return weighed[n]

            def v(item, b):
                s, hh, _ = item
                return big[:, i * 2 + (8 + s), b * P + hh * SB_DH:b * P + (hh + 1) * SB_DH]

            def evac(n, item, bank, done):
                s, hh, t = item
                dve.need(done)
                return dve.did(dve.e.tensor_copy(H[:, i * 2 + (4 + s), t * P + hh * SB_DH:t * P + (hh + 1) * SB_DH], bank))

            self.attend(items, lambda it: it[2] + 1, scores, before, after, v, evac, be, at_buf, wide=SB_DH,
                        side=side())

    def first_output(self, Y, rows):
        pr, H = self.pr, self.H
        act, dve, pool = pr.act, pr.dve, pr.pool
        with ExitStack() as c:
            UH, UL = self.operand(c, "o1")
            s0, s1 = (self.sb(c, f"o1_t{k}", [P, T]) for k in range(2))
            for t in range(TT):
                tk = slice(t * P, (t + 1) * P)
                act.need(act.count.now())
                s = act.did(act.e.activation(s0[:, 0:HALF].rearrange("p (k c) -> p k c", c=P), H[:, 4:8, tk],
                                             ACT.Square, accum_out=self.sums[:, t:t + 1]))
            r = self.token_rstd(self.rt[:], self.sums[:], HG, (s,))
            dve.need(r)
            scaled = []
            for k in range(4, 8):
                for t in range(TT):
                    tk = slice(t * P, (t + 1) * P)
                    m = dve.did(dve.e.tensor_scalar(H[:, k, tk], H[:, k, tk], self.rt[:, t:t + 1], None, ALU.mult))
                scaled.append(m)
            self.to_channels([H[:, k, :] for k in range(KT)], self.g("hg_sb_out_norm"), UH, UL,
                             [None] * 4 + scaled)
            pr.meet(self.free)
            x_in = [self.dma(H[:, k, :], self.a["x_t"][k]) for k in range(KT)]
            pool.did(pool.e.memset(s1[:], 0.0))
            st, g0 = self.st, self.st.g

            def step(j, index):
                p, done, s = self.product(index, UH, UL)
                act.need(done, pool.count.now())
                act.did(act.e.activation(Y[:, j, :], self.pair(p), ACT.Copy))
                q = self.free[p].inc(act.e.activation(s0[:], self.pair(p), ACT.Square))
                pool.need(q, pool.count.now())
                pool.did(pool.e.tensor_tensor(s1[:], s1[:], s0[:], ALU.add))
                st.split(s)

            self.turn = 0
            for j in range(2):
                step(j, g0 + j)
            g0 = st.g
            with pr.loop(2) as i:
                self.turn = 0
                for j in range(RING):
                    step(i * RING + (j + 2), i * RING + (g0 + j))
            st.g = g0 + 2 * RING
            pr.meet(self.free)
            for e in pr.compute:
                e.need(*x_in)
            self.statistics(self.token_sums(0, 1, s1[:]), D, rows[:])

    def to_channels(self, slots, gain, UH, UL, after):
        pr = self.pr
        act, dve, pe = pr.act, pr.dve, pr.pe
        for k, src in enumerate(slots):
            p = self.claim()
            pe.need(after[k])
            for t in range(TT):
                tk = slice(t * P, (t + 1) * P)
                mm = pe.e.transpose(self.pair(p)[:, tk], src[:, tk], self.ident[:])
            mm = pe.did(mm)
            self.scaled_parts(UH[:, k, :], UL[:, k, :], self.pair(p), 1.0 if gain is None else gain[:, k:k + 1],
                              mm, self.free[p])

    def scaled_parts(self, hi, lo, src, gain, after, free=None):
        pr = self.pr
        act, dve = pr.act, pr.dve
        act.need(after)
        h = act.did(act.e.activation(hi, src, ACT.Copy, scale=gain))
        dve.need(h, after)
        i = dve.e.scalar_tensor_tensor(lo, src, gain, hi.bitcast(F32), ALU.mult, ALU.subtract)
        return [h, free.inc(i) if free else dve.did(i)]

    def adder(self, Y, gain, rows):
        pr, H = self.pr, self.H
        dve, pool = pr.dve, pr.pool
        scaled = {}

        def scale(k):
            if k < KT:
                dve.need(self.rows_done)
                scaled[k] = dve.did(dve.e.scalar_tensor_tensor(Y[:, k, :], Y[:, k, :], gain[:, k:k + 1], rows[:],
                                                               ALU.mult, ALU.mult))

        def add(k):
            if k == 0:
                scale(0)
            scale(k + 1)
            e = dve if k % 2 else pool
            e.need(scaled[k])
            return e.did(e.e.tensor_tensor(H[:, k, :], H[:, k, :], Y[:, k, :], ALU.add))

        return add

    def feed_forward(self, conv, Y=None, add=None):
        pr, H, st, PS = self.pr, self.H, self.st, self.PS
        act, dve, pool, pe = pr.act, pr.dve, pr.pool, pr.pe
        tag = "f2" if conv else "f1"
        with ExitStack() as c:
            UH, UL = self.operand(c, tag)
            AH, AL = (self.sb(c, f"{tag}_a{x}", [P, 2, T], F32R) for x in "hl")
            sg = self.sb(c, f"{tag}_gate", [P, T])
            prod = self.sb(c, f"{tag}_prod", [P, T])
            rows = self.sb(c, f"{tag}_rows", [P, T])
            Y = H if Y is None else Y
            cw = self.sb(c, f"{tag}_cw", [P, 4]) if conv else None
            cg = self.sb(c, f"{tag}_conv_in", [P, T]) if conv else None
            first = self.first_products([H[:, k, :] for k in range(KT)],
                                        self.g("ffn_norm_g_2" if conv else "ffn_pre_norm"), UH, UL,
                                        [sg[:], prod[:]], add, rows[:])
            if not conv:
                for k in range(KT):
                    pool.need(dve.count.now(), pool.count.now())
                    pool.did(pool.e.memset(Y[:, k, :], 0.0))

            def gate(index, tile, out=None):
                p, done, s = out or self.product(index, UH, UL)
                if conv:
                    dve.need(act.count.now(), dve.count.now())
                    w = dve.did(dve.e.tensor_copy(cw[:], self.gains[:, bass.ds(tile * 4 + self.at["conv"][0], 4)]))
                    dve.need(done)
                    g = self.free[p].inc(dve.e.tensor_tensor(cg[:], self.pair(p), rows[:], ALU.mult))
                    act.need(g, w)
                    g = act.did(act.e.activation(sg[:], cg[:], ACT.Identity, scale=cw[:, 2:3], bias=cw[:, 3:4]))
                    for d, col in ((1, 1), (2, 0)):
                        dve.need(g)
                        g = dve.did(dve.e.scalar_tensor_tensor(
                            sg[:, d:], cg[:, :T - d], cw[:, col:col + 1], sg[:, d:], ALU.mult, ALU.add))
                else:
                    dve.need(done, dve.count.now(), act.count.now())
                    g = self.free[p].inc(dve.e.tensor_tensor(sg[:], self.pair(p), rows[:], ALU.mult))
                act.need(g)
                g = act.did(act.e.activation(sg[:], sg[:], ACT.Silu))
                st.split(s)
                return g

            def up(index, j, g, out=None):
                p, done, s = out or self.product(index, UH, UL)
                dve.need(done, act.count.now(), dve.count.now())
                m = self.free[p].inc(dve.e.tensor_tensor(prod[:], self.pair(p), rows[:], ALU.mult))
                dve.need(g, m)
                m = dve.did(dve.e.tensor_tensor(prod[:], prod[:], sg[:], ALU.mult))
                self.split_to(AH[:, j, :], AL[:, j, :], prod[:], after=(m, done))
                st.split(s)

            def down(index, last=False):
                s0, s1 = st.take(index), st.take(index + 1)
                pe.need(*self.a_ready)
                for n in range(KT):
                    p = self.claim()
                    for k, s in enumerate((s0, s1)):
                        mm = self.mm3([PS[:, 2 * p + h, :] for h in range(2)],
                                      st.hi[s][:, n * P:(n + 1) * P], st.lo[s][:, n * P:(n + 1) * P],
                                      [AH[:, k, h * HALF:(h + 1) * HALF] for h in range(2)],
                                      [AL[:, k, h * HALF:(h + 1) * HALF] for h in range(2)], k == 0, k == 1)
                        if n == KT - 1:
                            done = st.give(s, mm)
                        else:
                            done = pe.did(mm) if k else None
                    dve.need(done, self.free[p].now())
                    y = self.free[p].inc(dve.e.tensor_tensor(Y[:, n, :], Y[:, n, :], self.pair(p), ALU.add))
                    if last and not conv:
                        q = [sg, prod][n % 2][:]
                        act.need(y, squared[n % 2], dve.count.now())
                        q_done = act.did(act.e.activation(q, Y[:, n, :], ACT.Square))
                        if n:
                            pe.need(waiting[0])
                            squared[1 - n % 2] = self.token_sums(n - 1, KT, waiting[1])
                        waiting[:] = [q_done, q]
                if last and not conv:
                    pe.need(waiting[0])
                    self.statistics(self.token_sums(KT - 1, KT, waiting[1]), D, self.y_rows)
                st.split(s0)
                st.split(s1)

            squared, waiting = [None, None], []
            g = gate(None, 0, first[0])
            up(None, 0, g, first[1])
            g = gate(st.g, 1)
            up(st.g, 1, g)
            base = st.g
            pr.meet(self.free)
            with pr.loop(FF_TILES // 2 - 1) as i:
                self.turn = 0
                at = i * 6
                self.a_ready = [act.count.now(), dve.count.now()]
                g = gate(at + base, i * 2 + 2)
                down(at + (base + 1))
                up(at + (base + 3), 0, g)
                g = gate(at + (base + 4), i * 2 + 3)
                up(at + (base + 5), 1, g)
            st.g = base + 6 * (FF_TILES // 2 - 1)
            self.turn = 1
            self.a_ready = [act.count.now(), dve.count.now()]
            self.pairs = 3
            down(st.g, last=True)
            self.pairs = 4
            pr.meet(self.free)

    def ple(self, p_dram, norm, add=None, sg=None, out=None):
        pr, H, st = self.pr, self.H, self.st
        act, dve, pool, pe = pr.act, pr.dve, pr.pool, pr.pe
        tag = "p2" if norm else "p1"
        with ExitStack() as c:
            UH, UL = self.operand(c, tag)
            PP = self.sb(c, f"{tag}_pp", [P, KT, T])
            sg = sg or [self.sb(c, f"{tag}_s{i}", [P, T])[:] for i in range(2)]
            rows = self.sb(c, f"{tag}_rows", [P, T]) if norm else None
            raw = [self.dma(PP[:, k, :], p_dram[k]) for k in range(2)]
            ready = [list(self.split_to(UH[:, 6 + k, :], UL[:, 6 + k, :], PP[:, k, :], after=(raw[k],)))
                     for k in range(2)]
            pe.need(*ready)
            act.need(*ready)
            self.turn = 0
            for half in range(2):
                s = st.take(st.g)
                for n in range(4):
                    p, mm = self.channels(s, UH[:, 6:8, :], UL[:, 6:8, :], range(2),
                                          lambda k: slice((2 * n + k) * P, (2 * n + k + 1) * P))
                    done = st.give(s, mm) if n == 3 else pe.did(mm)
                    act.need(done)
                    self.free[p].inc(act.e.activation(PP[:, 4 * half + n, :], self.pair(p), ACT.Copy))
                st.split(s)
            for e in (act, dve):
                e.need(done)
            first = self.first_products([H[:, k, :] for k in range(KT)], self.g(norm) if norm else None, UH, UL,
                                        [sg[0], sg[1]] if norm else None, add, rows[:] if norm else None)

            def step(j, w, index, product=None):
                p, done, s = product or self.product(index, UH, UL)
                t = sg[w]
                if norm:
                    dve.need(done, act.count.now(), dve.count.now())
                    m = self.free[p].inc(dve.e.tensor_tensor(t, self.pair(p), rows[:], ALU.mult))
                    act.need(m)
                    g = act.did(act.e.activation(t, t, ACT.Sigmoid))
                else:
                    act.need(done, dve.count.now())
                    g = self.free[p].inc(act.e.activation(t, self.pair(p), ACT.Sigmoid))
                dve.need(g)
                m = dve.did(dve.e.tensor_tensor(t, t, PP[:, j, :], ALU.mult))
                dve.need(m)
                done = dve.did(dve.e.tensor_tensor(H[:, j, :], H[:, j, :], t, ALU.add))
                if out is not None:
                    pr.sp.need(done)
                    self.stored.inc(pr.sp.e.dma_start(out[j], H[:, j, :]))
                st.split(s)

            for j in range(2):
                step(j, j, None, first[j])
            g0 = st.g
            with pr.loop(2) as i:
                self.turn = 0
                for j in range(RING):
                    step(i * RING + (j + 2), j % 2, i * RING + (g0 + j))
            st.g = g0 + 2 * RING
            pr.meet(self.free)

    def second_mixer(self):
        pr, H = self.pr, self.H
        with ExitStack() as c:
            res = self.sb(c, "mixer2", [P, 16, T])
            with ExitStack() as cu:
                UH, UL = self.operand(cu, "2")
                rows = self.sb(cu, "mixer2_rows", [P, T])
                kept = self.nc.dram_tensor("h_kept", (KT, P, T), F32)
                self.h_kept = [self.dma(kept.ap()[k], H[:, k, :]) for k in range(KT)]
                first = self.first_products([H[:, k, :] for k in range(KT)], self.g("attn_norm_g_2"), UH, UL,
                                            [res[:, 0, :], res[:, 1, :]], rows=rows[:])
                self.project(4, UH, UL, lambda j: res[:, j + 12, :], rows[:], first)
                for first in (0, 4, 8):
                    self.project_tokens(UH, UL, res[:, first:first + 4, :])
                pr.meet(self.free)
            for e in pr.engines:
                e.need(*self.h_kept)
            with ExitStack() as cd:
                self.differential(cd, res)
            pr.meet(self.free)
            with ExitStack() as cm:
                self.mla(cm, res)
            pr.meet(self.free)
            h_back = [self.dma(H[:, k, :], kept.ap()[k]) for k in range(KT)]
            with ExitStack() as co:
                self.second_output(co, res, h_back)
            pr.meet(self.free)

    def second_output(self, ctx, res, h_back):
        pr, H, st = self.pr, self.H, self.st
        dve = pr.dve
        UH, UL = self.operand(ctx, "o2")
        self.turn = 0
        self.to_channels([res[:, k, :] for k in range(KT)], self.gout8, UH, UL, [None] * KT)
        pr.meet(self.free)
        dve.need(*h_back)
        g0 = st.g

        def step(j, index):
            p, done, s = self.product(index, UH, UL)
            dve.need(done)
            self.free[p].inc(dve.e.tensor_tensor(H[:, j, :], H[:, j, :], self.pair(p), ALU.add))
            st.split(s)

        with pr.loop(2) as i:
            self.turn = 0
            for j in range(RING):
                step(i * RING + j, i * RING + (g0 + j))
        st.g = g0 + 2 * RING
        self.turn = 0
        for j in range(2 * RING, KT):
            step(j, g0 + j)

    def head_parts(self, src, d, hi, lo, gain, after, free):
        pr, bank = self.pr, self.PS[0:d, 7, :]
        pe = pr.pe
        pr.act.need(free)
        pr.dve.need(free)
        for half in range(2):
            pe.need(after, self.bank7)
            for t in range(4):
                x = src[:, (4 * half + t) * d:(4 * half + t + 1) * d]
                mm = pe.e.transpose(bank[:, t * P:(t + 1) * P], x, self.ident[:])
            mm = self.turned = pe.did(mm)
            cols = slice(half * HALF, (half + 1) * HALF)
            self.bank7 = self.scaled_parts(hi[:, cols], lo[:, cols], bank, gain, mm)
            yield
        return self.bank7

    def differential(self, ctx, res):
        pr, PS = self.pr, self.PS
        act, dve, pool, pe = pr.act, pr.dve, pr.pool, pr.pe
        sb = lambda n, s, dt=F32: self.sb(ctx, n, s, dt)
        sets = [[sb(f"df_{n}{s}", [P, T], F32R) for n in ("qh", "ql", "kh", "kl")] for s in range(2)]
        toep = [sb(f"df_bias{s}", [P, T]) for s in range(2)]
        pm = [self.H[:, k, :] for k in range(6)]
        staged = [self.H[:, 6, :], self.H[:, 7, :]]
        squares = sb("df_squares", [P, T])[:]
        at_buf = [sb(f"df_at{i}", [P, T]) for i in range(2)]
        small = sb("df_small", [P, 4, 8])
        norms = sb("df_norms", [P, 2, 2 * TT])
        out_norm = sb("df_out_norm", [P, TT])
        gq, lam2, nlam = sb("df_gq", [P, 1]), sb("df_lam2", [P, 2]), sb("df_nlam", [P, 1])
        scale = 64 ** -0.5
        dve.did(dve.e.tensor_scalar(gq[:], self.g("diff_q_norm_g_2"), scale, None, ALU.mult))
        dve.did(dve.e.memset(self.gout8[:], 1.0))
        dve.need(dve.count.now())
        dve.did(dve.e.tensor_scalar(self.gout8[:, 0:DIFF_H], self.g("diff_out_norm_g_2").to_broadcast([P, DIFF_H]),
                                    1.0 - LAM_INIT, None, ALU.mult))
        for n in range(2):
            dve.did(dve.e.tensor_tensor(lam2[:, n:n + 1], self.g(f"lambda_q{n + 1}_2"), self.g(f"lambda_k{n + 1}_2"),
                                        ALU.mult))
        pe.need(dve.count.now())
        t = pe.did(pe.e.matmul(PS[:, 0, 0:2], self.ones[:], lam2[:], start=True, stop=True))
        act.need(t)
        t = act.did(act.e.activation(lam2[:], PS[:, 0, 0:2], ACT.Exp))
        dve.need(t)
        t = dve.did(dve.e.tensor_tensor(nlam[:], lam2[:, 1:2], lam2[:, 0:1], ALU.subtract))
        dve.need(t)
        dve.did(dve.e.tensor_scalar(nlam[:], nlam[:], -LAM_INIT, None, ALU.add))
        lines = self.lines
        bias_in = [Count(pr, f"df_bias_in{s}", 16) for s in range(2)]
        toeplitz = bass.AP(lines, P - 1, [[P * BIAS_LEN, DIFF_H], [BIAS_LEN - 1, P], [1, T]])

        ready, scored, biased = {}, {}, {}
        groups = lambda ap: ap.rearrange("p (g c) -> p g c", c=64)
        self.bank7 = self.turned = None

        def prepare(h, s):
            src = [res[:, h, :], res[:, h + 4, :]]
            act.need(self.turned, dve.count.now())
            sq = [act.did(act.e.activation(staged[n], src[n], ACT.Square)) for n in range(2)]
            for n in range(2):
                dve.need(sq[n], dve.count.now())
                t = dve.did(dve.e.tensor_reduce(norms[:, n, :], groups(staged[n]), AX.X, ALU.add))
            yield
            r = self.token_rstd(norms[:], norms[:], 64, (t,))
            dve.need(r)
            scaled = []
            for n in range(2):
                rb = norms[:, n, :].unsqueeze(2).to_broadcast([P, 2 * TT, 64])
                scaled.append(dve.did(dve.e.tensor_tensor(groups(staged[n]), groups(src[n]), rb, ALU.mult)))
                yield
            qh, ql, kh, kl = sets[s]
            free = scored.get(s)
            q = yield from self.head_parts(staged[0], P, qh, ql, gq[:], scaled[0], free)
            k = yield from self.head_parts(staged[1], P, kh, kl, self.g("diff_k_norm_g_2"), scaled[1], free)
            ready[s] = [*scaled, *q, *k]

        def load_bias(h, s):
            pr.sp.need(biased.get(s))
            bias_in[s].inc(pr.sp.e.dma_start(toep[s][:], toeplitz[h]))

        def out_normed(h, done):
            act.need(done, dve.count.now())
            t = act.did(act.e.activation(squares, res[:, h, :], ACT.Square))
            yield
            dve.need(t, dve.count.now())
            t = dve.did(dve.e.tensor_reduce(out_norm[:], squares.rearrange("p (g c) -> p g c", c=P),
                                            AX.X, ALU.add))
            r = self.token_rstd(out_norm[:], out_norm[:], P, (t,))
            yield
            dve.need(r)
            o3 = res[:, h, :].rearrange("p (g c) -> p g c", c=P)
            dve.did(dve.e.tensor_tensor(o3, o3, out_norm[:].unsqueeze(2).to_broadcast([P, TT, P]), ALU.mult))

        load_bias(0, 0)
        load_bias(1, 1)
        for _ in prepare(0, 0):
            pass
        with pr.loop(DIFF_H // 2) as i:
            pr.meet(self.free + bias_in)
            ready.clear()
            scored.clear()
            biased.clear()
            self.bank7 = self.turned = None
            read, weights, put = {}, {}, {}
            items = [(0, t) for t in range(TT)] + [(1, t) for t in reversed(range(TT))]

            def side():
                yield from prepare(i * 2 + 1, 1)
                for _ in range(TT - 7):
                    yield
                load_bias(2 - i * 2, 0)
                yield from prepare(2 - i * 2, 0)
                yield from out_normed(i * 2, put[0])

            def scores(n, item):
                s, t = item
                qh, ql, kh, kl = sets[s]
                out = []
                pe.need(ready.get(s))
                for m in range(2):
                    rows, tk = slice(64 * m, 64 * m + 64), slice(t * P, (t + 1) * P)
                    pe.need(read.get((n - 1, m)))
                    out.append(self.score(m, (t + 1) * P, qh[rows, tk], ql[rows, tk], kh[rows, :], kl[rows, :]))
                scored[s] = out[1]
                return out

            def before(n, item, z, free):
                head, t = item
                cols, w, s = (t + 1) * P, n % 3, n % 4
                dve.need(ready.get(head))
                ls = []
                for m in range(2):
                    pb = pm[2 * w + m]
                    ps = self.pair(m)
                    dve.need(z[m], free, weights.get(n - 3))
                    t0 = dve.did(dve.e.memset(ps[0:64, cols - 64:cols], -1e30))
                    dve.need(t0)
                    t1 = read[(n, m)] = dve.did(dve.e.tensor_tensor(
                        pb[:, 0:cols], ps[:, 0:cols], toep[head][:, (TT - 1 - t) * P:T], ALU.add))
                    biased[head] = t1
                    dve.need(t1)
                    t2 = dve.did(dve.e.tensor_reduce(small[:, s, m:m + 1], pb[:, 0:cols], AX.X, ALU.max,
                                                     negate=True))
                    act.need(t2)
                    ls.append(act.did(act.e.activation(pb[:, 0:cols], pb[:, 0:cols], ACT.Exp,
                                                       bias=small[:, s, m:m + 1],
                                                       accum_out=small[:, s, 2 + m:3 + m])))
                return ls

            def after(n, item, ls):
                t = item[1]
                cols, w, s = (t + 1) * P, n % 3, n % 4
                p0, p1 = pm[2 * w], pm[2 * w + 1]
                dve.need(*ls)
                t3 = dve.did(dve.e.reciprocal(small[:, s, 4:6], small[:, s, 2:4]))
                dve.need(t3)
                t4 = dve.did(dve.e.tensor_scalar(small[:, s, 6:7], small[:, s, 5:6], nlam[:], small[:, s, 2:3],
                                                 ALU.mult, ALU.mult))
                dve.need(t4)
                weights[n] = dve.did(dve.e.scalar_tensor_tensor(
                    p0[:, 0:cols], p1[:, 0:cols], small[:, s, 6:7], p0[:, 0:cols], ALU.mult, ALU.add))
                return weights[n]

            def evac(n, item, bank, done):
                head, t = item
                dve.need(done)
                put[head] = dve.did(dve.e.tensor_scalar(res[:, i * 2 + head, t * P:(t + 1) * P], bank, small[:, n % 4, 4:5], None,
                                                   ALU.mult))
                return put[head]

            self.attend(items, lambda it: it[1] + 1, scores, before, after,
                        lambda it, b: res[:, i * 2 + (8 + it[0]), b * P:(b + 1) * P], evac,
                        [pm[0], pm[2], pm[4]], at_buf, side=side())
            load_bias(3 - i * 2, 1)
            for _ in out_normed(i * 2 + 1, put[1]):
                pass
        pr.meet(self.free + bias_in)

    def mla(self, ctx, res):
        pr, PS, st = self.pr, self.PS, self.st
        act, dve, pool, pe = pr.act, pr.dve, pr.pool, pr.pe
        sb = lambda n, s, dt=F32: self.sb(ctx, n, s, dt)
        W = TT * MLA_QK
        HALF_R = MLA_ROPE // 2
        V = res[:, 8:12, :]
        qt = sb("mla_q", [P, MLA_H, W])
        kt = res[:, 12:16, :].rearrange("p s (a c) -> p (s a) c", a=2)
        kr = sb("mla_kr", [P, TT, MLA_ROPE])
        krope_sq = sb("mla_kr_sq", [P, TT])
        rope = sb("mla_rope", [P, 2, TT, HALF_R])
        rg = sb("mla_rope_gain", [P, 2, MLA_ROPE])
        ngain = sb("mla_nope_gain", [P, 2])
        small = sb("mla_small", [P, 4, 4])
        norms = sb("mla_norms", [P, 2, TT])
        rt = sb("mla_latent_r", [P, 2, TT])
        tmp = sb("mla_tmp", [P, 2, TT, MLA_ROPE])
        ins = [self.dma(rope[:].rearrange("p a b c -> p (a b c)"), self.a["rope"]),
               self.dma(rg[:].rearrange("p a b -> p (a b)"), self.a["rope_gain"].partition_broadcast(P))]
        for e in (act, dve, pool):
            e.need(*ins)
        dve.did(dve.e.memset(ngain[:], 1.0))
        dve.need(dve.count.now())
        dve.did(dve.e.tensor_copy(ngain[0:MLA_NOPE, 0:1], self.g("mla_q_norm_g_2")[0:MLA_NOPE]))
        dve.need(dve.count.now())
        dve.did(dve.e.tensor_scalar(ngain[:, 0:1], ngain[:, 0:1], MLA_QK ** -0.5, None, ALU.mult))
        dve.did(dve.e.tensor_copy(ngain[0:MLA_NOPE, 1:2], self.g("mla_k_norm_g_2")[0:MLA_NOPE]))
        with ExitStack() as c:
            LH, LL = (self.sb(c, f"mla_l{x}", [P, 3, T], F32R) for x in "hl")
            sq = [res[:, 4, :], res[:, 5, :]]
            for n, (first, count, name) in enumerate(((0, 2, "q_lat_norm_g_2"), (2, 1, "kv_lat_norm_g_2"))):
                src = [res[:, 12 + first + k, :] for k in range(count)]
                s = self.prepare(src, self.g(name), LH[:, first:first + count, :], LL[:, first:first + count, :],
                                 sq=sq)
                self.token_rstd(rt[:, n, :], PS[:, 7, 0:TT], count * P, (s,))
                pr.meet(self.free)
            for t in range(TT):
                mm = pe.e.transpose(PS[:, 6, t * MLA_ROPE:(t + 1) * MLA_ROPE],
                                    res[0:MLA_ROPE, 15, t * P:(t + 1) * P], self.ident[0:MLA_ROPE, 0:MLA_ROPE])
            mm = pe.did(mm)
            act.need(mm)
            act.did(act.e.activation(kr[:].rearrange("p a b -> p (a b)"), PS[:, 6, 0:TT * MLA_ROPE], ACT.Copy))
            pr.meet(self.free)
            s0, s1 = st.take(st.g), st.take(st.g)
            for t in range(TT):
                tk = slice(t * P, (t + 1) * P)
                p = self.claim()
                for b in range(2):
                    for k, s in enumerate((s0, s1)):
                        cols = slice(b * 384, (b + 1) * 384)
                        wh, wl, out = st.hi[s][:, cols], st.lo[s][:, cols], PS[:, 2 * p + b, 0:384]
                        pe.e.matmul(out, LH[:, k, tk], wh, start=k == 0, stop=False)
                        pe.e.matmul(out, LH[:, k, tk], wl, start=False, stop=False)
                        mm = pe.e.matmul(out, LL[:, k, tk], wh, start=False, stop=k == 1)
                        if t == TT - 1 and b == 1:
                            done = st.give(s, mm)
                if t < TT - 1:
                    done = pe.did(mm)
                act.need(done)
                for b in range(2):
                    i = act.e.activation(qt[:, 4 * b:4 * b + 4, t * MLA_QK:(t + 1) * MLA_QK],
                                         PS[:, 2 * p + b, 0:384].rearrange("p (h c) -> p h c", c=MLA_QK),
                                         ACT.Copy, scale=rt[:, 0, t:t + 1])
                    self.free[p].inc(i) if b else act.did(i)
            st.split(s0)
            st.split(s1)
            s = st.take(st.g)
            for t in range(TT):
                tk = slice(t * P, (t + 1) * P)
                p = self.claim()
                for b in range(2):
                    cols, out = slice(b * 512, (b + 1) * 512), PS[:, 2 * p + b, :]
                    pe.e.matmul(out, LH[:, 2, tk], st.hi[s][:, cols], start=True, stop=False)
                    pe.e.matmul(out, LH[:, 2, tk], st.lo[s][:, cols], start=False, stop=False)
                    mm = pe.e.matmul(out, LL[:, 2, tk], st.hi[s][:, cols], start=False, stop=True)
                done = st.give(s, mm) if t == TT - 1 else pe.did(mm)
                act.need(done)
                act.did(act.e.activation(kt[:, :, t * MLA_NOPE:(t + 1) * MLA_NOPE],
                                         PS[:, 2 * p, :].rearrange("p (h c) -> p h c", c=MLA_NOPE),
                                         ACT.Copy, scale=rt[:, 1, t:t + 1]))
                self.free[p].inc(act.e.activation(V[:, :, tk], PS[:, 2 * p + 1, :].rearrange(
                    "p (k c) -> p k c", c=P), ACT.Copy, scale=rt[:, 1, t:t + 1]))
            st.split(s)
            pr.meet(self.free)

        sets = [[sb(f"mla_{n}{s}", [P, T], F32R) for n in ("qh", "ql", "kh", "kl")] for s in range(2)]
        pm = [self.H[:, k, :] for k in range(3)]
        at_buf = [self.H[:, 3, :], self.H[:, 4, :]]
        staged = [self.H[:, 5, :], self.H[:, 6, :]]
        R = slice(0, MLA_QK)

        def rotate(e, x, gain):
            a, b = slice(0, HALF_R), slice(HALF_R, MLA_ROPE)
            cos, sin = rope[:, 0], rope[:, 1]
            e.need(e.count.now())
            t = e.did(e.e.tensor_tensor(x, x, gain.unsqueeze(1).to_broadcast([P, TT, MLA_ROPE]), ALU.mult))
            e.need(t)
            e.did(e.e.tensor_tensor(tmp[:, 0, :, a], x[:, :, b], sin, ALU.mult))
            e.did(e.e.tensor_tensor(tmp[:, 0, :, b], x[:, :, a], sin, ALU.mult))
            e.did(e.e.tensor_tensor(tmp[:, 1, :, a], x[:, :, a], cos, ALU.mult))
            t = e.did(e.e.tensor_tensor(tmp[:, 1, :, b], x[:, :, b], cos, ALU.mult))
            e.need(t)
            e.did(e.e.tensor_tensor(x[:, :, a], tmp[:, 1, :, a], tmp[:, 0, :, a], ALU.subtract))
            return e.did(e.e.tensor_tensor(x[:, :, b], tmp[:, 1, :, b], tmp[:, 0, :, b], ALU.add))

        t = act.did(act.e.activation(tmp[:, 0], kr[:], ACT.Square))
        dve.need(t)
        dve.did(dve.e.tensor_reduce(krope_sq[:], tmp[:, 0], AX.X, ALU.add))
        rotate(dve, kr[:], rg[:, 1])

        ready, scored = {}, {}
        self.bank7 = self.turned = None

        def prepare(h, s):
            q3 = qt[:, h, :].rearrange("p (g c) -> p g c", c=MLA_QK)
            k3 = kt[:, h, :].rearrange("p (g c) -> p g c", c=MLA_NOPE)
            x = [a[:, 0:W].rearrange("p (g c) -> p g c", c=MLA_QK) for a in staged]
            act.need(self.turned, dve.count.now())
            sk = act.did(act.e.activation(x[1][:, :, 0:MLA_NOPE], k3, ACT.Square))
            sq = act.did(act.e.activation(x[0], q3, ACT.Square))
            dve.need(sk, dve.count.now())
            t = dve.did(dve.e.tensor_reduce(norms[:, 1, :], x[1][:, :, 0:MLA_NOPE], AX.X, ALU.add))
            dve.need(t)
            t = dve.did(dve.e.tensor_tensor(norms[:, 1, :], norms[:, 1, :], krope_sq[:], ALU.add))
            dve.need(sq)
            tq = dve.did(dve.e.tensor_reduce(norms[:, 0, :], x[0], AX.X, ALU.add))
            yield
            r = self.token_rstd(norms[:], norms[:], MLA_QK, (t, tq))
            dve.need(r)
            rb = lambda n, d: norms[:, n, :].unsqueeze(2).to_broadcast([P, TT, d])
            dve.did(dve.e.tensor_tensor(x[1][:, :, 0:MLA_NOPE], k3, rb(1, MLA_NOPE), ALU.mult))
            mk = dve.did(dve.e.tensor_tensor(x[1][:, :, MLA_NOPE:MLA_QK], kr[:], rb(1, MLA_ROPE), ALU.mult))
            dve.did(dve.e.tensor_tensor(x[0], q3, rb(0, MLA_QK), ALU.mult))
            yield
            mq = rotate(dve, x[0][:, :, MLA_NOPE:MLA_QK], rg[:, 0])
            yield
            qh, ql, kh, kl = (a[R] for a in sets[s])
            free = scored.get(s)
            kp = yield from self.head_parts(staged[1], MLA_QK, kh, kl, ngain[R, 1:2], mk, free)
            qp = yield from self.head_parts(staged[0], MLA_QK, qh, ql, ngain[R, 0:1], mq, free)
            ready[s] = [*kp, *qp]

        def round_of(i, last):
            pr.meet(self.free)
            ready.clear()
            scored.clear()
            self.bank7 = self.turned = None
            read = {}

            def side():
                yield from prepare(i * 2 + 1, 1)
                if not last:
                    yield
                    yield from prepare(i * 2 + 2, 0)

            def scores(n, item):
                s, t = item
                qh, ql, kh, kl = (a[R] for a in sets[s])
                pe.need(read.get(n - 2), ready.get(s))
                tk = slice(t * P, (t + 1) * P)
                scored[s] = self.score(n % 2, (t + 1) * P, qh[:, tk], ql[:, tk], kh, kl)
                return scored[s]

            def before(n, item, z, free):
                cols, w = (item[1] + 1) * P, n % 4
                ps = self.pair(n % 2)
                dve.need(z)
                t0 = dve.did(dve.e.memset(ps[0:64, cols - 64:cols], -1e30))
                dve.need(t0)
                mx = dve.did(dve.e.tensor_reduce(small[:, w, 0:1], ps[:, 0:cols], AX.X, ALU.max, negate=True))
                act.need(mx, free)
                read[n] = act.did(act.e.activation(pm[n % 3][:, 0:cols], ps[:, 0:cols], ACT.Exp,
                                                   bias=small[:, w, 0:1], accum_out=small[:, w, 2:3]))
                return read[n]

            def after(n, item, e):
                dve.need(e)
                w = n % 4
                return dve.did(dve.e.reciprocal(small[:, w, 3:4], small[:, w, 2:3]))

            def evac(n, item, bank, done):
                hh, t = item
                dve.need(done)
                return dve.did(dve.e.tensor_scalar(
                    res[:, i + 4, t * P + hh * 64:t * P + (hh + 1) * 64], bank, small[:, n % 4, 3:4], None,
                    ALU.mult))

            self.attend([(0, t) for t in range(TT)] + [(1, t) for t in reversed(range(TT))], lambda it: it[1] + 1,
                        scores, before, after,
                        lambda it, b: V[:, i, b * P + it[0] * 64:b * P + (it[0] + 1) * 64], evac, pm, at_buf,
                        wide=64, side=side())

        for _ in prepare(0, 0):
            pass
        with pr.loop(MLA_H // 2 - 1) as i:
            round_of(i, last=False)
        round_of(MLA_H // 2 - 1, last=True)


BIAS_LEN = T + P - 1


def build_program(nc, rates, a, gains, out):
    k = Kernel.__new__(Kernel)
    k.at = gains
    k.__init__(nc, rates, a, out)


GAINS = {}


def _lay(inp):
    def tiles(v):
        return np.ascontiguousarray(np.asarray(v).reshape(-1, P).T)

    def chan(w, c0, width=P):
        k = w.shape[0] // P
        u = np.zeros((P, k, P), w.dtype)
        u[:, :, :width] = w[:, c0:c0 + width].reshape(k, P, width).transpose(1, 0, 2)
        return [u.reshape(P, k * P)]

    def chans(w, cols):
        return [u for c in cols for u in chan(w, c)]

    def tokens(w):
        u = w.reshape(4, 2, P, 512).transpose(0, 2, 1, 3).reshape(4, P, 1024)
        return list(u)

    def rows(w, k):
        return [w[k * P:(k + 1) * P]]

    def small(w):
        u = w.reshape(2, P, 2, 4, P).transpose(2, 1, 3, 0, 4).reshape(2, P, 1024)
        return list(u)

    def ffn(gate, up, down):
        n, u = FF_TILES // 2, []
        for g in range(n):
            if g:
                u += chan(gate, 2 * g * P)
                u += rows(down, 2 * g - 2) + rows(down, 2 * g - 1)
            else:
                u += chan(gate, 0)
            u += chan(up, 2 * g * P) + chan(gate, (2 * g + 1) * P) + chan(up, (2 * g + 1) * P)
        return u + rows(down, 2 * n - 2) + rows(down, 2 * n - 1)

    w1 = np.asarray(inp["w_in"])[0]
    w2 = np.asarray(inp["w_in_2"])[0]
    gu = np.asarray(inp["w_gate_up"])[0]
    span = lambda c, n: [c + P * j for j in range(n)]
    units = chans(w1, span(0, 8))
    units += tokens(w1[:, 1536:2048]) + tokens(w1[:, 1024:1536])
    for j in range(PAIRS):
        units += chans(w1, [2048 + P * j, 2560 + P * j, 3072 + P * j])
    units += chans(np.asarray(inp["w_out"])[0], span(0, 8))
    units += ffn(gu[:, :2816], gu[:, 2816:], np.asarray(inp["w_down"])[0])
    units += small(np.asarray(inp["ple_proj"])[0])
    units += chans(np.asarray(inp["ple_gate"])[0], span(0, 8))
    units += chans(w2, [0, 128, 256]) + chan(w2, 384, MLA_ROPE)
    for c in (416, 928, 1440):
        units += tokens(w2[:, c:c + 512])
    uq = np.asarray(inp["w_uq_2"])[0]
    for k in range(2):
        u = np.zeros((P, UNIT), w1.dtype)
        u[:, :uq.shape[1]] = uq[k * P:(k + 1) * P]
        units.append(u)
    ukv = np.asarray(inp["w_ukv_2"])[0].reshape(P, MLA_H, 2, 64)
    units.append(ukv.transpose(0, 2, 1, 3).reshape(P, 1024))
    wo = np.asarray(inp["w_out_2"])[0]
    wo = np.concatenate([wo[512:], wo[:512]])
    units += chans(wo, span(0, 8))
    units += ffn(np.asarray(inp["w_gate_2"])[0], np.asarray(inp["w_up_2"])[0], np.asarray(inp["w_down_2"])[0])
    units += small(np.asarray(inp["w_ple_proj_2"])[0])
    units += chans(np.asarray(inp["w_ple_gate_2"])[0], span(0, 8))
    units += [np.zeros((P, UNIT), w1.dtype)] * RING
    arrays = {"weights": np.stack(units)}

    def flat(w):
        return np.asarray(w)[0].T.reshape(-1, P, T)

    arrays["x_t"] = np.ascontiguousarray(np.asarray(inp["x"])[0].T).reshape(KT, P, T)
    arrays["p_t"] = np.ascontiguousarray(np.asarray(inp["p"])[0, 0].T).reshape(2, P, T)
    arrays["p2_t"] = np.ascontiguousarray(np.asarray(inp["p_2"])[0, 0].T).reshape(2, P, T)

    cols, at = [], 0
    GAINS.clear()

    def put(name, m):
        nonlocal at
        z = np.zeros((P, m.shape[1]), np.float32)
        z[:m.shape[0]] = m
        cols.append(z)
        GAINS[name] = (at, m.shape[1])
        at += m.shape[1]

    put("hg_sb_out_norm", tiles(np.concatenate([np.asarray(inp["hg_out_norm"])[0],
                                                np.asarray(inp["sb_out_norm"])[0]])))
    for name in ("attn_pre_norm", "attn_post_norm", "ffn_pre_norm",
                 "ffn_post_norm", "attn_norm_g_2", "q_lat_norm_g_2", "kv_lat_norm_g_2",
                 "diff_out_norm_g_2", "ffn_norm_g_2", "ple_norm_g_2"):
        put(name, tiles(np.asarray(inp[name])[0]))
    for name in ("mla_q_norm_g_2", "mla_k_norm_g_2", "lambda_q1_2", "lambda_k1_2", "lambda_q2_2", "lambda_k2_2"):
        put(name, np.asarray(inp[name])[0][:, None])
    for name in ("diff_q_norm_g_2", "diff_k_norm_g_2"):
        g = np.asarray(inp[name])[0]
        put(name, np.concatenate([g, g])[:, None])
    g = np.asarray(inp["hg_lower_gamma"])
    put("gamma0", tiles(g[0]))
    put("gamma1", tiles(g[1]))
    cw = np.asarray(inp["conv_w_2"])[0]
    taps = np.concatenate([cw, np.asarray(inp["conv_b_2"])])
    put("conv", taps.reshape(4, FF_TILES, P).transpose(2, 1, 0).reshape(P, 4 * FF_TILES))
    arrays["rope_gain"] = np.concatenate([np.asarray(inp["mla_q_norm_g_2"])[0, MLA_NOPE:],
                                          np.asarray(inp["mla_k_norm_g_2"])[0, MLA_NOPE:]])
    arrays["gains"] = np.concatenate(cols, axis=1)
    arrays["rel_bias"] = np.ascontiguousarray(np.asarray(inp["rel_bias_2"]))
    arrays.update(_constants())
    return arrays


def _constants():
    c = {"ident": np.eye(P, dtype=np.float32)}
    s, t = np.arange(P)[:, None], np.arange(P)[None, :]
    masks = [(s // (2 * h) == t // (2 * h)) & (s % (2 * h) < h) & (t % (2 * h) >= h) for h in LEVELS]
    masks.append(s == t)
    c["levels"] = np.stack(masks, axis=1).astype(np.float32)
    c["strict"] = (t < s).astype(np.float32)
    half = MLA_ROPE // 2
    ang = (np.arange(T, dtype=np.float32)[:, None]
           * (np.float32(10000.0) ** (-np.arange(half, dtype=np.float32) / half)).astype(np.float32)[None, :])
    tables = np.stack([np.cos(ang), np.sin(ang)]).astype(np.float32)
    c["rope"] = np.ascontiguousarray(tables.reshape(2, TT, P, half).transpose(2, 0, 1, 3)).reshape(P, -1)
    rel = np.arange(BIAS_LEN) - (T - 1)
    n = np.abs(rel)
    large = 8 + (np.log(np.maximum(n, 1).astype(np.float32) / 8) / math.log(1024 / 8) * 8).astype(np.int32)
    bucket = np.where(rel > 0, 16, 0) + np.where(n < 8, n, np.minimum(large, 15))
    c["bucket"] = (np.arange(NBUCKET)[:, None] == bucket[None, :]).astype(np.float32)
    return c


def kernel(**inputs):
    import concourse.bacc as _bacc
    from concourse.bass_utils import run_bass_kernel_spmd as _run

    arrays = _lay(inputs)
    gains = dict(GAINS)
    rates = {}
    for _ in range(2):
        nc = _bacc.Bacc("TRN2", target_bir_lowering=False, num_devices=1)
        aps = {n: nc.dram_tensor("in_" + n, v.shape, mybir.dt.from_np(v.dtype), kind="ExternalInput").ap()
               for n, v in arrays.items()}
        out = nc.dram_tensor("out_t", (KT, P, T), F32, kind="ExternalOutput").ap()
        build_program(nc, rates, aps, gains, out)
    r = _run(nc, [{"in_" + n: v for n, v in arrays.items()}], core_ids=[0])
    return np.ascontiguousarray(r.results[0]["out_t"].reshape(D, T).T).reshape(1, T, D)
```
